# Optimizing a Trainium2 kernel written in Bass

```python
import jax, jax.numpy as jnp
from jax import lax
import numpy as np

"""Two-layer hybrid decoder step serving prompt and sample requests with shared weights.

Each layer: x += W_out[ FoX | RWKV-7 | Retention ](W_in RMSNorm(x));  x += SwiGLU(RMSNorm(x)).
Head groups: FoX forgetting attention 8x64 (QK-norm, no positional encoding), RWKV-7 time mixing
4x64, RetNet retention 4x64 (rotary, multi-scale decay). Mixing width 1024 = D_MODEL.

Inputs
  x_prompt (BATCH, SEQ, D_MODEL), x_sample (DEC_BATCH, DEC_SEQ, D_MODEL)
  cache_fox_k, cache_fox_v (DEPTH, N_POOL, PAGE_SIZE, FOX_H, HEAD_DIM)  paged, N_POOL = 5/4 * DEC_BATCH * N_PAGES
  cache_fox_logf           (DEPTH, N_POOL, PAGE_SIZE, FOX_H)            paged log-forget values
  state_rwkv               (DEPTH, DEC_BATCH, RWKV_H, HEAD_DIM, HEAD_DIM)  [value x key]
  state_rwkv_shift         (DEPTH, DEC_BATCH, RWKV_PROJ)  last projected RWKV row (token shift)
  state_ret                (DEPTH, DEC_BATCH, RET_H, HEAD_DIM, HEAD_DIM)   [key x value]
  page_table               (DEC_BATCH, N_PAGES) int32, N_PAGES = PAST_LEN // PAGE_SIZE
  weights stacked over a leading DEPTH axis.
Output tuple
  y_prompt (BATCH, SEQ, D_MODEL), y_sample (DEC_BATCH, DEC_SEQ, D_MODEL),
  fox_k_prompt, fox_v_prompt (DEPTH, BATCH*SEQ//PAGE_SIZE, PAGE_SIZE, FOX_H, HEAD_DIM)  pages, sequence-major
  fox_logf_prompt (DEPTH, BATCH*SEQ//PAGE_SIZE, PAGE_SIZE, FOX_H)
  rwkv_state_prompt (DEPTH, BATCH, RWKV_H, HEAD_DIM, HEAD_DIM), rwkv_shift_prompt (DEPTH, BATCH, RWKV_PROJ)
  ret_state_prompt (DEPTH, BATCH, RET_H, HEAD_DIM, HEAD_DIM)
  fox_k_sample, fox_v_sample (DEPTH, DEC_BATCH, DEC_SEQ, FOX_H, HEAD_DIM)  rows for positions PAST_LEN..
  fox_logf_sample (DEPTH, DEC_BATCH, DEC_SEQ, FOX_H)
  rwkv_state_sample (DEPTH, DEC_BATCH, RWKV_H, HEAD_DIM, HEAD_DIM), rwkv_shift_sample (DEPTH, DEC_BATCH, RWKV_PROJ)
  ret_state_sample (DEPTH, DEC_BATCH, RET_H, HEAD_DIM, HEAD_DIM)
"""

D_MODEL = 1024
BATCH = 1
SEQ = 1024
DEPTH = 2
DEC_BATCH = 8
DEC_SEQ = 4
PAST_LEN = 1024
PAGE_SIZE = 128

HEAD_DIM = 64
FOX_H = 8
RWKV_H = 4
RET_H = 4
FOX_W = FOX_H * HEAD_DIM
RWKV_W = RWKV_H * HEAD_DIM
RET_W = RET_H * HEAD_DIM
MIX_W = FOX_W + RWKV_W + RET_W
RWKV_LORA_W = 32
RWKV_LORA_A = 32
RWKV_LORA_G = 64
FOX_PROJ = 3 * FOX_W + FOX_H
RWKV_PROJ = 3 * RWKV_W + RWKV_LORA_W + RWKV_LORA_A + RWKV_LORA_G
RET_PROJ = 4 * RET_W
PROJ_W = FOX_PROJ + RWKV_PROJ + RET_PROJ
D_FF = -(-8 * D_MODEL // (3 * 256)) * 256
Q_BLOCK = 128
RET_CHUNK = 128
ROPE_BASE = 10000.0
NORM_EPS = 1e-6
RWKV_GN_EPS = 64e-5
RET_GN_EPS = 1e-5
FORGET_BIAS_LO = 1.0
FORGET_BIAS_HI = 4.0
RWKV_W0_CENTER = -2.0

kernel_name = 'fox_rwkv7_retention_hybrid_step'

F32 = jnp.float32

def _split(x, sizes):
    offs = np.cumsum(np.array(sizes))[:-1].tolist()
    return jnp.split(x, offs, axis=-1)

def rms_norm(x, g, eps=NORM_EPS):
    xf = x.astype(F32)
    y = xf * lax.rsqrt(jnp.mean(xf * xf, -1, keepdims=True) + eps) * g.astype(F32)
    return y.astype(x.dtype)

def head_norm(x, w, b, eps):
    xf = x.astype(F32)
    xc = xf - jnp.mean(xf, -1, keepdims=True)
    y = xc * lax.rsqrt(jnp.mean(xc * xc, -1, keepdims=True) + eps) * w.astype(F32)
    return y if b is None else y + b.astype(F32)

def rotary(x, pos):
    half = HEAD_DIM // 2
    inv = ROPE_BASE ** (-jnp.arange(half, dtype=F32) / half)
    ang = pos.astype(F32)[:, None] * inv[None, :]
    cos = jnp.cos(ang)[None, :, None, :]
    sin = jnp.sin(ang)[None, :, None, :]
    x1 = x[..., :half].astype(F32)
    x2 = x[..., half:].astype(F32)
    return jnp.concatenate([x1 * cos - x2 * sin, x2 * cos + x1 * sin], -1).astype(x.dtype)

def fox_prompt(q, k, v, logf):
    B, T, H, D = q.shape
    c = jnp.cumsum(logf, axis=1)
    c_keys = c.transpose(0, 2, 1)
    nb = T // Q_BLOCK
    qb = q.reshape(B, nb, Q_BLOCK, H, D).transpose(1, 0, 2, 3, 4)
    cb = c.reshape(B, nb, Q_BLOCK, H).transpose(1, 0, 3, 2)
    key_pos = jnp.arange(T)
    scale = D ** -0.5

    def block(args):
        i, q_i, c_i = args
        s = jnp.einsum('bqhd,bkhd->bhqk', q_i, k, preferred_element_type=F32) * scale
        s = s + (c_i[..., :, None] - c_keys[..., None, :])
        qpos = i * Q_BLOCK + jnp.arange(Q_BLOCK)
        s = jnp.where(key_pos[None, :] <= qpos[:, None], s, -jnp.inf)
        p = jax.nn.softmax(s, axis=-1)
        return jnp.einsum('bhqk,bkhd->bqhd', p.astype(v.dtype), v)

    o = lax.map(block, (jnp.arange(nb), qb, cb))
    return o.transpose(1, 0, 2, 3, 4).reshape(B, T, H, D)

def fox_sample(q, k, v, logf, k_past, v_past, logf_past):
    B, T, H, D = q.shape
    P = k_past.shape[1]
    scale = D ** -0.5
    c_past = jnp.cumsum(logf_past.astype(F32), axis=1)
    c_new = c_past[:, -1:, :] + jnp.cumsum(logf.astype(F32), axis=1)
    cp = c_past.transpose(0, 2, 1)
    cn = c_new.transpose(0, 2, 1)
    s_past = jnp.einsum('bthd,bshd->bhts', q, k_past, preferred_element_type=F32) * scale
    s_past = s_past + (cn[..., :, None] - cp[..., None, :])
    s_new = jnp.einsum('bthd,bshd->bhts', q, k, preferred_element_type=F32) * scale
    s_new = s_new + (cn[..., :, None] - cn[..., None, :])
    s_new = jnp.where(jnp.tril(jnp.ones((T, T), bool)), s_new, -jnp.inf)
    p = jax.nn.softmax(jnp.concatenate([s_past, s_new], -1), axis=-1).astype(v.dtype)
    return (jnp.einsum('bhts,bshd->bthd', p[..., :P], v_past)
            + jnp.einsum('bhts,bshd->bthd', p[..., P:], v))

def rwkv7(p, shift_prev, S0, lp):
    dt = p.dtype
    B, T, _ = p.shape
    p_prev = jnp.concatenate([shift_prev[:, None, :].astype(dt), p[:, :-1]], axis=1)
    xs = p + (p_prev - p) * lp['rwkv_mu']
    r, k, v, w_lo, a_lo, g_lo = _split(xs, [RWKV_W, RWKV_W, RWKV_W, RWKV_LORA_W, RWKV_LORA_A, RWKV_LORA_G])
    w = -jax.nn.softplus(-(lp['rwkv_w0'] + jnp.tanh(w_lo) @ lp['rwkv_w2'])) - 0.5
    decay = jnp.exp(-jnp.exp(w.astype(F32)))
    a = jax.nn.sigmoid(lp['rwkv_a0'] + a_lo @ lp['rwkv_a2'])
    g = jax.nn.sigmoid(g_lo) @ lp['rwkv_g2']
    heads = lambda t: t.reshape(B, T, RWKV_H, HEAD_DIM).astype(F32)
    kk = heads(k * lp['rwkv_k_k'])
    kk = kk / jnp.maximum(jnp.sqrt(jnp.sum(kk * kk, -1, keepdims=True)), 1e-12)
    k = k * (1 + (a - 1) * lp['rwkv_k_a'])
    r_h, k_h, v_h, w_h, a_h = heads(r), heads(k), heads(v), heads(decay), heads(a)
    a_vec = -kk
    b_vec = kk * a_h

    def step(S, inp):
        r_t, w_t, k_t, v_t, a_t, b_t = inp
        sa = jnp.einsum('bhvk,bhk->bhv', S, a_t)
        S = S * w_t[:, :, None, :] + sa[..., None] * b_t[:, :, None, :] + v_t[..., None] * k_t[:, :, None, :]
        return S, jnp.einsum('bhvk,bhk->bhv', S, r_t)

    tm = lambda t: jnp.moveaxis(t, 1, 0)
    S_T, y = lax.scan(step, S0.astype(F32), (tm(r_h), tm(w_h), tm(k_h), tm(v_h), tm(a_vec), tm(b_vec)))
    y = jnp.moveaxis(y, 0, 1)
    y = head_norm(y, lp['rwkv_lnx_w'].reshape(RWKV_H, HEAD_DIM), lp['rwkv_lnx_b'].reshape(RWKV_H, HEAD_DIM), RWKV_GN_EPS)
    bonus = jnp.sum(r_h * k_h * lp['rwkv_r_k'].astype(F32), -1, keepdims=True) * v_h
    out = ((y + bonus).reshape(B, T, RWKV_W) * g.astype(F32)).astype(dt)
    return out, S_T.astype(dt), p[:, -1]

def retention(q, k, v, R0):
    dt = q.dtype
    B, T, H, D = q.shape
    L = RET_CHUNK if T % RET_CHUNK == 0 else T
    nc = T // L
    log_gamma = jnp.log1p(-jnp.exp2(-5.0 - jnp.arange(H, dtype=F32)))
    idx = jnp.arange(L, dtype=F32)
    diff = idx[:, None] - idx[None, :]
    dmask = jnp.where(diff >= 0, jnp.exp(log_gamma[:, None, None] * jnp.maximum(diff, 0.0)), 0.0)
    cross = jnp.exp(log_gamma[:, None] * (idx + 1.0)).T[None, :, :, None]
    inner_w = jnp.exp(log_gamma[:, None] * (L - 1.0 - idx))
    chunk_decay = jnp.exp(log_gamma * L)[None, :, None, None]
    ch = lambda t: t.astype(F32).reshape(B, nc, L, H, D).transpose(1, 0, 2, 3, 4)

    def step(R, inp):
        qi, ki, vi = inp
        s = jnp.einsum('blhd,bmhd->bhlm', qi, ki) * dmask
        o = jnp.einsum('bhlm,bmhd->blhd', s, vi) + jnp.einsum('blhd,bhde->blhe', qi, R) * cross
        R = R * chunk_decay + jnp.einsum('blhd,blhe,hl->bhde', ki, vi, inner_w)
        return R, o

    R_T, o = lax.scan(step, R0.astype(F32), (ch(q), ch(k), ch(v)))
    return o.transpose(1, 0, 2, 3, 4).reshape(B, T, H, D), R_T.astype(dt)

def mixer(h, pos, lp, fox_past, rwkv_S, rwkv_shift, ret_R):
    dt = h.dtype
    B, T, _ = h.shape
    proj = jnp.einsum('btd,dp->btp', h, lp['w_in'])
    fq, fk, fv, f_lin, rwkv_p, eq, ek, ev, eg = _split(
        proj, [FOX_W, FOX_W, FOX_W, FOX_H, RWKV_PROJ, RET_W, RET_W, RET_W, RET_W])
    heads = lambda t, n: t.reshape(B, T, n, HEAD_DIM)
    fq = rms_norm(heads(fq, FOX_H), lp['fox_qn_g'])
    fk = rms_norm(heads(fk, FOX_H), lp['fox_kn_g'])
    fv = heads(fv, FOX_H)
    logf = jax.nn.log_sigmoid(f_lin.astype(F32) + lp['fox_f_b'].astype(F32))
    if fox_past is None:
        fo = fox_prompt(fq, fk, fv, logf)
    else:
        fo = fox_sample(fq, fk, fv, logf, *fox_past)
    ro, rwkv_S, rwkv_shift = rwkv7(rwkv_p, rwkv_shift, rwkv_S, lp)
    eq = rotary(heads(eq, RET_H), pos)
    ek = rotary(heads(ek, RET_H), pos) * (HEAD_DIM ** -0.5)
    eo, ret_R = retention(eq, ek, heads(ev, RET_H), ret_R)
    eo = head_norm(eo, lp['ret_gn_w'].reshape(RET_H, HEAD_DIM), None, RET_GN_EPS) * jax.nn.silu(heads(eg, RET_H).astype(F32))
    mixed = jnp.concatenate([fo.reshape(B, T, FOX_W).astype(dt), ro, eo.reshape(B, T, RET_W).astype(dt)], -1)
    out = jnp.einsum('btm,md->btd', mixed, lp['w_out'])
    return out, (fk, fv, logf.astype(dt)), rwkv_S, rwkv_shift, ret_R

def layer(x, pos, lp, fox_past, rwkv_S, rwkv_shift, ret_R):
    m, fox_rows, rwkv_S, rwkv_shift, ret_R = mixer(rms_norm(x, lp['ln_mix_g']), pos, lp, fox_past, rwkv_S, rwkv_shift, ret_R)
    x = x + m
    h = rms_norm(x, lp['ln_ffn_g'])
    x = x + (jax.nn.silu(h @ lp['w_gate']) * (h @ lp['w_up'])) @ lp['w_down']
    return x, fox_rows, rwkv_S, rwkv_shift, ret_R

def setup_inputs(seed: int = 0) -> dict:
    key = jax.random.key(seed)
    ks = iter(jax.random.split(key, 48))
    nrm = lambda shape, scale: jax.random.normal(next(ks), shape, F32) * scale
    wgt = lambda shape, fan_in: nrm(shape, fan_in ** -0.5)
    gain = lambda shape: 1.0 + nrm(shape, 0.05)
    n_pages = PAST_LEN // PAGE_SIZE
    n_pool = (DEC_BATCH * n_pages * 5) // 4
    f_sched = jnp.linspace(FORGET_BIAS_LO, FORGET_BIAS_HI, FOX_H, dtype=F32)
    x_prompt = nrm((BATCH, SEQ, D_MODEL), 1.0)
    x_sample = nrm((DEC_BATCH, DEC_SEQ, D_MODEL), 1.0)
    cache_fox_k = nrm((DEPTH, n_pool, PAGE_SIZE, FOX_H, HEAD_DIM), 1.0)
    cache_fox_v = nrm((DEPTH, n_pool, PAGE_SIZE, FOX_H, HEAD_DIM), 1.0)
    cache_fox_logf = jax.nn.log_sigmoid(f_sched + nrm((DEPTH, n_pool, PAGE_SIZE, FOX_H), 1.0))
    state_rwkv = nrm((DEPTH, DEC_BATCH, RWKV_H, HEAD_DIM, HEAD_DIM), 0.5)
    state_rwkv_shift = nrm((DEPTH, DEC_BATCH, RWKV_PROJ), 1.0)
    state_ret = nrm((DEPTH, DEC_BATCH, RET_H, HEAD_DIM, HEAD_DIM), 0.5)
    perm = jax.random.permutation(next(ks), n_pool)[:DEC_BATCH * n_pages]
    page_table = perm.reshape(DEC_BATCH, n_pages).astype(jnp.int32)
    return {
        'x_prompt': x_prompt, 'x_sample': x_sample,
        'cache_fox_k': cache_fox_k, 'cache_fox_v': cache_fox_v, 'cache_fox_logf': cache_fox_logf,
        'state_rwkv': state_rwkv, 'state_rwkv_shift': state_rwkv_shift, 'state_ret': state_ret,
        'page_table': page_table,
        'ln_mix_g': gain((DEPTH, D_MODEL)),
        'w_in': wgt((DEPTH, D_MODEL, PROJ_W), D_MODEL),
        'fox_qn_g': gain((DEPTH, HEAD_DIM)),
        'fox_kn_g': gain((DEPTH, HEAD_DIM)),
        'fox_f_b': f_sched[None, :] + nrm((DEPTH, FOX_H), 0.1),
        'rwkv_mu': jax.random.uniform(next(ks), (DEPTH, RWKV_PROJ), F32),
        'rwkv_w0': RWKV_W0_CENTER + nrm((DEPTH, RWKV_W), 0.5),
        'rwkv_w2': nrm((DEPTH, RWKV_LORA_W, RWKV_W), 0.1 * RWKV_LORA_W ** -0.5),
        'rwkv_a0': nrm((DEPTH, RWKV_W), 0.1),
        'rwkv_a2': wgt((DEPTH, RWKV_LORA_A, RWKV_W), RWKV_LORA_A),
        'rwkv_g2': wgt((DEPTH, RWKV_LORA_G, RWKV_W), RWKV_LORA_G),
        'rwkv_k_k': gain((DEPTH, RWKV_W)),
        'rwkv_k_a': gain((DEPTH, RWKV_W)),
        'rwkv_r_k': nrm((DEPTH, RWKV_H, HEAD_DIM), 0.1),
        'rwkv_lnx_w': gain((DEPTH, RWKV_W)),
        'rwkv_lnx_b': nrm((DEPTH, RWKV_W), 0.02),
        'ret_gn_w': gain((DEPTH, RET_W)),
        'w_out': wgt((DEPTH, MIX_W, D_MODEL), MIX_W),
        'ln_ffn_g': gain((DEPTH, D_MODEL)),
        'w_gate': wgt((DEPTH, D_MODEL, D_FF), D_MODEL),
        'w_up': wgt((DEPTH, D_MODEL, D_FF), D_MODEL),
        'w_down': wgt((DEPTH, D_FF, D_MODEL), D_FF),
    }

def reference(x_prompt, x_sample, cache_fox_k, cache_fox_v, cache_fox_logf, state_rwkv, state_rwkv_shift,
              state_ret, page_table, ln_mix_g, w_in, fox_qn_g, fox_kn_g, fox_f_b, rwkv_mu, rwkv_w0, rwkv_w2,
              rwkv_a0, rwkv_a2, rwkv_g2, rwkv_k_k, rwkv_k_a, rwkv_r_k, rwkv_lnx_w, rwkv_lnx_b, ret_gn_w,
              w_out, ln_ffn_g, w_gate, w_up, w_down):
    B, T, _ = x_prompt.shape
    DB, TS, _ = x_sample.shape
    n_pages = page_table.shape[1]
    past_len = n_pages * PAGE_SIZE
    pos_p = jnp.arange(T)
    pos_s = past_len + jnp.arange(TS)
    dt = x_prompt.dtype
    yp, ys = x_prompt, x_sample
    kp, vp, lfp, Sp, shp, Rp = [], [], [], [], [], []
    ks_, vs_, lfs, Ss, shs, Rs = [], [], [], [], [], []
    for l in range(DEPTH):
        lp = dict(ln_mix_g=ln_mix_g[l], w_in=w_in[l], fox_qn_g=fox_qn_g[l], fox_kn_g=fox_kn_g[l],
                  fox_f_b=fox_f_b[l], rwkv_mu=rwkv_mu[l], rwkv_w0=rwkv_w0[l], rwkv_w2=rwkv_w2[l],
                  rwkv_a0=rwkv_a0[l], rwkv_a2=rwkv_a2[l], rwkv_g2=rwkv_g2[l], rwkv_k_k=rwkv_k_k[l],
                  rwkv_k_a=rwkv_k_a[l], rwkv_r_k=rwkv_r_k[l], rwkv_lnx_w=rwkv_lnx_w[l],
                  rwkv_lnx_b=rwkv_lnx_b[l], ret_gn_w=ret_gn_w[l], w_out=w_out[l], ln_ffn_g=ln_ffn_g[l],
                  w_gate=w_gate[l], w_up=w_up[l], w_down=w_down[l])
        yp, (fk, fv, flf), S_new, sh_new, R_new = layer(
            yp, pos_p, lp, None,
            jnp.zeros((B, RWKV_H, HEAD_DIM, HEAD_DIM), F32),
            jnp.zeros((B, RWKV_PROJ), dt),
            jnp.zeros((B, RET_H, HEAD_DIM, HEAD_DIM), F32))
        kp.append(fk); vp.append(fv); lfp.append(flf); Sp.append(S_new); shp.append(sh_new); Rp.append(R_new)
        k_past = cache_fox_k[l, page_table].reshape(DB, past_len, FOX_H, HEAD_DIM)
        v_past = cache_fox_v[l, page_table].reshape(DB, past_len, FOX_H, HEAD_DIM)
        lf_past = cache_fox_logf[l, page_table].reshape(DB, past_len, FOX_H)
        ys, (fk, fv, flf), S_new, sh_new, R_new = layer(
            ys, pos_s, lp, (k_past, v_past, lf_past), state_rwkv[l], state_rwkv_shift[l], state_ret[l])
        ks_.append(fk); vs_.append(fv); lfs.append(flf); Ss.append(S_new); shs.append(sh_new); Rs.append(R_new)
    n_prompt_pages = B * T // PAGE_SIZE
    fox_k_prompt = jnp.stack(kp).reshape(DEPTH, n_prompt_pages, PAGE_SIZE, FOX_H, HEAD_DIM)
    fox_v_prompt = jnp.stack(vp).reshape(DEPTH, n_prompt_pages, PAGE_SIZE, FOX_H, HEAD_DIM)
    fox_logf_prompt = jnp.stack(lfp).reshape(DEPTH, n_prompt_pages, PAGE_SIZE, FOX_H)
    rwkv_state_prompt = jnp.stack(Sp)
    rwkv_shift_prompt = jnp.stack(shp)
    ret_state_prompt = jnp.stack(Rp)
    fox_k_sample = jnp.stack(ks_)
    fox_v_sample = jnp.stack(vs_)
    fox_logf_sample = jnp.stack(lfs)
    rwkv_state_sample = jnp.stack(Ss)
    rwkv_shift_sample = jnp.stack(shs)
    ret_state_sample = jnp.stack(Rs)
    return (yp, ys, fox_k_prompt, fox_v_prompt, fox_logf_prompt, rwkv_state_prompt, rwkv_shift_prompt,
            ret_state_prompt, fox_k_sample, fox_v_sample, fox_logf_sample, rwkv_state_sample,
            rwkv_shift_sample, ret_state_sample)


_drawn_inputs = setup_inputs


def setup_inputs(seed=0):
    import zlib

    import numpy as np

    out = dict(_drawn_inputs(seed))
    spreads = {}
    factors = {'fox_qn_g': 3.679,
     'rwkv_w2': 5.553,
     'rwkv_k_k': 9.81,
     'rwkv_lnx_w': 2.843,
     'rwkv_lnx_b': 7.047,
     'ret_gn_w': 2.892}
    for name, (base, spread) in spreads.items():
        noise = np.random.default_rng([zlib.crc32(name.encode()), seed]).standard_normal(out[name].shape)
        drawn = base * np.exp(spread * noise) if base else spread * noise
        out[name] = __import__('jax').numpy.asarray(drawn.astype(out[name].dtype))
    for name, factor in factors.items():
        out[name] = (out[name] * factor).astype(out[name].dtype)
    return out
```

```python
from contextlib import ExitStack

import concourse.bass as bass
from concourse import mybir

F32 = mybir.dt.float32
ALU = mybir.AluOpType
ACT = mybir.ActivationFunctionType
AX = mybir.AxisListType

D = 1024
T = 1024
DEPTH = 2
DB, TS = 8, 4
NPG, PG = 8, 128
HD = 64
FH, RH, EH = 8, 4, 4
FW, RW, EW = FH * HD, RH * HD, EH * HD
RPROJ = 3 * RW + 128
FF = 2816
N_POOL = DB * NPG * 5 // 4
EPS = 1e-6
RWKV_EPS = 64e-5
RET_EPS = 1e-5
KAPPA = 0.6065306597126334

P = 128
NS = DB * TS
NT = T + NS
KT = D // P
TB = NT // 3
NTT = T // P
FT = FF // P

C_FQ, C_FK, C_FV, C_FL = 0, FW, 2 * FW, 3 * FW
C_R = 3 * FW + FH
C_EQ = C_R + RPROJ
C_EV = C_EQ + 2 * EW

J_R, J_EQ, J_EV, J_FQ, J_FV, J_OUT, J_FF = 0, 8, 12, 16, 24, 28, 36
JOBS = J_FF + 2 * FT
J_DOWN = JOBS
PJOBS = JOBS + KT
RING = 4

CONSTS = {}
_n = 0
for _name, _w in (("ident", P), ("blk", P), ("rot", P),
                  ("m_d", P), ("m_n", P), ("m_dt", P), ("m_u", P), ("m_ui", P), ("fmask", P),
                  ("s_l", NS), ("s_lt", NS), ("s_u", NS), ("s_ui", NS), ("s_row", DB), ("s_col", DB * NS),
                  ("s_fmask", 4), ("s_dmask", EH * NS), ("s_cross", 2 * NS), ("s_inner", EH), ("s_gam", 2),
                  ("s_sel", 2 * P), ("s_req", 2 * DB),
                  ("cross", 2 * P), ("inner", EH), ("gam", 2),
                  ("dmask", EH * P), ("cos", NT), ("sin", NT)):
    CONSTS[_name] = (_n, _w)
    _n += _w
NCONST = _n

COLS = {}
_n = 0
for _name, _w in (("ln_mix", 8), ("ln_ffn", 8), ("mu", 7), ("w0", 2), ("a0", 2), ("kk", 2), ("ka", 2),
                  ("rk", 4), ("qn", 1), ("kn", 1), ("fb", 1)):
    COLS[_name] = (_n, _w)
    _n += _w
NCOLS = _n


class Steps:

    def __init__(self, *names):
        self.names = names
        self.n = len(names)
        self.seen = 0

    def at(self, it, name):
        return it * self.n + self.names.index(name) + 1

    def start(self):
        self.seen = 0

    def mark(self, ins, sem, name):
        assert self.names[self.seen] == name, (self.names[self.seen], name)
        self.seen += 1
        ins.then_inc(sem, 1)


def names(pattern, *counts):
    out = [pattern]
    for c in counts:
        out = [o + str(i) for o in out for i in range(c)]
    return out


def build(nc, I, O, decay_rows):
    ctx = ExitStack()
    with ctx:
        def sb(name, shape):
            return ctx.enter_context(nc.sbuf_tensor(name, shape, F32))

        def sem(name):
            return ctx.enter_context(nc.semaphore(name))

        xT = sb("xT", [P, KT, NT])
        hT = sb("hT", [P, KT, NT])
        big = sb("big", [P, FT * NT])
        ring = sb("ring", [P, RING, KT, P])
        wd = sb("wd", [P, 2, FT, P])
        sil = sb("sil", [P, 2 * NT])
        ident = sb("ident", [P, P])
        blk = sb("blk", [P, P])
        ones = sb("ones", [P, P])
        cols = sb("cols", [P, NCOLS])
        ptab = ctx.enter_context(nc.sbuf_tensor("ptab", [1, DB * NPG], mybir.dt.int32))
        ps = ctx.enter_context(nc.psum_tensor("ps", [P, 8, 512], F32))

        wdf = wd[:, :, :, :].rearrange("p a b c -> p (a b c)")

        def region(base, *dims):
            n = 1
            for d in dims:
                n *= d
            a, off = base
            ap = a[:, off:off + n]
            if len(dims) == 2:
                ap = ap.rearrange("p (a b) -> p a b", a=dims[0])
            if len(dims) == 3:
                ap = ap.rearrange("p (a b c) -> p a b c", a=dims[0], b=dims[1])
            return ap

        def col(name, i=0, rows=slice(0, P)):
            return cols[rows, COLS[name][0] + i:COLS[name][0] + i + 1]

        mixB0 = FT * NT - 4 * NT
        mixB = region((big, mixB0), 4, NT)
        fl = region((big, mixB0 - NT), NT)
        PW = 1 + T + DB * (TS + 1)
        XW = PW - 1
        rp = region((big, 0), 7, PW)
        xs = region((big, 7 * PW), 7, XW)
        kk_ = region((big, 0), 2, XW)
        bv = region((big, 2 * XW), 2, XW)
        sw = region((big, 4 * XW), 2, XW)
        prB = 7 * PW + 7 * XW
        WM = 0
        m_d, m_n, m_dt, m_u, m_ui = (region((wdf, WM + P * i), P) for i in range(5))
        rows = region((wdf, 640), 3, RW)
        lora = region((wdf, 1408), RW)
        SM_ = 1664
        A0 = 2096
        rn = region((wdf, A0), XW)
        sq1 = region((wdf, A0 + XW), XW)
        sl = [region((wdf, A0 + 512 * i), 4, P) for i in range(6)] + [region((big, prB + 512 * i), 4, P) for i in range(5)]
        cum = region((wdf, A0 + 3072), 2, P + 1)
        f0 = prB + 2560
        st = region((big, f0), 2, HD)
        stm = region((big, f0 + 128), 2, HD)
        small = region((big, f0 + 256), 96)
        kpos, kneg, fmid, cbon, stats, mv, rstd = (small[:, a:b] for a, b in
            ((0, 2), (2, 4), (4, 6), (8, 12), (12, 36), (36, 44), (44, 48)))
        kac = small[:, 48:50]
        vbk = region((sil, 0), 6, P)
        ar = region((sil, 768), 2, 2, P)
        bt = region((sil, 1280), 2, P)
        kt_ = region((sil, 1536), 2, P)
        pe_ = region((sil, 1792), 2, P + 1)
        c0 = 6 * XW
        pinv = region((big, c0), 2, P)
        rk2 = region((big, c0 + 256), 2, P)
        vs = region((big, c0 + 512), 2, P)
        sg = region((big, c0 + 768), P)
        s_l, s_lt, s_u, s_ui = (region((wdf, SM_ + NS * i), NS) for i in range(4))
        s_row = region((wdf, SM_ + 4 * NS), DB)
        s_col = region((wdf, SM_ + 4 * NS + DB), DB, NS)
        nat = region((wdf, A0), DB, RH * HD)
        smat = [region((wdf, A0 + 2048 + P * i), RH, NS) for i in range(8)]
        sts = region((big, prB), 2, DB, HD)
        aex = region((big, prB + 1024), 2, DB, NS)
        rex = region((big, prB + 2048), 2, DB, NS)
        x0s = region((big, c0), RW)
        us = region((big, c0 + 256), RW)
        uex = region((big, 0), RH, DB, HD)
        vex = region((big, 2048), RH, DB, HD)
        yns = region((big, 4096), RW)
        nat_out = region((big, 8832), DB, RH * HD)
        vbks = region((sil, 0), 6, P)
        ars = region((sil, 768), 2, 2, NS)
        bts = region((sil, 896), 2, NS)
        kts = region((sil, 960), 2, NS)
        rk2s = region((sil, 1024), 2, NS)
        vss = region((sil, 1088), 2, NS)
        sgs = region((sil, 1152), NS)
        cum5 = region((sil, 1184), 2, DB, TS + 1)
        e5 = region((sil, 1264), 2, DB, TS + 1)
        pi5 = region((sil, 1344), 2, DB, TS + 1)
        eqk = region((big, 0), 4, NT)
        evg = region((big, 4 * NT), NTT + 1, 2 * EW)
        RC = 8832 + DB * RH * HD
        rconst = region((big, RC), 2 * P + EH + 2 + EH * P + 2 * NT)
        cross = rconst[:, 0:2 * P].rearrange("p (m t) -> p m t", m=2)
        inner = rconst[:, 2 * P:2 * P + EH]
        gam = rconst[:, 2 * P + EH:2 * P + EH + 2]
        dmask = rconst[:, 262:262 + EH * P].rearrange("p (a b t) -> p b a t", a=2, b=2)
        cos_t = rconst[:, 774:774 + NT]
        sin_t = rconst[:, 774 + NT:774 + 2 * NT]
        RS0 = RC + 2886
        s_dmask = region((big, RS0), EH * NS).rearrange("p (a b t) -> p b a t", a=2, b=2)
        s_cross = region((big, RS0 + P), 2, NS)
        s_inner = region((big, RS0 + 192), EH)
        s_gam = region((big, RS0 + 196), 2)
        rot = region((big, RS0 + 198), P)
        W0 = RS0 + 198 + P
        ropet = region((big, W0), NT)
        qs = region((big, W0 + NT), 2, P)
        ks = region((big, W0 + NT + 256), 2, P)
        qd = region((big, W0 + NT + 512), 2, P)
        ve = region((big, W0 + NT + 768), EW)
        rst = region((big, W0 + NT + 1024), 2, HD)
        assert W0 + NT + 1024 + 128 <= prB + 1536
        kd = region((sil, 0), EH, HD)
        stt = region((sil, 256), EH, P)
        yne = region((sil, 768), EW)
        qex = region((sil, 1024), 2, DB, NS)
        qds = region((sil, 1536), 2, NS)
        stts = region((sil, 1600), EH, NS)
        kds = region((sil, 1728), EH, HD)
        rss = region((wdf, A0), 2, DB, HD)
        vexe = region((wdf, A0 + 1024), EH, DB, HD)
        fqk = region((big, 0), 8, NT)
        fv = region((big, 8 * NT), NTT + 1, FW)
        FB = 8 * NT + (NTT + 1) * FW
        fsq = region((big, FB), 2, NT)
        frs = region((big, FB + 2 * NT), 2, NT)
        fz = hT[0:FH, 4, :]
        fe = hT[0:FH, 5, :]
        ncr = region((big, FB), T)[0:FH]
        lft = region((big, FB + T), (NTT + 1) * FH)
        qtp = hT[:, 4, :]
        ktp = hT[:, 5, :]
        ncb = region((hT[:, 6:8, :].rearrange("p a b -> p (a b)"), 0), 2, T)
        ncd = region((sil, 0), 2 * NTT, P)
        sp_ = region((wdf, 0), 2, T)
        ptt = region((wdf, 2 * T), 2, NTT, P)
        vp = region((wdf, 4 * T), NTT, P)
        otok = region((big, FB + T + 72), NTT, P)
        ko = region((big, FB + 2 * T + 72), NTT, P)
        kos = region((big, FB + 3 * T + 72), P)
        fmask = region((big, FB + 3 * T + 72 + P), P)
        fcol = region((big, FB + 4 * NT), 72)
        mx, nmx, rsum, rrec = (fcol[:, 16 * i:16 * i + 16] for i in range(4))
        gq8 = fcol[:, 64:65]
        NP = NPG * PG
        slot = [region((big, 4 * T * i), NPG, FW) for i in range(4)]
        qb = region((wdf, 0), DB, 4, NS)
        kn = region((wdf, 1024), 4, NS)
        vn = region((wdf, 1152), FW)
        ssel = region((wdf, 1664), 2, P)
        sreq = region((wdf, 1920), 2, DB)
        sfm = region((wdf, 1936), TS)
        cur_q = region((wdf, 1940), 4, 4, NS)
        cur_k = region((wdf, 2452), 4, 16)
        cur_sel = region((wdf, 2516), P)
        cur_req = region((wdf, 2644), DB)
        lfp = region((wdf, 2652), NPG, DB * FH)
        ncs = region((wdf, 3164), NP + TS)
        pss = region((wdf, 4192), NP + TS)
        fsm = region((wdf, 5220), 24)
        pn = region((wdf, 5244), DB, TS)
        pnt = region((wdf, 5276), P)
        keyt = [region((sil, NP * i), NP) for i in range(2)]
        pts = hT[:, 4, 0:NPG * PG].rearrange("p (j r) -> p j r", j=NPG)
        smn = hT[:, 5, 0:TS]
        lfs = hT[:, 6, 0:NP + TS]
        h2 = region((big, 0), FT, NT)
        nsq = region((big, 0), 2, NT)
        nrs = region((big, 2 * NT), NT)
        xstage = region((big, 0), 2, D)
        ytile = region((big, 2 * D), KT, P)
        yrows = region((big, 3 * D), 2, D)

        consts_in = sem("consts_in")
        x_in = [sem("x_in0"), sem("x_in1")]
        params_in = sem("params_in")
        loaded = [sem(f"loaded{i}") for i in range(RING)]
        down_loaded = [sem(f"down_loaded{i}") for i in range(2)]
        gemm_done = sem("gemm_done")
        evac = [sem("evac0"), sem("evac1")]
        xt_pe, xt_ev = sem("xt_pe"), sem("xt_ev")
        n_pe, n_dve, n_act = sem("norm_pe"), sem("norm_dve"), sem("norm_act")
        out_done = sem("out_done")
        zero_done = sem("zero_done")
        shift_in, shift_out = sem("shift_in"), sem("shift_out")
        pr_dve, pr_act, pr_pe = sem("prep_dve"), sem("prep_act"), sem("prep_pe")
        rw_dve, rw_act, rw_pe, rw_pool = sem("rwkv_dve"), sem("rwkv_act"), sem("rwkv_pe"), sem("rwkv_pool")
        rs_dve, rs_act, rs_pe, rs_in, rs_out = (sem(f"rsample_{x}") for x in ("dve", "act", "pe", "in", "out"))
        re_in, re_out, re_dve, re_act, re_pe = (sem(f"ret_{x}") for x in ("in", "out", "dve", "act", "pe"))
        rt_dve, rt_act, rt_pe, rt_pool = (sem(f"retchunk_{x}") for x in ("dve", "act", "pe", "pool"))
        fn_dve, fn_act, fn_pe = (sem(f"foxnorm_{x}") for x in ("dve", "act", "pe"))
        fg_dve, fg_act, fg_pe = (sem(f"gate_{x}") for x in ("dve", "act", "pe"))
        fp_dve, fp_act, fp_pe, fp_pool, fp_ncb = (sem(f"foxprompt_{x}") for x in ("dve", "act", "pe", "pool", "rows_in"))
        fs_dve, fs_pe = sem("foxsample_dve"), sem("foxsample_pe")
        fgr_dve, fgr_act, fgr_pe = (sem(f"foxgroup_{x}") for x in ("dve", "act", "pe"))
        fox_const, fox_out, fox_out2, ko_out = sem("fox_const"), sem("fox_v_out"), sem("fox_v_sample_out"), sem("fox_k_out")
        decay_out, past_in = sem("decay_rows_out"), sem("past_gates_in")
        page_in = [sem(f"pages_in{i}") for i in range(4)]
        table_in, lft_out = sem("table_in"), sem("log_gates_out")
        ro_pe, ro_act, ro_out = sem("rstate_pe"), sem("rstate_act"), sem("rstate_out")
        one_done = sem("one_done")
        passed = sem("passed")
        y_st, y_pe, y_ev, y_out = sem("y_st"), sem("y_pe"), sem("y_ev"), [sem("y_out0"), sem("y_out1")]

        HALF = PJOBS // 2
        NPAST = (NPG + 1) * DB * 16
        NPARAM = 24

        def evac_at(l, j):
            return evac[j % 2], l * HALF + j // 2 + 2

        def job_psum(j):
            s = 3 * (j % 2)
            return ps[:, s:s + 3, 0:TB]

        def job_psum_tm(j):
            s = 3 * (j % 2)
            return ps[:, s:s + 3, :].rearrange("p a (b c) -> p (a b) c", c=P)

        NRM_DVE = Steps(*names("sq", KT), *names("h", KT))
        NRM_PE = Steps(*names("sum", KT))
        NRM_ACT = Steps("ln", "rstd")
        PR_DVE = Steps("zero", "cum0", "st0", "kac", *names("diff", 7), *names("xs", 7),
                       *[f"{a}{m}" for m in range(2) for a in ("kk", "ksq", "kmax", "kkn", "kmul", "bv", "k2")])
        PR_ACT = Steps("tanh", "sg", *[f"{a}{m}" for m in range(2) for a in ("sw", "a")],
                       "ln0", "rn0", "ln1", "rn1")
        PR_PE = Steps(*[f"{a}{m}" for m in range(2) for a in ("w", "a")], "ss0", "ss1")
        RW_POOL = Steps("vs", "sg")
        RW_DVE = Steps("cum0", "cum1", "kp", "kn", "A", "R", "B", "K", "rk2", "sm0", "sm1",
                       "D", "N", "DT", "Z1", "Lrb", "Lak", "Lrk", "Z2", "D8", "Z3", "Z4", "QT", "Y0",
                       "Q2T", "Y1", "Y2", "X0", "s0", "sf0", "sf1",
                       *names("bn", 4), *names("ag", 4), *names("yn", 4), "yw", "yb", *names("bo", 4), "yg")
        RW_ACT = Steps("e0", "e1", "pi0", "pi1", "fm", "vbk", "bon", "D2", "D2T", "D4", "D4T",
                       "Q", "M", "Q2", "Q4", "TT", "U", "ln", "rstd", "ro")
        RW_PE = Steps("L", "tr", "D2", "D2T", "D4", "D4T", "Z2", "D8", "Z3", "Z4", "Q", "QT", "M",
                      "Q2", "Q2T", "Q4", "Y1", "Y2", "TT", "g", "X0", "U", "Y", "dS", "ro")

        RS_DVE = Steps("zero", "cum0", "cum1", "cum2", "cum3", "A0", "A1", "R", "B", "K", "rk2", "vs", "sg", "aex", "rex", "sts",
                       "D", "DT", "Z1", "Lrb", "Lak", "Lrk", "Z2", "X0", *names("uex", 4), *names("vex", 4), "s0", "sf",
                       *names("bn", 4), *names("ag", 4), *names("yn", 4), "yw", "yb", *names("bo", 4), "yg")
        RS_ACT = Steps("e5", "pi5", "vbk", "bon", "D2", "U", "ln", "rstd", "ro", "nat")
        RS_PE = Steps("st", "L", "tr", "D2", "Z2", "g", "X0", "U", "Y", "dS", "ro", "nat")

        NORM4 = (*names("bn", 4), *names("ag", 4), *names("yn", 4), "yw", "yg")
        RE_DVE = Steps("R", *[f"{a}{i}" for i in range(4) for a in ("xc", "ts", "add")],
                       "qd", "qex", "st", "kd", *names("vex", 4), "R0", "R1", *NORM4)
        RE_PE = Steps(*names("rot", 4), "S", "kt", "O", "dR", "ro")
        RE_ACT = Steps("ln", "rstd", "ro")
        RT_POOL = Steps("q", "k", "qd", "v")
        RT_DVE = Steps("st", "kd", "R0", "R1", *NORM4)
        RT_PE = Steps("S", "kt", "O", "dR", "ro")
        RT_ACT = Steps("ln", "rstd", "ro")

        FN_DVE = Steps("sq0", "sq1", "n0", "n1")
        FN_ACT = Steps("ln0", "rs0", "ln1", "rs1")
        FN_PE = Steps("ss0", "ss1")
        FG_DVE = Steps("gq", "z", "abs", "logf", "nc")
        FG_ACT = Steps("exp", "ln", "lft")
        FG_PE = Steps("lft")
        SC = range(2 * NTT)
        FP_POOL = Steps("q", "k", "v", "ncd")
        FP_DVE = Steps(*[x for s in SC for x in ([f"m{s}"] if s >= 2 else []) + [f"d{s}", f"n{s}"] + ([f"pt{s}"] if s % 2 else []) + [f"r{s}", f"o{s}"]])
        FP_ACT = Steps("ko", "kos", *[x for s in SC for x in [f"e{s}"] + ([f"pt{s}"] if s % 2 == 0 else [])], "oT")
        FP_PE = Steps("ko", "S0", *[x for s in SC for x in ([f"S{s + 1}"] if s + 1 < 2 * NTT else []) + [f"T{s}", f"V{s}"]], "oT")
        FS_DVE = Steps("qz", *[f"q{p}{k}" for p in range(4) for k in range(2)], "kn", "vn", "lfs", "lfn", "ncs")
        G_DVE = Steps("cq", "ck", "csel", "creq", *[f"kt{b}{p}" for b in range(4) for p in (1, 3)],
                      "sn", "mx", "mn", "max", "neg", "sum", "rec", "pn", "pne", "pt1", "pnt", "o0", "o1")
        G_ACT = Steps(*[f"kt{b}{p}" for b in range(4) for p in (0, 2)], "e", "en", "pt0")
        G_PE = Steps("bias", *[x for b in range(4) for x in [f"T{b}0"] + [y for p in range(4) for y in ([f"T{b}{p + 1}"] if p < 3 else []) + [f"S{b}{p}"]]],
                     "P0", "P1", "Pn", "V0", "V1", "V2", "V3")

        block = ctx.enter_context(nc.Block())
        w_in = I["w_in"]

        @block.sync
        def _(sp):
            def w_block(l, w, c, kt=KT):
                return w[bass.ds(l, 1), :, bass.ds(c, P)].rearrange("a (k p) c -> p (a k) c", p=P)

            def load(l, j, src):
                sp.dma_start(ring[:, j % RING, :, :], src).then_inc(loaded[j % RING], 16)

            def free(l, j):
                sp.wait_ge(gemm_done, l * PJOBS + j - RING + 1)
                sp.sem_inc(passed, 1)

            RFC = [C_R + P * m for m in range(7)] + [C_FL]
            for j in range(RING):
                load(0, j, w_block(0, w_in, RFC[j]))
            with sp.Fori(0, DEPTH) as l:
                for j in range(RING, 8):
                    free(l, j)
                    load(l, j, w_block(l, w_in, RFC[j]))
                for j0, c0_, n in ((J_EQ, C_EQ, 4), (J_EV, C_EV, 4), (J_FQ, C_FQ, 8), (J_FV, C_FV, 4)):
                    for j in range(j0, j0 + n):
                        free(l, j)
                        load(l, j, w_block(l, w_in, c0_ + P * (j - j0)))
                for j in range(J_OUT, J_OUT + RING):
                    free(l, j)
                    load(l, j, w_block(l, I["w_out"], P * (j - J_OUT)))
                sp.wait_ge(table_in, 16)
                sp.wait_ge(fs_dve, FS_DVE.at(l, "vn"))
                sp.wait_ge(fp_act, FP_ACT.at(l * 4 + 3, "oT"))
                sp.wait_ge(lft_out, l * 32 + 32)
                sp.wait_ge(ko_out, l * 128 + 128)
                sp.wait_ge(fox_out, l * 16 + 16)
                sp.sem_inc(passed, 1)
                with sp.Fori(0, 2) as g:
                    it = l * 2 + g
                    for kind in range(2):
                        for b in range(4):
                            if kind == 1:
                                sp.wait_ge(fgr_pe, G_PE.at(it, f"T{b}3"))
                                sp.sem_inc(passed, 1)
                            for j in range(NPG):
                                page = sp.value_load(ptab[0:1, bass.ds(g * (4 * NPG) + (b * NPG + j), 1)], min_val=0, max_val=N_POOL - 1)
                                sp.dma_start(slot[b][:, j, :], I["cache_fox_k" if kind == 0 else "cache_fox_v"][bass.ds(l, 1), bass.ds(page, 1)].rearrange(
                                    "a n p h d -> p (a n h d)")).then_inc(page_in[b], 16)
                    sp.wait_ge(fgr_pe, G_PE.at(it, "V3"))
                    sp.sem_inc(passed, 1)
                for j in range(J_OUT + RING, J_FF):
                    free(l, j)
                    load(l, j, w_block(l, I["w_out"], P * (j - J_OUT)))
                with sp.Fori(0, FT // 2) as q:
                    for u in range(RING):
                        sp.wait_ge(gemm_done, l * PJOBS + q * RING + (J_FF + u - RING + 1))
                        load(l, u, w_block(l, I["w_gate" if u % 2 == 0 else "w_up"], q * (2 * P) + P * (u // 2)))
                for j in range(2):
                    if j == 0:
                        sp.wait_ge(gemm_done, l * PJOBS + J_OUT + 1)
                    sp.dma_start(wd[:, j, :, :], w_block(l, I["w_down"], P * j)).then_inc(down_loaded[j], 16)
                for j in range(2, KT):
                    sp.wait_ge(gemm_done, l * PJOBS + J_DOWN + j - 2 + 1)
                    sp.dma_start(wd[:, j % 2, :, :], w_block(l, I["w_down"], P * j)).then_inc(down_loaded[j % 2], 16)
                for j in range(RING):
                    sp.wait_ge(gemm_done, l * PJOBS + JOBS - RING + j + 1)
                    sp.sem_inc(passed, 1)
                    load(0, j, w_block(DEPTH - 1 - l, w_in, RFC[j]))
            for s in range(RING):
                sp.wait_ge(loaded[s], 16 * (DEPTH * JOBS // RING + 1))

        @block.gpsimd
        def _(pool):
            cst = I["consts"]

            def const(dst, name, width=None):
                c, w = CONSTS[name]
                pool.dma_start(dst, cst[:, c:c + (width or w)]).then_inc(consts_in, 16)

            const(ident[:, :], "ident")
            const(blk[:, :], "blk")
            pool.dma_start(ptab[:, :], I["page_table"].rearrange("b j -> (b j)").unsqueeze(0)).then_inc(table_in, 16)
            for u in range(2):
                pool.dma_start(xstage[:, u, :], I["x_prompt"][0, P * u:P * u + P, :]).then_inc(x_in[u], 16)
            with pool.Fori(1, NTT // 2) as t:
                for u in range(2):
                    pool.wait_ge(xt_pe, t * 2 + u - 1)
                    pool.dma_start(xstage[:, u, :], I["x_prompt"][0, bass.ds((t * 2 + u) * P, P), :]).then_inc(x_in[u], 16)
            pool.wait_ge(xt_pe, NTT - 1)
            pool.dma_start(xstage[0:NS, 0, :], I["x_sample"].rearrange("b t d -> (b t) d")).then_inc(x_in[0], 16)
            with pool.Fori(0, DEPTH) as l:
                vecs = (("ln_mix", "ln_mix_g", 8), ("ln_ffn", "ln_ffn_g", 8), ("mu", "rwkv_mu", 7), ("w0", "rwkv_w0", 2),
                        ("a0", "rwkv_a0", 2), ("kk", "rwkv_k_k", 2), ("ka", "rwkv_k_a", 2))
                pool.wait_ge(evac[0], l * HALF + 1)
                pool.wait_ge(evac[1], l * HALF + 1)
                pool.wait_ge(one_done, 2)
                with nc.allow_non_contiguous_dma("short parameter vectors"):
                    for name, src, n in vecs:
                        pool.dma_start(cols[:, COLS[name][0]:COLS[name][0] + n],
                                       I[src][bass.ds(l, 1), :].rearrange("a (m p) -> p (a m)", p=P)).then_inc(params_in, 16)
                    for h in range(RH):
                        c = COLS["rk"][0] + h
                        r = slice(HD * (h % 2), HD * (h % 2) + HD)
                        pool.dma_start(cols[r, c:c + 1], I["rwkv_r_k"][bass.ds(l, 1), h, :].rearrange("a d -> d a")).then_inc(params_in, 16)
                    for name, src in (("qn", "fox_qn_g"), ("kn", "fox_kn_g")):
                        for k in range(2):
                            pool.dma_start(cols[HD * k:HD * k + HD, COLS[name][0]:COLS[name][0] + 1],
                                           I[src][bass.ds(l, 1), :].rearrange("a d -> d a")).then_inc(params_in, 16)
                    pool.dma_start(cols[0:FH, COLS["fb"][0]:COLS["fb"][0] + 1],
                                   I["fox_f_b"][bass.ds(l, 1), :].rearrange("a d -> d a")).then_inc(params_in, 16)
                for r0, src, n in ((0, "rwkv_w2", 32), (32, "rwkv_a2", 32), (64, "rwkv_g2", 64)):
                    pool.dma_start(lora[r0:r0 + n, :], I[src][bass.ds(l, 1), :, :].rearrange("a k c -> k (a c)")).then_inc(params_in, 16)
                for k, src in enumerate(("rwkv_lnx_w", "rwkv_lnx_b", "ret_gn_w")):
                    pool.dma_start(rows[:, k, :], I[src][bass.ds(l, 1), :].to_broadcast((P, RW))).then_inc(params_in, 16)
                pool.dma_start(region((wdf, WM), 5 * P), cst[:, CONSTS["m_d"][0]:CONSTS["m_d"][0] + 5 * P]).then_inc(params_in, 16)
                pool.dma_start(region((wdf, SM_), 392), cst[:, CONSTS["s_l"][0]:CONSTS["s_l"][0] + 392]).then_inc(params_in, 16)
                pool.wait_ge(pr_dve, PR_DVE.at(l, "zero"))
                with nc.allow_non_contiguous_dma("feature-major rows"):
                    for m in range(7):
                        pool.dma_start(rp[:, m, 1 + T:PW].rearrange("p (b t) -> p b t", t=TS + 1)[:, :, 0],
                                       I["state_rwkv_shift"][bass.ds(l, 1), :, P * m:P * m + P].rearrange("a b p -> p (a b)")).then_inc(shift_in, 16)
                    pool.wait_ge(*evac_at(l, 6))
                    pool.wait_ge(*evac_at(l, 5))
                    pool.sem_inc(passed, 1)
                    pool.dma_start(O["rwkv_shift_prompt"][bass.ds(l, 1), 0, :].rearrange("a (m p) -> p (a m)", p=P), rp[:, :, T]).then_inc(shift_out, 16)
                    for m in range(7):
                        pool.dma_start(O["rwkv_shift_sample"][bass.ds(l, 1), :, P * m:P * m + P].rearrange("a b p -> p (a b)"),
                                       rp[:, m, 1 + T:PW].rearrange("p (b t) -> p b t", t=TS + 1)[:, :, TS]).then_inc(shift_out, 16)
                pool.wait_ge(pr_dve, PR_DVE.at(l, "xs6"))
                pool.wait_ge(pr_act, PR_ACT.at(l, "sg"))
                pool.sem_inc(passed, 1)
                with pool.Fori(0, NTT) as c:
                    it = l * NTT + c
                    RW_POOL.start()
                    pool.wait_ge(rw_dve, RW_DVE.at(it, "cum0"))
                    RW_POOL.mark(pool.tensor_copy(vs, xs[:, 4:6, bass.ds(c * P, P)]), rw_pool, "vs")
                    pool.wait_ge(rw_pool, RW_POOL.at(it, "vs"))
                    RW_POOL.mark(pool.tensor_copy(sg[64:P], xs[64:P, 6, bass.ds(c * P, P)]), rw_pool, "sg")
                pool.wait_ge(rw_pool, l * (RW_POOL.n * NTT) + RW_POOL.n * NTT)
                pool.wait_ge(rw_act, RW_ACT.at(l * NTT + NTT - 1, "ro"))
                pool.dma_start(nat[0:HD].rearrange("v b (h k) -> v (b h) k", h=RH),
                               I["state_rwkv"][bass.ds(l, 1)].rearrange("a b h v k -> v (a b h) k")).then_inc(rs_in, 16)
                pool.wait_ge(ro_act, l + 1)
                pool.sem_inc(passed, 1)
                pool.dma_start(O["rwkv_state_prompt"][bass.ds(l, 1), 0].rearrange("a h v k -> v (a h) k"),
                               sl[9][0:HD, 0:2, :].rearrange("v m (h k) -> v (m h) k", h=2)).then_inc(ro_out, 16)
                pool.wait_ge(rs_act, RS_ACT.at(l, "nat"))
                pool.sem_inc(passed, 1)
                pool.dma_start(O["rwkv_state_sample"][bass.ds(l, 1)].rearrange("a b h v k -> v (a b h) k"),
                               nat_out[0:HD].rearrange("v b (h k) -> v (b h) k", h=RH)).then_inc(rs_out, 16)
                pool.wait_ge(rs_dve, RS_DVE.at(l, "vex3"))
                pool.sem_inc(passed, 1)
                for dst, name, w in ((rconst, "cross", 2886), (region((big, RS0), 198), "s_dmask", 198), (rot, "rot", P)):
                    pool.dma_start(dst, cst[:, CONSTS[name][0]:CONSTS[name][0] + w]).then_inc(re_in, 16)
                for m in range(2):
                    pool.dma_start(rss[:, m, :, :], I["state_ret"][bass.ds(l, 1), :, 2 * m:2 * m + 2].rearrange("a b h d e -> (h d) (a b) e")).then_inc(re_in, 16)
                pool.wait_ge(re_dve, RE_DVE.at(l, "add3"))
                pool.sem_inc(passed, 1)
                with pool.Fori(0, NTT) as c:
                    it = l * NTT + c
                    tk = bass.ds(c * P, P)
                    RT_POOL.start()
                    RT_POOL.mark(pool.tensor_copy(qs, eqk[:, 0:2, tk]), rt_pool, "q")
                    RT_POOL.mark(pool.tensor_copy(ks, eqk[:, 2:4, tk]), rt_pool, "k")
                    RT_POOL.mark(pool.tensor_tensor(qd, eqk[:, 0:2, tk], cross, ALU.mult), rt_pool, "qd")
                    RT_POOL.mark(pool.tensor_copy(ve, evg[:, bass.ds(c, 1), 0:EW].rearrange("p a e -> p (a e)")), rt_pool, "v")
                    pool.wait_ge(rt_pe, RT_PE.at(it, "dR"))
                pool.wait_ge(rt_dve, RT_DVE.at(l * NTT + NTT - 1, "R1"))
                pool.sem_inc(passed, 1)
                pool.dma_start(O["ret_state_prompt"][bass.ds(l, 1), 0].rearrange("a (m h) d e -> (h d) (a m) e", m=2), rst).then_inc(re_out, 16)
                pool.wait_ge(re_dve, RE_DVE.at(l, "R1"))
                pool.sem_inc(passed, 1)
                for m in range(2):
                    pool.dma_start(O["ret_state_sample"][bass.ds(l, 1), :, 2 * m:2 * m + 2].rearrange("a b h d e -> (h d) (a b) e"), rss[:, m, :, :]).then_inc(re_out, 16)
                pool.wait_ge(*evac_at(l, J_OUT - 2))
                pool.wait_ge(*evac_at(l, J_OUT - 1))
                pool.dma_start(O["fox_v_prompt"][bass.ds(l, 1)].rearrange("a n p h d -> p (a n) (h d)"), fv[:, 0:NTT, :]).then_inc(fox_out, 16)
                pool.dma_start(O["fox_v_sample"][bass.ds(l, 1)].rearrange("a b t h d -> (a b t) (h d)"), fv[0:NS, NTT, :]).then_inc(fox_out2, 16)
                pool.wait_ge(fg_act, FG_ACT.at(l, "lft"))
                pool.sem_inc(passed, 1)
                lf3 = lft.rearrange("p (n h) -> p n h", h=FH)
                pool.dma_start(O["fox_logf_prompt"][bass.ds(l, 1)].rearrange("a n p h -> p (a n) h"), lf3[:, 0:NTT, :]).then_inc(lft_out, 16)
                pool.dma_start(O["fox_logf_sample"][bass.ds(l, 1)].rearrange("a b t h -> (a b t) h"), lf3[0:NS, NTT, :]).then_inc(lft_out, 16)
                pool.wait_ge(fg_dve, FG_DVE.at(l, "nc"))
                pool.sem_inc(passed, 1)
                pool.dma_start(decay_rows, ncr).then_inc(decay_out, 16)
                pool.dma_start(fmask, cst[:, CONSTS["fmask"][0]:CONSTS["fmask"][0] + P]).then_inc(fox_const, 16)
                pool.wait_ge(decay_out, l * 16 + 16)
                pool.sem_inc(passed, 1)
                with pool.Fori(0, 4) as p:
                    it = l * 4 + p
                    FP_POOL.start()
                    pool.dma_start(ncb, decay_rows[bass.ds(p * 2, 2), :].unsqueeze(0).to_broadcast((P, 2, T))).then_inc(fp_ncb, 16)
                    FP_POOL.mark(pool.tensor_copy(qtp, fqk[:, bass.ds(p, 1), :].rearrange("p a t -> p (a t)")), fp_pool, "q")
                    FP_POOL.mark(pool.tensor_copy(ktp, fqk[:, bass.ds(p + 4, 1), :].rearrange("p a t -> p (a t)")), fp_pool, "k")
                    FP_POOL.mark(pool.tensor_copy(vp, fv[:, 0:NTT, bass.ds(p * P, P)]), fp_pool, "v")
                    pool.wait_ge(fp_ncb, it * 16 + 16)
                    pool.wait_ge(fox_const, l * 64 + 16)
                    FP_POOL.mark(pool.tensor_tensor(ncd, ncb.rearrange("p a (i t) -> p (a i) t", t=P), fmask.unsqueeze(1).to_broadcast((P, 2 * NTT, P)), ALU.add), fp_pool, "ncd")
                    pool.wait_ge(fp_act, FP_ACT.at(it, "kos"))
                    pool.dma_start(O["fox_k_prompt"][bass.ds(l, 1), :, :, bass.ds(p * 2, 2), :].rearrange("a n p h d -> p (a n) (h d)"), ko).then_inc(ko_out, 16)
                    pool.dma_start(O["fox_k_sample"][bass.ds(l, 1), :, :, bass.ds(p * 2, 2), :].rearrange("a b t h d -> (a b t) (h d)"), kos[0:NS]).then_inc(ko_out, 16)
                    pool.wait_ge(fp_act, FP_ACT.at(it, "oT"))
                    pool.wait_ge(ko_out, it * 32 + 32)
                for dst, name, w in ((ssel, "s_sel", 2 * P), (sreq, "s_req", 2 * DB), (sfm, "s_fmask", TS)):
                    pool.dma_start(dst, cst[:, CONSTS[name][0]:CONSTS[name][0] + w]).then_inc(fox_const, 16)
                for b in range(DB):
                    pool.dma_start(ncs[FH * b:FH * b + FH, NP:NP + TS], fl[0:FH, T + TS * b:T + TS * b + TS]).then_inc(past_in, 16)
                pool.wait_ge(table_in, 16)
                with pool.Fori(0, DB) as b:
                    for j in range(NPG):
                        page = pool.value_load(ptab[0:1, bass.ds(b * NPG + j, 1)], min_val=0, max_val=N_POOL - 1)
                        pool.dma_start(lfp[:, j, bass.ds(b * FH, FH)], I["cache_fox_logf"][bass.ds(l, 1), bass.ds(page, 1)].rearrange("a n p h -> p (a n h)")).then_inc(past_in, 16)
            pool.wait_ge(fox_out, DEPTH * 16)
            pool.wait_ge(fox_out2, DEPTH * 16)
            pool.wait_ge(lft_out, DEPTH * 32)
            pool.wait_ge(ko_out, DEPTH * 128)
            pool.wait_ge(re_out, DEPTH * 48)
            pool.wait_ge(shift_out, DEPTH * 8 * 16)
            pool.wait_ge(rs_out, DEPTH * 16)
            pool.wait_ge(ro_out, DEPTH * 16)
            with pool.Fori(0, NTT // 2) as t:
                for u in range(2):
                    pool.wait_ge(y_ev, t * 2 + u + 1)
                    pool.dma_start(O["y_prompt"][0, bass.ds((t * 2 + u) * P, P), :], yrows[:, u, :]).then_inc(y_out[u], 16)
            pool.wait_ge(y_ev, NTT + 1)
            pool.dma_start(O["y_sample"].rearrange("b t d -> (b t) d"), yrows[0:NS, 0, :]).then_inc(y_out[0], 16)
            pool.wait_ge(y_out[0], 16 * (NTT // 2 + 1))
            pool.wait_ge(y_out[1], 16 * (NTT // 2))

        @block.tensor
        def _(pe):
            def mm(out, lhsT, rhs, start=True, stop=True):
                return pe.matmul(out, lhsT, rhs, start=start, stop=stop, skip_group_check=True)

            def tr(out, in_):
                n = in_.shape[0]
                return pe.transpose(out, in_, ident[0:n, 0:n])

            def norm_sums(l, which):
                it = 2 * l + which
                NRM_PE.start()
                for k in range(KT):
                    pe.wait_ge(n_dve, NRM_DVE.at(it, f"sq{k}"))
                    for b in range(3):
                        last = mm(ps[:, b, 0:TB], ones[:, :], nsq[:, k % 2, TB * b:TB * b + TB], k == 0, k == KT - 1)
                    NRM_PE.mark(last, n_pe, f"sum{k}")

            def job_fm(l, j, rhs, u=0, q=0):
                pe.wait_ge(loaded[j % RING], l * (16 * JOBS // RING) + q * 16 + 16 * (j // RING + 1))
                pe.wait_ge(evac[j % 2], l * HALF + q * 2 + (j // 2 + 1))
                for b in range(3):
                    for k in range(KT):
                        last = mm(ps[:, 3 * (j % 2) + b, 0:TB], ring[:, j % RING, k, :], rhs(k)[:, TB * b:TB * b + TB], k == 0, k == KT - 1)
                last.then_inc(gemm_done, 1)

            def job_tm(l, j):
                pe.wait_ge(loaded[j % RING], l * (16 * JOBS // RING) + 16 * (j // RING + 1))
                pe.wait_ge(evac[j % 2], l * HALF + (j // 2 + 1))
                for i in range(NTT + 1):
                    n = P if i < NTT else NS
                    for k in range(KT):
                        last = mm(ps[0:n, 3 * (j % 2) + i // 4, P * (i % 4):P * (i % 4) + P], hT[:, k, P * i:P * i + n], ring[:, j % RING, k, :], k == 0, k == KT - 1)
                last.then_inc(gemm_done, 1)

            def h_tile(k):
                return hT[:, k, :]

            def col2(name, i):
                return cols[:, COLS[name][0] + i:COLS[name][0] + i + 2]

            pe.wait_ge(consts_in, 2 * 16)
            with pe.Fori(0, NTT // 2) as t:
                for u in range(2):
                    pe.wait_ge(x_in[u], t * 16 + 16)
                    pe.wait_ge(xt_ev, t * 2 + u + 1)
                    for k in range(KT):
                        last = tr(ps[:, 4 * u + k // 4, P * (k % 4):P * (k % 4) + P], xstage[:, u, P * k:P * k + P])
                    last.then_inc(xt_pe, 1)
            pe.wait_ge(x_in[0], 16 * (NTT // 2 + 1))
            pe.wait_ge(xt_ev, NTT + 1)
            for k in range(KT):
                last = tr(ps[:, 0, NS * k:NS * k + NS], xstage[0:NS, 0, P * k:P * k + P])
            last.then_inc(xt_pe, 1)

            with pe.Fori(0, DEPTH) as l:
                norm_sums(l, 0)
                pe.wait_ge(n_dve, NRM_DVE.at(2 * l, "h7"))
                for j in range(J_R, J_EQ):
                    job_fm(l, j, h_tile)

                PR_PE.start()
                for m in range(2):
                    for s, (name, r0) in enumerate((("w", 0), ("a", 32))):
                        if m == 0:
                            pe.wait_ge(*((pr_act, PR_ACT.at(l, "tanh")) if s == 0 else (pr_dve, PR_DVE.at(l, "xs6"))))
                            if s == 0:
                                pe.wait_ge(*evac_at(l, 6))
                                pe.wait_ge(*evac_at(l, 7))
                                pe.wait_ge(params_in, l * (16 * NPARAM) + 16 * NPARAM)
                        else:
                            pe.wait_ge(pr_act, PR_ACT.at(l, f"{'sw' if s == 0 else 'a'}0"))
                        for b, (a, e) in enumerate(((0, 512), (512, 1024), (1024, XW))):
                            last = mm(ps[:, 4 * s + b, 0:e - a], lora[r0:r0 + 32, P * m:P * m + P], xs[r0:r0 + 32, 6, a:e])
                        PR_PE.mark(last, pr_pe, f"{name}{m}")
                for m in range(2):
                    pe.wait_ge(pr_dve, PR_DVE.at(l, f"ksq{m}"))
                    pe.wait_ge(*((pr_act, PR_ACT.at(l, "a1")) if m == 0 else (pr_dve, PR_DVE.at(l, "kmax0"))))
                    for b, (a, e) in enumerate(((0, 512), (512, 1024), (1024, XW))):
                        last = mm(ps[:, b, 0:e - a], blk[:, :], sq1[:, a:e])
                    PR_PE.mark(last, pr_pe, f"ss{m}")

                pe.wait_ge(pr_dve, PR_DVE.at(l, "k21"))
                pe.sem_inc(passed, 1)
                with pe.Fori(0, NTT) as c:
                    it = l * NTT + c
                    RW_PE.start()

                    def heads(name, bank, lhsT, rhs, waits, width=P):
                        for s, v in waits:
                            pe.wait_ge(s, v)
                        for h in range(RH):
                            o = ps[:, bank, width * h:width * h + width]
                            last = mm(o, lhsT(h), rhs(h))
                        RW_PE.mark(last, rw_pe, name)

                    def dv(n):
                        return (rw_dve, RW_DVE.at(it, n))

                    def ac(n):
                        return (rw_act, RW_ACT.at(it, n))

                    pos = lambda h: 2 * (h % 2) + h // 2
                    half = lambda h: slice(HD * (h % 2), HD * (h % 2) + HD)
                    S = lambda i: (lambda h: sl[i][:, h, :])
                    pe.wait_ge(*dv("rk2"))
                    for h in range(RH):
                        m, r = h // 2, half(h)
                        arh = ar[r, m, :, :].rearrange("p a t -> p (a t)")
                        mm(ps[:, h % 2, 256 * m:256 * m + 256], bt[r, m, :], arh)
                        mm(ps[:, 2 + h % 2, 256 * m:256 * m + 256], kt_[r, m, :], arh)
                        last = mm(ps[:, 4 + h % 2, P * m:P * m + P], ar[r, m, 0, :], bt[r, m, :])
                    RW_PE.mark(last, rw_pe, "L")
                    pe.wait_ge(rw_pool, RW_POOL.at(it, "sg"))
                    for m in range(2):
                        tr(ps[:, 6, P * m:P * m + P], vs[:, m, :])
                        tr(ps[:, 6, 256 + P * m:256 + P * m + P], bt[:, m, :])
                        tr(ps[:, 7, P * m:P * m + P], kt_[:, m, :])
                        last = mm(ps[:, 7, 256 + 2 * m:258 + 2 * m], rk2[:, m, :], col2("rk", 2 * m))
                    RW_PE.mark(last, rw_pe, "tr")
                    heads("D2", 0, S(5), S(4), [dv("Lrk")])
                    heads("D2T", 1, S(4), S(5), [])
                    heads("D4", 2, S(7), S(6), [ac("D2T")])
                    heads("D4T", 3, S(6), S(7), [])
                    heads("Z2", 4, S(6), S(8), [])
                    heads("D8", 0, S(5), S(4), [ac("D4T")])
                    heads("Z3", 1, S(4), S(8), [dv("Z2")])
                    heads("Z4", 2, S(6), S(8), [dv("Z3")])
                    heads("Q", 3, S(8), S(0), [dv("Z4")])
                    heads("QT", 4, S(0), S(8), [])
                    for h in range(RH):
                        last = tr(ps[:, 0, P * h:P * h + P], sl[8][:, h, :])
                    RW_PE.mark(last, rw_pe, "M")
                    heads("Q2", 1, S(5), S(4), [ac("Q"), dv("Y0")])
                    heads("Q2T", 2, S(4), S(5), [])
                    heads("Q4", 3, S(7), S(6), [ac("Q2"), dv("Q2T")])
                    heads("Y1", 4, S(6), S(10), [])
                    heads("Y2", 0, S(4), S(10), [ac("Q4"), dv("Y1")])
                    heads("TT", 1, S(9), S(10), [dv("Y2")])
                    pe.wait_ge(*ac("bon"))
                    last = mm(ps[:, 7, 0:RW], sg[64:P, :], lora[64:P, :])
                    RW_PE.mark(last, rw_pe, "g")
                    vtok = lambda h: vbk[:, h // 2, half(h)]
                    btok = lambda h: vbk[:, 2 + h // 2, half(h)]
                    ktok = lambda h: vbk[:, 4 + h // 2, half(h)]
                    x0 = lambda h: sl[4][:, 0:2, :].rearrange("p a b -> p (a b)")[:, HD * h:HD * h + HD]
                    uu = lambda h: sl[5][:, 0:2, :].rearrange("p a b -> p (a b)")[:, HD * h:HD * h + HD]
                    for h in range(RH):
                        m, r = h // 2, half(h)
                        mm(ps[:, 2 + h % 2, HD * m:HD * m + HD], ar[r, m, 0, :], stm[r, m, :], True, False)
                        last = mm(ps[:, 2 + h % 2, HD * m:HD * m + HD], sl[1][:, pos(h), :], vtok(h), False, True)
                    RW_PE.mark(last, rw_pe, "X0")
                    pe.wait_ge(*ac("TT"))
                    pe.wait_ge(*dv("X0"))
                    for h in range(RH):
                        last = mm(ps[:, 6, HD * h:HD * h + HD], sl[8][:, pos(h), :], x0(h))
                    RW_PE.mark(last, rw_pe, "U")
                    for h in range(RH):
                        m, r = h // 2, half(h)
                        o = ps[:, 4 - h % 2, HD * m:HD * m + HD]
                        mm(o, ar[r, m, 1, :], stm[r, m, :], True, False)
                        mm(o, sl[3][:, pos(h), :], vtok(h), False, False)
                        if h == 0:
                            pe.wait_ge(*ac("U"))
                        last = mm(o, sl[2][:, pos(h), :], uu(h), False, True)
                    RW_PE.mark(last, rw_pe, "Y")
                    for h in range(RH):
                        m, r = h // 2, half(h)
                        o = ps[r, 5, HD * m:HD * m + HD]
                        mm(o, btok(h), uu(h), True, False)
                        last = mm(o, ktok(h), vtok(h), False, True)
                    RW_PE.mark(last, rw_pe, "dS")
                    pe.wait_ge(*dv("yg"))
                    for m in range(2):
                        last = tr(ps[:, 6, P * m:P * m + P], sl[6][:, m, :])
                    RW_PE.mark(last, rw_pe, "ro")
                pe.wait_ge(rw_act, RW_ACT.at(l * NTT + NTT - 1, "ro"))
                pe.sem_inc(passed, 1)
                for m in range(2):
                    last = tr(ps[0:HD, 0, P * m:P * m + P], st[:, m, :])
                last.then_inc(ro_pe, 1)

                RS_PE.start()
                ac = lambda n: (rs_act, RS_ACT.at(l, n))
                dv = lambda n: (rs_dve, RS_DVE.at(l, n))
                SR = slice(0, NS)
                pe.wait_ge(rs_in, l * 16 + 16)
                pe.wait_ge(ro_act, l + 1)
                pe.sem_inc(passed, 1)
                for m in range(2):
                    for b in range(DB):
                        last = tr(ps[:, m, HD * b:HD * b + HD], nat[0:HD, b, P * m:P * m + P])
                RS_PE.mark(last, rs_pe, "st")
                pe.wait_ge(*dv("sts"))
                pe.sem_inc(passed, 1)
                for h in range(RH):
                    m, r = h // 2, half(h)
                    arh = ars[r, m, :, :].rearrange("p a t -> p (a t)")
                    mm(ps[SR, h % 2, 64 * m:64 * m + 64], bts[r, m, :], arh)
                    mm(ps[SR, 2 + h % 2, 64 * m:64 * m + 64], kts[r, m, :], arh)
                    last = mm(ps[SR, 4 + h % 2, NS * m:NS * m + NS], ars[r, m, 0, :], bts[r, m, :])
                RS_PE.mark(last, rs_pe, "L")
                for m in range(2):
                    tr(ps[SR, 6, P * m:P * m + P], vss[:, m, :])
                    tr(ps[SR, 6, 256 + P * m:256 + P * m + P], bts[:, m, :])
                    tr(ps[SR, 7, P * m:P * m + P], kts[:, m, :])
                    last = mm(ps[SR, 7, 256 + 2 * m:258 + 2 * m], rk2s[:, m, :], col2("rk", 2 * m))
                RS_PE.mark(last, rs_pe, "tr")
                pe.wait_ge(*dv("Lrk"))
                pe.sem_inc(passed, 1)
                for h in range(RH):
                    last = mm(ps[SR, 0, NS * h:NS * h + NS], smat[1][SR, h, :], smat[0][SR, h, :])
                RS_PE.mark(last, rs_pe, "D2")
                pe.wait_ge(*ac("D2"))
                pe.sem_inc(passed, 1)
                for h in range(RH):
                    last = mm(ps[SR, 1, NS * h:NS * h + NS], smat[2][SR, h, :], smat[3][SR, h, :])
                RS_PE.mark(last, rs_pe, "Z2")
                last = mm(ps[SR, 7, 0:RW], sgs[64:P, :], lora[64:P, :])
                RS_PE.mark(last, rs_pe, "g")
                vts = lambda h: vbks[SR, h // 2, half(h)]
                hd = lambda t, h: t[SR, HD * h:HD * h + HD]
                for h in range(RH):
                    m, r = h // 2, half(h)
                    o = ps[SR, 2 + h % 2, HD * m:HD * m + HD]
                    for b in range(DB):
                        mm(o, aex[r, m, b, :], sts[r, m, b, :], b == 0, False)
                    last = mm(o, smat[5][SR, pos(h), :], vts(h), False, True)
                RS_PE.mark(last, rs_pe, "X0")
                pe.wait_ge(*dv("X0"))
                pe.sem_inc(passed, 1)
                for h in range(RH):
                    last = mm(ps[SR, 6, HD * h:HD * h + HD], smat[3][SR, pos(h), :], hd(x0s, h))
                RS_PE.mark(last, rs_pe, "U")
                pe.wait_ge(*ac("U"))
                pe.sem_inc(passed, 1)
                for h in range(RH):
                    m, r = h // 2, half(h)
                    o = ps[SR, 4 - h % 2, HD * m:HD * m + HD]
                    for b in range(DB):
                        mm(o, rex[r, m, b, :], sts[r, m, b, :], b == 0, False)
                    mm(o, smat[6][SR, pos(h), :], vts(h), False, False)
                    last = mm(o, smat[4][SR, pos(h), :], hd(us, h), False, True)
                RS_PE.mark(last, rs_pe, "Y")
                pe.wait_ge(*dv("vex3"))
                for h in range(RH):
                    m, r = h // 2, half(h)
                    o = ps[r, m, :]
                    mm(o, vbks[SR, 2 + m, half(h)], uex[SR, h].rearrange("p b d -> p (b d)"), True, False)
                    last = mm(o, vbks[SR, 4 + m, half(h)], vex[SR, h].rearrange("p b d -> p (b d)"), False, True)
                RS_PE.mark(last, rs_pe, "dS")
                pe.wait_ge(*dv("yg"))
                pe.sem_inc(passed, 1)
                for m in range(2):
                    last = tr(ps[:, 6, NS * m:NS * m + NS], yns[SR, P * m:P * m + P])
                RS_PE.mark(last, rs_pe, "ro")
                for m in range(2):
                    for b in range(DB):
                        last = tr(ps[0:HD, 2 * m + b // 4, P * (b % 4):P * (b % 4) + P], sts[:, m, b, :])
                RS_PE.mark(last, rs_pe, "nat")

                pe.wait_ge(*ac("nat"))
                pe.wait_ge(ro_act, l + 1)
                for j in range(J_EQ, J_EV):
                    job_fm(l, j, h_tile)
                for j in range(J_EV, J_FQ):
                    job_tm(l, j)
                pe.wait_ge(*evac_at(l, J_EV + 2))
                pe.wait_ge(*evac_at(l, J_EV + 3))
                pe.wait_ge(re_in, l * 80 + 80)
                RE_PE.start()
                for i in range(4):
                    if i >= 2:
                        pe.wait_ge(re_dve, RE_DVE.at(l, f"ts{i - 2}"))
                    for b in range(3):
                        last = mm(ps[:, 3 * (i % 2) + b, 0:TB], rot, eqk[:, i, TB * b:TB * b + TB])
                    RE_PE.mark(last, re_pe, f"rot{i}")
                pe.wait_ge(re_dve, RE_DVE.at(l, "add3"))
                pe.sem_inc(passed, 1)
                with pe.Fori(0, NTT) as c:
                    it = l * NTT + c
                    RT_PE.start()
                    pe.wait_ge(rt_pool, RT_POOL.at(it, "v"))
                    for h in range(EH):
                        m, r = h // 2, half(h)
                        last = mm(ps[:, h % 2, P * m:P * m + P], ks[r, m, :], qs[r, m, :])
                    RT_PE.mark(last, rt_pe, "S")
                    for m in range(2):
                        last = tr(ps[:, 2, P * m:P * m + P], ks[:, m, :])
                    RT_PE.mark(last, rt_pe, "kt")
                    pe.wait_ge(rt_dve, RT_DVE.at(it, "st"))
                    for h in range(EH):
                        m, r = h // 2, half(h)
                        o = ps[:, 4 - h % 2, HD * m:HD * m + HD]
                        mm(o, stt[:, pos(h), :], ve[:, HD * h:HD * h + HD], True, False)
                        last = mm(o, qd[r, m, :], rst[r, m, :], False, True)
                    RT_PE.mark(last, rt_pe, "O")
                    pe.wait_ge(rt_dve, RT_DVE.at(it, "kd"))
                    for h in range(EH):
                        last = mm(ps[half(h), 5, HD * (h // 2):HD * (h // 2) + HD], kd[:, h, :], ve[:, HD * h:HD * h + HD])
                    RT_PE.mark(last, rt_pe, "dR")
                    pe.wait_ge(rt_dve, RT_DVE.at(it, "yg"))
                    for m in range(2):
                        last = tr(ps[:, 6, P * m:P * m + P], yne[:, P * m:P * m + P])
                    RT_PE.mark(last, rt_pe, "ro")
                pe.wait_ge(rt_act, RT_ACT.at(l * NTT + NTT - 1, "ro"))
                pe.sem_inc(passed, 1)
                for h in range(EH):
                    m, r = h // 2, half(h)
                    last = mm(ps[SR, h % 2, NS * m:NS * m + NS], eqk[r, 2 + m, T:NT], eqk[r, m, T:NT])
                RE_PE.mark(last, re_pe, "S")
                for m in range(2):
                    last = tr(ps[SR, 2, P * m:P * m + P], eqk[:, 2 + m, T:NT])
                RE_PE.mark(last, re_pe, "kt")
                pe.wait_ge(re_dve, RE_DVE.at(l, "st"))
                pe.sem_inc(passed, 1)
                for h in range(EH):
                    m, r = h // 2, half(h)
                    o = ps[SR, 4 - h % 2, HD * m:HD * m + HD]
                    mm(o, stts[SR, pos(h), :], evg[SR, NTT, HD * h:HD * h + HD], True, False)
                    for b in range(DB):
                        last = mm(o, qex[r, m, b, :], rss[r, m, b, :], False, b == DB - 1)
                RE_PE.mark(last, re_pe, "O")
                pe.wait_ge(re_dve, RE_DVE.at(l, "vex3"))
                for h in range(EH):
                    last = mm(ps[half(h), h // 2, :], kds[SR, h, :], vexe[SR, h].rearrange("p b e -> p (b e)"))
                RE_PE.mark(last, re_pe, "dR")
                pe.wait_ge(re_dve, RE_DVE.at(l, "yg"))
                pe.sem_inc(passed, 1)
                for m in range(2):
                    last = tr(ps[:, 6, NS * m:NS * m + NS], yne[SR, P * m:P * m + P])
                RE_PE.mark(last, re_pe, "ro")
                pe.wait_ge(re_act, RE_ACT.at(l, "ro"))
                for j in range(J_FQ, J_FV):
                    job_fm(l, j, h_tile)
                for j in range(J_FV, J_OUT):
                    job_tm(l, j)
                pe.wait_ge(*evac_at(l, J_OUT - 1))
                pe.wait_ge(*evac_at(l, J_OUT - 2))
                pe.sem_inc(passed, 1)
                with pe.Fori(0, 4) as i:
                    it = l * 4 + i
                    FN_PE.start()
                    for u in range(2):
                        pe.wait_ge(fn_dve, FN_DVE.at(it, f"sq{u}"))
                        for b in range(3):
                            last = mm(ps[:, 3 * u + b, 0:TB], blk[:, :], fsq[:, u, TB * b:TB * b + TB])
                        FN_PE.mark(last, fn_pe, f"ss{u}")
                FG_PE.start()
                pe.wait_ge(fg_dve, FG_DVE.at(l, "logf"))
                pe.sem_inc(passed, 1)
                for i in range(NTT + 1):
                    n = P if i < NTT else NS
                    last = tr(ps[0:n, 7, FH * i:FH * i + FH], fl[0:FH, P * i:P * i + n])
                FG_PE.mark(last, fg_pe, "lft")
                pe.wait_ge(fg_act, FG_ACT.at(l, "lft"))
                pe.sem_inc(passed, 1)
                with pe.Fori(0, 4) as p:
                    it = l * 4 + p
                    FP_PE.start()
                    fd = lambda n: (fp_dve, FP_DVE.at(it, n))
                    fa = lambda n: (fp_act, FP_ACT.at(it, n))

                    def scores(s):
                        i, hh = s // 2, s % 2
                        if s >= 2:
                            pe.wait_ge(*fd(f"d{s - 2}"))
                        r = slice(HD * hh, HD * hh + HD)
                        for a in range(0, P * (i + 1), 512):
                            e = min(a + 512, P * (i + 1))
                            last = mm(ps[:, 2 * hh + a // 512, 0:e - a], qtp[r, P * i:P * i + P], ktp[r, a:e])
                        FP_PE.mark(last, fp_pe, f"S{s}")

                    pe.wait_ge(fp_pool, FP_POOL.at(it, "v"))
                    for i in range(NTT):
                        tr(ps[:, 4 + i // 4, P * (i % 4):P * (i % 4) + P], ktp[:, P * i:P * i + P])
                    last = tr(ps[0:NS, 6, 0:P], ktp[:, T:NT])
                    FP_PE.mark(last, fp_pe, "ko")
                    scores(0)
                    for s in SC:
                        i, hh = s // 2, s % 2
                        if s + 1 < 2 * NTT:
                            scores(s + 1)
                        pe.wait_ge(*fa(f"e{s}"))
                        pe.wait_ge(*(fa("kos") if s == 0 else fd(f"pt{s - 1}") if (s - 1) % 2 else fa(f"pt{s - 1}")))
                        for k in range(i + 1):
                            last = tr(ps[:, 4 + k // 4, P * (k % 4):P * (k % 4) + P], sp_[:, hh, P * k:P * k + P])
                        FP_PE.mark(last, fp_pe, f"T{s}")
                        pe.wait_ge(*(fd(f"pt{s}") if s % 2 else fa(f"pt{s}")))
                        if s >= 2:
                            pe.wait_ge(*fd(f"o{s - 2}"))
                        for k in range(i + 1):
                            last = mm(ps[:, 6 + hh, 0:HD], ptt[:, hh, k, :], vp[:, k, HD * hh:HD * hh + HD], k == 0, k == i)
                        FP_PE.mark(last, fp_pe, f"V{s}")
                    pe.wait_ge(*fd(f"o{2 * NTT - 1}"))
                    for i in range(NTT):
                        last = tr(ps[:, 4 + i // 4, P * (i % 4):P * (i % 4) + P], otok[:, i, :])
                    FP_PE.mark(last, fp_pe, "oT")
                pe.wait_ge(fp_act, FP_ACT.at(l * 4 + 3, "oT"))
                pe.wait_ge(past_in, l * NPAST + NPAST)
                pe.wait_ge(fox_const, l * 64 + 64)
                pe.sem_inc(passed, 1)
                for j in range(NPG):
                    last = tr(ps[0:DB * FH, j // 4, P * (j % 4):P * (j % 4) + P], lfp[:, j, :])
                last.then_inc(fs_pe, 1)
                with pe.Fori(0, 2) as g:
                    it = l * 2 + g
                    G_PE.start()
                    gd = lambda n: (fgr_dve, G_DVE.at(it, n))
                    ga = lambda n: (fgr_act, G_ACT.at(it, n))
                    ev = lambda b, p: (gd if p % 2 else ga)(f"kt{b}{p}")
                    pe.wait_ge(*gd("creq"))
                    R64 = slice(0, DB * FH)
                    for a in range(2):
                        mm(ps[:, a, :], cur_sel[R64, :], ncs[R64, 512 * a:512 * a + 512], True, False)
                    last = mm(ps[:, 2, 0:TS], cur_sel[R64, :], ncs[R64, NP:NP + TS], True, False)
                    G_PE.mark(last, fgr_pe, "bias")

                    def key_tr(b, p):
                        if b or p >= 2:
                            pe.wait_ge(*(ev(b, p - 2) if p >= 2 else ev(b - 1, p + 2)))
                        for j in range(NPG):
                            last = tr(ps[:, 3 + 2 * (p % 2) + j // 4, P * (j % 4):P * (j % 4) + P], slot[b][:, j, P * p:P * p + P])
                        G_PE.mark(last, fgr_pe, f"T{b}{p}")

                    for b in range(4):
                        pe.wait_ge(page_in[b], it * (2 * NPG * 16) + NPG * 16)
                        key_tr(b, 0)
                        for p in range(4):
                            if p < 3:
                                key_tr(b, p + 1)
                            pe.wait_ge(*ev(b, p))
                            o = slice(NS * b, NS * b + NS)
                            last_one = p == 3
                            for a in range(2):
                                mm(ps[o, a, :], cur_q[:, b, p, :], keyt[p % 2][:, 512 * a:512 * a + 512], False, last_one)
                            last = mm(ps[o, 2, 0:TS], cur_q[:, b, p, :], cur_k[:, p, TS * b:TS * b + TS], False, last_one)
                            G_PE.mark(last, fgr_pe, f"S{b}{p}")
                    pe.wait_ge(*gd("pn"))
                    for c in range(2):
                        for j in range(4 * c, 4 * c + 4):
                            last = tr(ps[:, 3 + c, P * (j % 4):P * (j % 4) + P], pss[:, P * j:P * j + P])
                        G_PE.mark(last, fgr_pe, f"P{c}")
                    pe.wait_ge(*gd("pne"))
                    last = tr(ps[0:NS, 5, 0:P], pn.rearrange("p b s -> p (b s)"))
                    G_PE.mark(last, fgr_pe, "Pn")
                    pe.wait_ge(*gd("pnt"))
                    pe.wait_ge(*ga("pt0"))
                    for b in range(4):
                        pe.wait_ge(page_in[b], it * (2 * NPG * 16) + 2 * NPG * 16)
                        for p in range(4):
                            o = ps[:, 7, 32 * p + 8 * b:32 * p + 8 * b + 8]
                            c = slice(NS * b + 8 * p, NS * b + 8 * p + 8)
                            for j in range(NPG):
                                mm(o, slot[b][:, j, P * p:P * p + P], pts[:, j, c], j == 0, False)
                            last = mm(o, vn[0:NS, P * p:P * p + P], pnt[0:NS, c], False, True)
                        G_PE.mark(last, fgr_pe, f"V{b}")
                pe.wait_ge(fgr_dve, G_DVE.at(l * 2 + 1, "o1"))
                for j in range(J_OUT, J_FF):
                    job_fm(l, j, lambda k: hT[:, k, :] if k < 4 else mixB[:, k - 4, :])
                norm_sums(l, 1)
                pe.wait_ge(n_dve, NRM_DVE.at(2 * l + 1, "h7"))
                pe.sem_inc(passed, 1)
                with pe.Fori(0, FT // 2) as q:
                    for u in range(RING):
                        job_fm(l, J_FF + u, h_tile, q=q)
                pe.wait_ge(*evac_at(l, JOBS - 1))
                for j in range(KT):
                    pe.wait_ge(down_loaded[j % 2], l * (16 * KT // 2) + 16 * (j // 2 + 1))
                    pe.wait_ge(evac[j % 2], l * HALF + ((J_DOWN + j) // 2 + 1))
                    for b in range(3):
                        for k in range(FT):
                            last = mm(ps[:, 3 * (j % 2) + b, 0:TB], wd[:, j % 2, k, :], h2[:, k, TB * b:TB * b + TB], k == 0, k == FT - 1)
                    last.then_inc(gemm_done, 1)
            def y_tile(t, u):
                pe.wait_ge(y_st, t * 2 + (u + 1))
                for k in range(KT):
                    last = tr(ps[:, 4 * u + k // 4, P * (k % 4):P * (k % 4) + P], ytile[:, k, :])
                last.then_inc(y_pe, 1)

            for u in range(2):
                y_tile(0, u)
            with pe.Fori(1, NTT // 2) as t:
                for u in range(2):
                    pe.wait_ge(y_ev, t * 2 + (u - 1))
                    y_tile(t, u)
            pe.wait_ge(y_ev, NTT - 1)
            pe.wait_ge(y_st, NTT + 1)
            for k in range(KT):
                last = tr(ps[0:NS, k // 4, P * (k % 4):P * (k % 4) + P], ytile[:, k, 0:NS])
            last.then_inc(y_pe, 1)

        @block.vector
        def _(v):
            def on(*waits):
                for s, val in waits:
                    v.wait_ge(s, val)

            def norm(l, which, gain):
                it = 2 * l + which
                NRM_DVE.start()
                for k in range(KT):
                    if k >= 2:
                        on((n_pe, NRM_PE.at(it, f"sum{k - 2}")))
                    NRM_DVE.mark(v.tensor_tensor(nsq[:, k % 2, :], xT[:, k, :], xT[:, k, :], ALU.mult), n_dve, f"sq{k}")
                on((n_act, NRM_ACT.at(it, "rstd")), (params_in, l * (16 * NPARAM) + 16 * NPARAM))
                for k in range(KT):
                    NRM_DVE.mark(v.scalar_tensor_tensor(hT[:, k, :], xT[:, k, :], col(gain, k), nrs, ALU.mult, ALU.mult), n_dve, f"h{k}")

            v.memset(ones[:, :], 1.0).then_inc(one_done, 1)
            v.memset(cols[:, :], 0.0).then_inc(one_done, 1)
            v.sem_inc(evac[0], 1)
            v.sem_inc(evac[1], 1)
            v.sem_inc(xt_ev, 2)
            v.wait_ge(one_done, 2)
            with v.Fori(0, NTT // 2) as t:
                for u in range(2):
                    v.wait_ge(xt_pe, t * 2 + u + 1)
                    v.tensor_copy(xT[:, :, bass.ds((t * 2 + u) * P, P)],
                                  ps[:, 4 * u:4 * u + 2, :].rearrange("p a (b c) -> p (a b) c", c=P)).then_inc(xt_ev, 1)
            v.wait_ge(xt_pe, NTT + 1)
            v.tensor_copy(xT[:, :, T:NT], ps[:, 0, 0:KT * NS].rearrange("p (a b) -> p a b", a=KT)).then_inc(xt_ev, 1)
            v.wait_ge(xt_ev, NTT + 3)

            def evac_tm(l, j, dst, n):
                v.wait_ge(gemm_done, l * PJOBS + j + 1)
                v.tensor_copy(dst[:, 0:NTT, P * n:P * n + P], job_psum_tm(j)[:, 0:NTT, :])
                v.tensor_copy(dst[0:NS, NTT, P * n:P * n + P], job_psum_tm(j)[0:NS, NTT, :]).then_inc(evac[j % 2], 1)

            def evac_rows(l, j):
                v.wait_ge(gemm_done, l * PJOBS + j + 1)
                s = 3 * (j % 2)
                v.tensor_copy(rp[:, j, 1:1 + 2 * TB].rearrange("p (a b) -> p a b", a=2), ps[:, s:s + 2, 0:TB])
                v.tensor_copy(rp[:, j, 1 + 2 * TB:1 + T], ps[:, s + 2, 0:T - 2 * TB])
                v.tensor_copy(rp[:, j, 1 + T:PW].rearrange("p (b t) -> p b t", t=TS + 1)[:, :, 1:],
                              ps[:, s + 2, T - 2 * TB:TB].rearrange("p (b t) -> p b t", t=TS)).then_inc(evac[j % 2], 1)

            with v.Fori(0, DEPTH) as l:
                norm(l, 0, "ln_mix")
                pd = lambda n: (pr_dve, PR_DVE.at(l, n))
                pa = lambda n: (pr_act, PR_ACT.at(l, n))
                mark = PR_DVE.mark
                PR_DVE.start()
                on((n_dve, NRM_DVE.at(2 * l, "h7")))
                mark(v.memset(rp[:, :, 0], 0.0), pr_dve, "zero")
                mark(v.memset(cum[:, :, 0], 0.0), pr_dve, "cum0")
                mark(v.memset(st, 0.0), pr_dve, "st0")
                mark(v.tensor_scalar(kac, cols[:, COLS["ka"][0]:COLS["ka"][0] + 2], -1.0, 1.0, ALU.mult, ALU.add), pr_dve, "kac")
                for j in (0, 2, 4, 6):
                    evac_rows(l, j)
                on((shift_in, l * (7 * 16) + 7 * 16))
                for m in range(7):
                    on(evac_at(l, m))
                    mark(v.tensor_tensor(xs[:, m, :], rp[:, m, 0:XW], rp[:, m, 1:PW], ALU.subtract), pr_dve, f"diff{m}")
                for m in range(7):
                    on(pd(f"diff{m}"))
                    mark(v.scalar_tensor_tensor(xs[:, m, :], xs[:, m, :], col("mu", m), rp[:, m, 1:PW], ALU.mult, ALU.add), pr_dve, f"xs{m}")
                on((shift_out, l * (8 * 16) + 8 * 16), pd("xs6"))
                psf = ps[:, 0:3, :].rearrange("p a b -> p (a b)")[:, 0:XW]
                for m in range(2):
                    mark(v.tensor_scalar(kk_[:, m, :], xs[:, 2 + m, :], col("kk", m), None, ALU.mult), pr_dve, f"kk{m}")
                    on(pd(f"kk{m}"))
                    mark(v.tensor_tensor(sq1, kk_[:, m, :], kk_[:, m, :], ALU.mult), pr_dve, f"ksq{m}")
                    on((pr_pe, PR_PE.at(l, f"ss{m}")))
                    mark(v.tensor_scalar(rn, psf, 1e-24, None, ALU.max), pr_dve, f"kmax{m}")
                    on(pa(f"rn{m}"))
                    mark(v.tensor_tensor(kk_[:, m, :], kk_[:, m, :], rn, ALU.mult), pr_dve, f"kkn{m}")
                    mark(v.tensor_scalar(sq1, bv[:, m, :], col("ka", m), kac[:, m:m + 1], ALU.mult, ALU.add), pr_dve, f"kmul{m}")
                    on(pd(f"kmul{m}"))
                    mark(v.tensor_tensor(bv[:, m, :], bv[:, m, :], kk_[:, m, :], ALU.mult), pr_dve, f"bv{m}")
                    mark(v.tensor_tensor(xs[:, 2 + m, :], xs[:, 2 + m, :], sq1, ALU.mult), pr_dve, f"k2{m}")
                on(pd("k21"))
                v.sem_inc(passed, 1)

                with v.Fori(0, NTT) as c:
                    it = l * NTT + c
                    RW_DVE.start()
                    tk = bass.ds(c * P, P)
                    dv = lambda n: (rw_dve, RW_DVE.at(it, n))
                    ac = lambda n: (rw_act, RW_ACT.at(it, n))
                    pp = lambda n: (rw_pe, RW_PE.at(it, n))
                    mk = lambda ins, n: RW_DVE.mark(ins, rw_dve, n)
                    four = lambda b: ps[:, b, :].rearrange("p (h t) -> p h t", h=4)
                    pair = lambda b, a: ps[:, b:b + 2, :].rearrange("p b (h a t) -> p (b h) a t", h=2, a=2)[:, :, a, :]
                    bc = lambda mask: mask.unsqueeze(1).to_broadcast((P, 4, P))
                    for m in range(2):
                        mk(v.tensor_tensor_scan(cum[:, m, 1:P + 1], ones[:, :], sw[:, m, tk], 0.0, ALU.mult, ALU.add), f"cum{m}")
                    on(dv("cum1"))
                    mk(v.tensor_scalar(kpos, cum[:, :, 64], KAPPA, None, ALU.mult), "kp")
                    mk(v.tensor_scalar(kneg, cum[:, :, 64], -KAPPA, None, ALU.mult), "kn")
                    on(ac("fm"))
                    mk(v.scalar_tensor_tensor(ar[:, :, 0, :], kk_[:, :, tk], -1.0, pe_[:, :, 0:P], ALU.mult, ALU.mult), "A")
                    mk(v.tensor_tensor(ar[:, :, 1, :], xs[:, 0:2, tk], pe_[:, :, 1:P + 1], ALU.mult), "R")
                    mk(v.tensor_tensor(bt, bv[:, :, tk], pinv, ALU.mult), "B")
                    mk(v.tensor_tensor(kt_, xs[:, 2:4, tk], pinv, ALU.mult), "K")
                    mk(v.tensor_tensor(rk2, xs[:, 0:2, tk], xs[:, 2:4, tk], ALU.mult), "rk2")
                    for m in range(2):
                        mk(v.tensor_scalar(stm[:, m, :], st[:, m, :], fmid[:, m:m + 1], None, ALU.mult), f"sm{m}")
                    on(pp("L"))
                    lab = ps[:, 4:6, 0:256].rearrange("p b (h t) -> p b h t", h=2)
                    bc2 = lambda mask: mask.unsqueeze(1).unsqueeze(1).to_broadcast((P, 2, 2, P))
                    sl2 = lambda i: sl[i].rearrange("p (b h) t -> p b h t", b=2)
                    mk(v.tensor_tensor(sl2(4), lab, bc2(m_d), ALU.mult), "D")
                    mk(v.tensor_tensor(sl2(0), lab, bc2(m_n), ALU.mult), "N")
                    mk(v.tensor_tensor(sl[5], pair(0, 0), bc(m_dt), ALU.mult), "DT")
                    on(dv("DT"))
                    mk(v.tensor_tensor(sl[8], sl[5], bc(ident[:, :]), ALU.add), "Z1")
                    mk(v.tensor_tensor(sl[2], pair(0, 1), bc(m_ui), ALU.mult), "Lrb")
                    mk(v.tensor_tensor(sl[1], pair(2, 0), bc(m_u), ALU.mult), "Lak")
                    mk(v.tensor_tensor(sl[3], pair(2, 1), bc(m_ui), ALU.mult), "Lrk")
                    on(pp("Z2"), dv("Z1"))
                    mk(v.tensor_tensor(sl[8], four(4), sl[8], ALU.add), "Z2")
                    on(pp("D8"))
                    mk(v.tensor_copy(sl[6], four(0)), "D8")
                    on(pp("Z3"), dv("Z2"))
                    mk(v.tensor_tensor(sl[8], four(1), sl[8], ALU.add), "Z3")
                    on(pp("Z4"), dv("Z3"))
                    mk(v.tensor_tensor(sl[8], four(2), sl[8], ALU.add), "Z4")
                    on(pp("QT"))
                    mk(v.tensor_copy(sl[5], four(4)), "QT")
                    mk(v.tensor_tensor(sl[10], four(4), bc(ident[:, :]), ALU.add), "Y0")
                    on(pp("Q2T"))
                    mk(v.tensor_copy(sl[7], four(2)), "Q2T")
                    on(pp("Y1"), dv("Y0"))
                    mk(v.tensor_tensor(sl[10], four(4), sl[10], ALU.add), "Y1")
                    on(pp("Y2"), dv("Y1"))
                    mk(v.tensor_tensor(sl[10], four(0), sl[10], ALU.add), "Y2")
                    on(pp("X0"))
                    mk(v.tensor_copy(sl[4][:, 0:2, :].rearrange("p a (b d) -> p b a d", b=2), ps[:, 2:4, 0:P].rearrange("p b (a d) -> p b a d", a=2)), "X0")
                    on(pp("dS"))
                    mk(v.tensor_tensor(st, ps[:, 5, 0:P].rearrange("p (m k) -> p m k", m=2), stm, ALU.add), "s0")
                    on(dv("s0"))
                    for m in range(2):
                        mk(v.tensor_scalar(st[:, m, :], st[:, m, :], pe_[:, m, P:P + 1], None, ALU.mult), f"sf{m}")
                    y4 = lambda h: ps[:, 4 - h % 2, HD * (h // 2):HD * (h // 2) + HD]
                    yn = sl[6][:, 0:2, :].rearrange("p a b -> p (a b)")
                    st4 = stats.rearrange("p (h s) -> p h s", h=RH)
                    for h in range(RH):
                        mk(v.bn_stats(st4[:, h, :], y4(h)), f"bn{h}")
                    on(dv("bn3"))
                    v.sem_inc(passed, 1)
                    for h in range(RH):
                        mk(v.bn_aggr(mv[:, 2 * h:2 * h + 2], st4[:, h, :]), f"ag{h}")
                    on(ac("rstd"), dv("ag3"))
                    for h in range(RH):
                        mk(v.tensor_scalar(yn[:, HD * h:HD * h + HD], y4(h), mv[:, 2 * h:2 * h + 1], rstd[:, h:h + 1], ALU.subtract, ALU.mult), f"yn{h}")
                    on(dv("yn3"))
                    mk(v.tensor_tensor(yn, yn, rows[:, 0, :], ALU.mult), "yw")
                    on(dv("yw"))
                    mk(v.tensor_tensor(yn, yn, rows[:, 1, :], ALU.add), "yb")
                    on(dv("yb"))
                    for h in range(RH):
                        y = yn[:, HD * h:HD * h + HD]
                        mk(v.scalar_tensor_tensor(y, vbk[:, h // 2, HD * (h % 2):HD * (h % 2) + HD], cbon[:, h:h + 1], y, ALU.mult, ALU.add), f"bo{h}")
                    on(dv("bo3"))
                    mk(v.tensor_tensor(yn, ps[:, 7, 0:RW], yn, ALU.mult), "yg")
                on((rw_dve, RW_DVE.at(l * NTT + NTT - 1, "yg")), (rw_act, RW_ACT.at(l * NTT + NTT - 1, "ro")))

                RS_DVE.start()
                dv = lambda n: (rs_dve, RS_DVE.at(l, n))
                ac = lambda n: (rs_act, RS_ACT.at(l, n))
                pp = lambda n: (rs_pe, RS_PE.at(l, n))
                mk = lambda ins, n: RS_DVE.mark(ins, rs_dve, n)
                SR = slice(0, NS)
                tok = lambda t, m: t[:, m, T:XW].rearrange("p (b t) -> p b t", t=TS + 1)[:, :, 1:]
                tok2 = lambda t, m0: t[:, m0:m0 + 2, T:XW].rearrange("p m (b t) -> p m b t", t=TS + 1)[:, :, :, 1:]
                bt4 = lambda t: t.rearrange("p m (b t) -> p m b t", t=TS)
                mk(v.memset(cum5[:, :, :, 0], 0.0), "zero")
                mk(v.tensor_copy(cum5[:, :, :, 1:], tok2(sw, 0)), "cum0")
                for i in range(2, TS + 1):
                    on(dv(f"cum{i - 2}"))
                    mk(v.tensor_tensor(cum5[:, :, :, i], cum5[:, :, :, i], cum5[:, :, :, i - 1], ALU.add), f"cum{i - 1}")
                on(ac("pi5"))
                for m in range(2):
                    mk(v.scalar_tensor_tensor(ars[:, m, 0, :].rearrange("p (b t) -> p b t", t=TS), tok(kk_, m), -1.0, e5[:, m, :, 0:TS], ALU.mult, ALU.mult), f"A{m}")
                mk(v.tensor_tensor(bt4(ars[:, :, 1, :]), tok2(xs, 0), e5[:, :, :, 1:], ALU.mult), "R")
                mk(v.tensor_tensor(bt4(bts), tok2(bv, 0), pi5[:, :, :, 1:], ALU.mult), "B")
                mk(v.tensor_tensor(bt4(kts), tok2(xs, 2), pi5[:, :, :, 1:], ALU.mult), "K")
                mk(v.tensor_tensor(bt4(rk2s), tok2(xs, 0), tok2(xs, 2), ALU.mult), "rk2")
                mk(v.tensor_copy(bt4(vss), tok2(xs, 4)), "vs")
                mk(v.tensor_copy(sgs[64:P].rearrange("p (b t) -> p b t", t=TS), tok(xs, 6)[64:P]), "sg")
                on(dv("R"))
                for n, dst, i in (("aex", aex, 0), ("rex", rex, 1)):
                    mk(v.tensor_tensor(dst, ars[:, :, i, :].unsqueeze(2).to_broadcast((P, 2, DB, NS)), s_col.unsqueeze(1).to_broadcast((P, 2, DB, NS)), ALU.mult), n)
                on(pp("st"))
                mk(v.tensor_copy(sts.rearrange("p m b d -> p m (b d)"), ps[:, 0:2, :]), "sts")
                on(pp("L"))
                lab = ps[SR, 4:6, 0:2 * NS].rearrange("p b (h t) -> p b h t", h=2)
                spair = lambda b, i: ps[SR, b:b + 2, 0:4 * NS].rearrange("p b (h a t) -> p b h a t", h=2, a=2)[:, :, :, i, :]
                sm2 = lambda i: smat[i][SR].rearrange("p (b h) t -> p b h t", b=2)
                sbc = lambda t: t[SR].unsqueeze(1).unsqueeze(1).to_broadcast((NS, 2, 2, NS))
                mk(v.tensor_tensor(sm2(0), lab, sbc(s_l), ALU.mult), "D")
                mk(v.tensor_tensor(sm2(1), spair(0, 0), sbc(s_lt), ALU.mult), "DT")
                on(dv("DT"))
                mk(v.tensor_tensor(smat[3][SR], smat[1][SR], ident[SR, SR].unsqueeze(1).to_broadcast((NS, RH, NS)), ALU.add), "Z1")
                mk(v.tensor_tensor(sm2(4), spair(0, 1), sbc(s_ui), ALU.mult), "Lrb")
                mk(v.tensor_tensor(sm2(5), spair(2, 0), sbc(s_u), ALU.mult), "Lak")
                mk(v.tensor_tensor(sm2(6), spair(2, 1), sbc(s_ui), ALU.mult), "Lrk")
                on(pp("Z2"), dv("Z1"))
                mk(v.tensor_tensor(smat[3][SR], ps[SR, 1, 0:P].rearrange("p (h t) -> p h t", h=RH), smat[3][SR], ALU.add), "Z2")
                on(pp("X0"))
                mk(v.tensor_copy(x0s[SR].rearrange("p (a b d) -> p b a d", a=2, b=2), ps[SR, 2:4, 0:P].rearrange("p b (a d) -> p b a d", a=2)), "X0")
                on(ac("U"))
                rowm = s_row[SR].unsqueeze(2).to_broadcast((NS, DB, HD))
                for h in range(RH):
                    mk(v.tensor_tensor(uex[SR, h], us[SR, HD * h:HD * h + HD].unsqueeze(1).to_broadcast((NS, DB, HD)), rowm, ALU.mult), f"uex{h}")
                for h in range(RH):
                    mk(v.tensor_tensor(vex[SR, h], vbks[SR, h // 2, HD * (h % 2):HD * (h % 2) + HD].unsqueeze(1).to_broadcast((NS, DB, HD)), rowm, ALU.mult), f"vex{h}")
                on(pp("dS"))
                mk(v.tensor_tensor(sts.rearrange("p m b d -> p m (b d)"), ps[:, 0:2, :], sts.rearrange("p m b d -> p m (b d)"), ALU.add), "s0")
                on(dv("s0"))
                mk(v.tensor_tensor(sts, sts, e5[:, :, :, TS].unsqueeze(3).to_broadcast((P, 2, DB, HD)), ALU.mult), "sf")
                y4 = lambda h: ps[SR, 4 - h % 2, HD * (h // 2):HD * (h // 2) + HD]
                for h in range(RH):
                    mk(v.bn_stats(stats[SR, 6 * h:6 * h + 6], y4(h)), f"bn{h}")
                on(dv("bn3"))
                v.sem_inc(passed, 1)
                for h in range(RH):
                    mk(v.bn_aggr(mv[SR, 2 * h:2 * h + 2], stats[SR, 6 * h:6 * h + 6]), f"ag{h}")
                on(ac("rstd"), dv("ag3"))
                for h in range(RH):
                    mk(v.tensor_scalar(yns[SR, HD * h:HD * h + HD], y4(h), mv[SR, 2 * h:2 * h + 1], rstd[SR, h:h + 1], ALU.subtract, ALU.mult), f"yn{h}")
                on(dv("yn3"))
                mk(v.tensor_tensor(yns[SR], yns[SR], rows[SR, 0, :], ALU.mult), "yw")
                on(dv("yw"))
                mk(v.tensor_tensor(yns[SR], yns[SR], rows[SR, 1, :], ALU.add), "yb")
                on(dv("yb"))
                for h in range(RH):
                    y = yns[SR, HD * h:HD * h + HD]
                    mk(v.scalar_tensor_tensor(y, vbks[SR, h // 2, HD * (h % 2):HD * (h % 2) + HD], cbon[SR, h:h + 1], y, ALU.mult, ALU.add), f"bo{h}")
                on(dv("bo3"))
                mk(v.tensor_tensor(yns[SR], ps[SR, 7, 0:RW], yns[SR], ALU.mult), "yg")

                for j in (J_EQ, J_EQ + 2):
                    on((gemm_done, l * PJOBS + j + 1))
                    v.tensor_copy(eqk[:, j - J_EQ, :].rearrange("p (a b) -> p a b", a=3), job_psum(j)).then_inc(evac[0], 1)
                evac_tm(l, J_EV, evg, 0)
                RE_DVE.start()
                on((re_in, l * 80 + 80))
                mk = lambda ins, n: RE_DVE.mark(ins, re_dve, n)
                dv = lambda n: (re_dve, RE_DVE.at(l, n))
                pp = lambda n: (re_pe, RE_PE.at(l, n))
                mk(v.memset(rst, 0.0), "R")
                for i in range(4):
                    scale = 1.0 if i < 2 else HD ** -0.5
                    x = eqk[:, i, :]
                    on(pp(f"rot{i}"), evac_at(l, J_EQ + i))
                    mk(v.scalar_tensor_tensor(x, x, scale, cos_t, ALU.mult, ALU.mult), f"xc{i}")
                    if i:
                        on(dv(f"add{i - 1}"))
                    mk(v.scalar_tensor_tensor(ropet.rearrange("p (a b) -> p a b", a=3), ps[:, 3 * (i % 2):3 * (i % 2) + 3, 0:TB], scale,
                                              sin_t.rearrange("p (a b) -> p a b", a=3), ALU.mult, ALU.mult), f"ts{i}")
                    on(dv(f"ts{i}"))
                    mk(v.tensor_tensor(x, x, ropet, ALU.add), f"add{i}")

                def ret_norm(mk, dv, ac, R, gate):
                    y4 = lambda h: ps[R, 4 - h % 2, HD * (h // 2):HD * (h // 2) + HD]
                    for h in range(EH):
                        mk(v.bn_stats(stats[R, 6 * h:6 * h + 6], y4(h)), f"bn{h}")
                    on(dv("bn3"))
                    v.sem_inc(passed, 1)
                    for h in range(EH):
                        mk(v.bn_aggr(mv[R, 2 * h:2 * h + 2], stats[R, 6 * h:6 * h + 6]), f"ag{h}")
                    on(ac("rstd"), dv("ag3"))
                    for h in range(EH):
                        mk(v.tensor_scalar(yne[R, HD * h:HD * h + HD], y4(h), mv[R, 2 * h:2 * h + 1], rstd[R, h:h + 1], ALU.subtract, ALU.mult), f"yn{h}")
                    on(dv("yn3"))
                    mk(v.tensor_tensor(yne[R], yne[R], rows[R, 2, :], ALU.mult), "yw")
                    on(dv("yw"))
                    mk(v.tensor_tensor(yne[R], yne[R], gate, ALU.mult), "yg")

                on(evac_at(l, J_EV + 1), evac_at(l, J_EV + 3))
                v.sem_inc(passed, 1)
                with v.Fori(0, NTT) as c:
                    it = l * NTT + c
                    RT_DVE.start()
                    mkt = lambda ins, n: RT_DVE.mark(ins, rt_dve, n)
                    dvt = lambda n: (rt_dve, RT_DVE.at(it, n))
                    act_ = lambda n: (rt_act, RT_ACT.at(it, n))
                    ppt = lambda n: (rt_pe, RT_PE.at(it, n))
                    on(ppt("S"))
                    mkt(v.tensor_tensor(stt.rearrange("p (b a) t -> p b a t", b=2), ps[:, 0:2, 0:2 * P].rearrange("p b (a t) -> p b a t", a=2), dmask, ALU.mult), "st")
                    on(ppt("kt"))
                    mkt(v.tensor_tensor(kd, ps[:, 2, 0:EW].rearrange("p (h d) -> p h d", h=EH), inner.unsqueeze(2).to_broadcast((P, EH, HD)), ALU.mult), "kd")
                    on(ppt("dR"))
                    for m in range(2):
                        mkt(v.scalar_tensor_tensor(rst[:, m, :], rst[:, m, :], gam[:, m:m + 1], ps[:, 5, HD * m:HD * m + HD], ALU.mult, ALU.add), f"R{m}")
                    ret_norm(mkt, dvt, act_, slice(0, P), evg[:, bass.ds(c, 1), EW:2 * EW].rearrange("p a e -> p (a e)"))
                ac = lambda n: (re_act, RE_ACT.at(l, n))
                mk(v.tensor_tensor(qds, eqk[:, 0:2, T:NT], s_cross, ALU.mult), "qd")
                on(dv("qd"))
                mk(v.tensor_tensor(qex, qds.unsqueeze(2).to_broadcast((P, 2, DB, NS)), s_col.unsqueeze(1).to_broadcast((P, 2, DB, NS)), ALU.mult), "qex")
                on(pp("S"))
                mk(v.tensor_tensor(stts[SR].rearrange("p (b a) t -> p b a t", b=2), ps[SR, 0:2, 0:2 * NS].rearrange("p b (a t) -> p b a t", a=2), s_dmask[SR], ALU.mult), "st")
                on(pp("kt"))
                mk(v.tensor_tensor(kds[SR], ps[SR, 2, 0:EW].rearrange("p (h d) -> p h d", h=EH), s_inner[SR].unsqueeze(2).to_broadcast((NS, EH, HD)), ALU.mult), "kd")
                for h in range(EH):
                    mk(v.tensor_tensor(vexe[SR, h], evg[SR, NTT, HD * h:HD * h + HD].unsqueeze(1).to_broadcast((NS, DB, HD)),
                                       s_row[SR].unsqueeze(2).to_broadcast((NS, DB, HD)), ALU.mult), f"vex{h}")
                on(pp("dR"))
                for m in range(2):
                    rm = rss[:, m].rearrange("p b e -> p (b e)")
                    mk(v.scalar_tensor_tensor(rm, rm, s_gam[:, m:m + 1], ps[:, m, :], ALU.mult, ALU.add), f"R{m}")
                ret_norm(mk, dv, ac, SR, evg[SR, NTT, EW:2 * EW])
                on(dv("yg"), (re_out, l * 48 + 48), (re_act, RE_ACT.at(l, "ro")), (rs_out, l * 16 + 16), (ro_out, l * 16 + 16))
                for j in range(J_FQ, J_FV, 2):
                    on((gemm_done, l * PJOBS + j + 1))
                    v.tensor_copy(fqk[:, j - J_FQ, :].rearrange("p (a b) -> p a b", a=3), job_psum(j)).then_inc(evac[0], 1)
                for j in range(J_FV, J_OUT, 2):
                    evac_tm(l, j, fv, j - J_FV)
                FG_DVE.start()
                on((params_in, l * (16 * NPARAM) + 16 * NPARAM))
                FG_DVE.mark(v.tensor_scalar(gq8, col("qn"), HD ** -0.5, None, ALU.mult), fg_dve, "gq")
                on(evac_at(l, J_OUT - 1), evac_at(l, J_FV - 1), (fg_dve, FG_DVE.at(l, "gq")))
                v.sem_inc(passed, 1)
                with v.Fori(0, 4) as i:
                    it = l * 4 + i
                    FN_DVE.start()
                    for u in range(2):
                        x = fqk[:, bass.ds(i + 4 * u, 1), :].rearrange("p a t -> p (a t)")
                        FN_DVE.mark(v.tensor_tensor(fsq[:, u, :], x, x, ALU.mult), fn_dve, f"sq{u}")
                    for u in range(2):
                        x = fqk[:, bass.ds(i + 4 * u, 1), :].rearrange("p a t -> p (a t)")
                        v.wait_ge(fn_act, FN_ACT.at(it, f"rs{u}"))
                        FN_DVE.mark(v.scalar_tensor_tensor(x, x, gq8 if u == 0 else col("kn"), frs[:, u, :], ALU.mult, ALU.mult), fn_dve, f"n{u}")
                fr = slice(0, FH)
                fgm = lambda ins, n: FG_DVE.mark(ins, fg_dve, n)
                fgd = lambda n: (fg_dve, FG_DVE.at(l, n))
                fgm(v.tensor_scalar(fl[fr], fl[fr], col("fb", 0, fr), None, ALU.add), "z")
                on(fgd("z"))
                fgm(v.scalar_tensor_tensor(fz, fl[fr], -1.0, fl[fr], ALU.mult, ALU.max), "abs")
                on((fg_act, FG_ACT.at(l, "ln")))
                fgm(v.scalar_tensor_tensor(fl[fr], fl[fr], 0.0, fe, ALU.min, ALU.subtract), "logf")
                on(fgd("logf"), (fn_dve, FN_DVE.at(l * 4 + 3, "n1")))
                fgm(v.tensor_tensor_scan(ncr, ones[fr, 0:1].to_broadcast((FH, T)), fl[fr, 0:T], 0.0, ALU.mult, ALU.subtract), "nc")
                with v.Fori(0, 4) as p:
                    it = l * 4 + p
                    FP_DVE.start()
                    fm = lambda ins, n: FP_DVE.mark(ins, fp_dve, n)
                    fd = lambda n: (fp_dve, FP_DVE.at(it, n))
                    fa = lambda n: (fp_act, FP_ACT.at(it, n))
                    fpp = lambda n: (fp_pe, FP_PE.at(it, n))
                    on((fp_pool, FP_POOL.at(it, "ncd")))

                    def soft(s):
                        i, hh = s // 2, s % 2
                        S_ = ps[:, 2 * hh:2 * hh + 2, :].rearrange("p a b -> p (a b)")
                        on(fpp(f"S{s}"))
                        if s >= 2:
                            v.sem_inc(passed, 1)
                            fm(v.tensor_tensor_reduce(sp_[:, hh, 0:P * i], S_[:, 0:P * i], ncb[:, hh, 0:P * i], 1.0, -3.0e38, ALU.add, ALU.max, mx[:, s:s + 1]), f"m{s}")
                            on(fd(f"m{s}"))
                        v.sem_inc(passed, 1)
                        fm(v.tensor_tensor_reduce(sp_[:, hh, P * i:P * i + P], S_[:, P * i:P * i + P], ncd[:, NTT * hh + i, :], 1.0,
                                                  mx[:, s:s + 1] if s >= 2 else -3.0e38, ALU.add, ALU.max, mx[:, s:s + 1]), f"d{s}")
                        on(fd(f"d{s}"))
                        fm(v.tensor_scalar(nmx[:, s:s + 1], mx[:, s:s + 1], -1.0, None, ALU.mult), f"n{s}")

                    def out_(s):
                        i, hh = s // 2, s % 2
                        if s % 2:
                            on(fpp(f"T{s}"))
                            fm(v.tensor_copy(ptt[:, hh, 0:i + 1, :], ps[:, 4:6, :].rearrange("p a (b c) -> p (a b) c", c=P)[:, 0:i + 1, :]), f"pt{s}")
                        on(fa(f"e{s}"))
                        fm(v.reciprocal(rrec[:, s:s + 1], rsum[:, s:s + 1]), f"r{s}")
                        on(fd(f"r{s}"), fpp(f"V{s}"))
                        fm(v.tensor_scalar(otok[:, i, HD * hh:HD * hh + HD], ps[:, 6 + hh, 0:HD], rrec[:, s:s + 1], None, ALU.mult), f"o{s}")

                    for s in SC:
                        soft(s)
                        out_(s)
                fsm_ = lambda ins, n: FS_DVE.mark(ins, fs_dve, n)
                fsd = lambda n: (fs_dve, FS_DVE.at(l, n))
                FS_DVE.start()
                on((fp_act, FP_ACT.at(l * 4 + 3, "oT")))
                fsm_(v.memset(qb, 0.0), "qz")
                on(fsd("qz"))
                for p in range(4):
                    for k in range(2):
                        r = slice(HD * k, HD * k + HD)
                        c = 8 * p + 4 * k
                        fsm_(v.tensor_copy(qb[r, :, p, c:c + TS], fqk[r, p, T:NT].rearrange("p (b t) -> p b t", t=TS)), f"q{p}{k}")
                fsm_(v.tensor_copy(kn, fqk[:, 4:8, T:NT]), "kn")
                fsm_(v.tensor_copy(vn[SR], fv[SR, NTT, :]), "vn")
                R64 = slice(0, DB * FH)
                on((fs_pe, l + 1), (past_in, l * NPAST + NPAST))
                fsm_(v.tensor_copy(lfs[R64, 0:NP], ps[R64, 0:2, :].rearrange("p a b -> p (a b)")), "lfs")
                fsm_(v.tensor_copy(lfs[R64, NP:NP + TS], ncs[R64, NP:NP + TS]), "lfn")
                on(fsd("lfn"))
                fsm_(v.tensor_tensor_scan(ncs[R64], ones[R64, 0:1].to_broadcast((DB * FH, NP + TS)), lfs[R64], 0.0, ALU.mult, ALU.subtract), "ncs")
                on(fsd("ncs"), (fox_const, l * 64 + 64))
                v.sem_inc(passed, 1)
                with v.Fori(0, 2) as g:
                    it = l * 2 + g
                    G_DVE.start()
                    gm = lambda ins, n: G_DVE.mark(ins, fgr_dve, n)
                    gd = lambda n: (fgr_dve, G_DVE.at(it, n))
                    ga = lambda n: (fgr_act, G_ACT.at(it, n))
                    gp = lambda n: (fgr_pe, G_PE.at(it, n))
                    gm(v.tensor_copy(cur_q, qb[:, bass.ds(g * 4, 4), :, :]), "cq")
                    gm(v.tensor_copy(cur_k, kn[:, :, bass.ds(g * 16, 16)]), "ck")
                    gm(v.tensor_copy(cur_sel[R64], ssel[R64, bass.ds(g, 1), :].rearrange("p a b -> p (a b)")), "csel")
                    gm(v.tensor_copy(cur_req, sreq[:, bass.ds(g, 1), :].rearrange("p a b -> p (a b)")), "creq")
                    for b in range(4):
                        for p in (1, 3):
                            on(gp(f"T{b}{p}"))
                            if b or p == 3:
                                on(gp(f"S{b}1") if p == 3 else gp(f"S{b - 1}3"))
                            gm(v.tensor_copy(keyt[1], ps[:, 5:7, :].rearrange("p a b -> p (a b)")), f"kt{b}{p}")
                    on(gp("S33"))
                    past = ps[:, 0:2, :].rearrange("p a b -> p (a b)")
                    gm(v.tensor_tensor(smn, ps[:, 2, 0:TS], sfm, ALU.add), "sn")
                    gm(v.tensor_reduce(fsm[:, 0:1], past, AX.X, ALU.max), "mx")
                    on(gd("sn"))
                    gm(v.tensor_reduce(fsm[:, 1:2], smn, AX.X, ALU.max), "mn")
                    on(gd("mn"))
                    gm(v.tensor_tensor(fsm[:, 2:3], fsm[:, 0:1], fsm[:, 1:2], ALU.max), "max")
                    on(gd("max"))
                    gm(v.tensor_scalar(fsm[:, 3:4], fsm[:, 2:3], -1.0, None, ALU.mult), "neg")
                    on(ga("en"))
                    gm(v.tensor_tensor(fsm[:, 6:7], fsm[:, 4:5], fsm[:, 5:6], ALU.add), "sum")
                    on(gd("sum"))
                    gm(v.reciprocal(fsm[:, 7:8], fsm[:, 6:7]), "rec")
                    on(gd("rec"))
                    gm(v.tensor_scalar(pss, pss, fsm[:, 7:8], None, ALU.mult), "pn")
                    on(gd("pn"))
                    gm(v.tensor_tensor(pn, pss[:, NP:NP + TS].unsqueeze(1).to_broadcast((P, DB, TS)), cur_req.unsqueeze(2).to_broadcast((P, DB, TS)), ALU.mult), "pne")
                    on(gp("P1"))
                    gm(v.tensor_copy(pts[:, 4:8, :], ps[:, 4, :].rearrange("p (j r) -> p j r", j=4)), "pt1")
                    on(gp("Pn"))
                    gm(v.tensor_copy(pnt[SR], ps[SR, 5, 0:P]), "pnt")
                    on(gp("V3"))
                    o7 = ps[:, 7, 0:P].rearrange("p (m b k t) -> p m b k t", m=4, b=4, k=2)
                    for k in range(2):
                        r = slice(HD * k, HD * k + HD)
                        gm(v.tensor_copy(hT[r, 0:4, bass.ds(g * 16 + T, 16)].rearrange("p m (b t) -> p m b t", t=TS), o7[r, :, :, k, :]), f"o{k}")
                on((fgr_dve, G_DVE.at(l * 2 + 1, "o1")), (fox_out2, l * 16 + 16), (lft_out, l * 32 + 32))
                for j in range(J_OUT, J_FF):
                    on((gemm_done, l * PJOBS + j + 1))
                    xk = xT[:, j - J_OUT, :].rearrange("p (a b) -> p a b", a=3)
                    v.tensor_tensor(xk, job_psum(j), xk, ALU.add).then_inc(evac[j % 2], 1)
                on(evac_at(l, J_FF - 2), evac_at(l, J_FF - 1))
                norm(l, 1, "ln_ffn")
                with v.Fori(0, FT // 2) as q:
                    for u in range(2):
                        v.wait_ge(evac[0], l * HALF + q * 2 + ((J_FF + 2 * u) // 2 + 2))
                        v.wait_ge(gemm_done, l * PJOBS + q * RING + (J_FF + 2 * u + 2))
                        v.tensor_tensor(big[:, bass.ds((q * 2 + u) * NT, NT)].rearrange("p (a b) -> p a b", a=3), job_psum(1),
                                        sil[:, u * NT:(u + 1) * NT].rearrange("p (a b) -> p a b", a=3), ALU.mult).then_inc(evac[1], 1)
                for j in range(KT):
                    on((gemm_done, l * PJOBS + J_DOWN + j + 1))
                    xk = xT[:, j, :].rearrange("p (a b) -> p a b", a=3)
                    v.tensor_tensor(xk, job_psum(j), xk, ALU.add).then_inc(evac[j % 2], 1)
                v.wait_ge(evac[0], l * HALF + HALF + 1)
                v.wait_ge(evac[1], l * HALF + HALF + 1)
            v.tensor_copy(ytile, xT[:, :, 0:P]).then_inc(y_st, 1)
            with v.Fori(1, NTT) as t:
                v.wait_ge(y_pe, t)
                v.tensor_copy(ytile, xT[:, :, bass.ds(t * P, P)]).then_inc(y_st, 1)
            v.wait_ge(y_pe, NTT)
            v.tensor_copy(ytile[:, :, 0:NS], xT[:, :, T:NT]).then_inc(y_st, 1)

        @block.scalar
        def _(a):
            def on(*waits):
                for s, val in waits:
                    a.wait_ge(s, val)

            act = a.activation

            def evac_tm(l, j, dst, n, func=ACT.Copy):
                a.wait_ge(gemm_done, l * PJOBS + j + 1)
                act(dst[:, 0:NTT, P * n:P * n + P], job_psum_tm(j)[:, 0:NTT, :], func)
                act(dst[0:NS, NTT, P * n:P * n + P], job_psum_tm(j)[0:NS, NTT, :], func).then_inc(evac[j % 2], 1)

            def norm(l, which):
                it = 2 * l + which
                NRM_ACT.start()
                on((n_pe, NRM_PE.at(it, "sum7")))
                NRM_ACT.mark(act(nrs.rearrange("p (a b) -> p a b", a=3), ps[:, 0:3, 0:TB], ACT.Ln, scale=1.0 / D, bias=EPS), n_act, "ln")
                on((n_act, NRM_ACT.at(it, "ln")))
                NRM_ACT.mark(act(nrs, nrs, ACT.Exp, scale=-0.5), n_act, "rstd")

            with a.Fori(0, DEPTH) as l:
                norm(l, 0)
                for j in (1, 3, 5):
                    on((gemm_done, l * PJOBS + j + 1))
                    s = 3 * (j % 2)
                    a.copy(rp[:, j, 1:1 + 2 * TB].rearrange("p (a b) -> p a b", a=2), ps[:, s:s + 2, 0:TB])
                    a.copy(rp[:, j, 1 + 2 * TB:1 + T], ps[:, s + 2, 0:T - 2 * TB])
                    a.copy(rp[:, j, 1 + T:PW].rearrange("p (b t) -> p b t", t=TS + 1)[:, :, 1:],
                           ps[:, s + 2, T - 2 * TB:TB].rearrange("p (b t) -> p b t", t=TS)).then_inc(evac[j % 2], 1)
                on((gemm_done, l * PJOBS + 7 + 1))
                a.copy(fl.rearrange("p (a b) -> p a b", a=3), job_psum(7)).then_inc(evac[1], 1)
                pd = lambda n: (pr_dve, PR_DVE.at(l, n))
                pa = lambda n: (pr_act, PR_ACT.at(l, n))
                mark = PR_ACT.mark
                PR_ACT.start()
                on(pd("xs6"))
                mark(act(xs[0:32, 6, :], xs[0:32, 6, :], ACT.Tanh), pr_act, "tanh")
                mark(act(xs[64:P, 6, :], xs[64:P, 6, :], ACT.Sigmoid), pr_act, "sg")
                on((shift_out, l * (8 * 16) + 8 * 16))
                for m in range(2):
                    for s, (n, dst, b0) in enumerate((("w", sw, "w0"), ("a", bv, "a0"))):
                        on((pr_pe, PR_PE.at(l, f"{n}{m}")))
                        mark(act(dst[:, m, :], ps[:, 4 * s:4 * s + 3, :].rearrange("p a b -> p (a b)")[:, 0:XW], ACT.Sigmoid, bias=col(b0, m)),
                             pr_act, f"{'sw' if s == 0 else 'a'}{m}")
                for m in range(2):
                    on(pd(f"kmax{m}"))
                    mark(act(rn, rn, ACT.Ln, scale=2.0 ** 30), pr_act, f"ln{m}")
                    on(pa(f"ln{m}"))
                    mark(act(rn, rn, ACT.Exp, scale=-0.5, bias=15 * 0.6931471805599453), pr_act, f"rn{m}")
                with a.Fori(0, NTT) as c:
                    it = l * NTT + c
                    RW_ACT.start()
                    dv = lambda n: (rw_dve, RW_DVE.at(it, n))
                    ac = lambda n: (rw_act, RW_ACT.at(it, n))
                    pp = lambda n: (rw_pe, RW_PE.at(it, n))
                    mk = lambda ins, n: RW_ACT.mark(ins, rw_act, n)
                    four = lambda b: ps[:, b, :].rearrange("p (h t) -> p h t", h=4)
                    on(dv("kn"))
                    for m in range(2):
                        mk(act(pe_[:, m, :], cum[:, m, :], ACT.Exp, scale=-KAPPA, bias=kpos[:, m:m + 1]), f"e{m}")
                    for m in range(2):
                        mk(act(pinv[:, m, :], cum[:, m, 1:], ACT.Exp, scale=KAPPA, bias=kneg[:, m:m + 1]), f"pi{m}")
                    mk(act(fmid, kneg, ACT.Exp), "fm")
                    on(pp("tr"))
                    mk(a.copy(region((sil, 0), 6 * P), ps[:, 6:8, :].rearrange("p a b -> p (a b)")[:, 0:6 * P]), "vbk")
                    mk(a.copy(cbon, ps[:, 7, 256:260]), "bon")
                    for n, b, s in (("D2", 0, 6), ("D2T", 1, 7), ("D4", 2, 4), ("D4T", 3, 5), ("Q", 3, 4), ("M", 0, 9), ("Q2", 1, 6), ("Q4", 3, 4), ("TT", 1, 8)):
                        on(pp(n))
                        mk(a.copy(sl[s], four(b)), n)
                    on(pp("U"))
                    mk(a.copy(sl[5][:, 0:2, :].rearrange("p a b -> p (a b)"), ps[:, 6, 0:RW]), "U")
                    on(dv("ag3"))
                    mk(act(rstd, mv.rearrange("p (h s) -> p h s", s=2)[:, :, 1], ACT.Ln, bias=RWKV_EPS), "ln")
                    on(ac("ln"))
                    mk(act(rstd, rstd, ACT.Exp, scale=-0.5), "rstd")
                    on(pp("ro"))
                    mk(a.copy(mixB[:, 0:2, bass.ds(c * P, P)], ps[:, 6, 0:2 * P].rearrange("p (m t) -> p m t", m=2)), "ro")
                on((ro_pe, l + 1))
                a.copy(sl[9][0:HD, 0:2, :], ps[0:HD, 0, 0:2 * P].rearrange("p (m t) -> p m t", m=2)).then_inc(ro_act, 1)
                RS_ACT.start()
                dv = lambda n: (rs_dve, RS_DVE.at(l, n))
                ac = lambda n: (rs_act, RS_ACT.at(l, n))
                pp = lambda n: (rs_pe, RS_PE.at(l, n))
                mk = lambda ins, n: RS_ACT.mark(ins, rs_act, n)
                SR = slice(0, NS)
                on(dv("cum3"))
                mk(act(e5, cum5, ACT.Exp, scale=-KAPPA), "e5")
                mk(act(pi5, cum5, ACT.Exp, scale=KAPPA), "pi5")
                on(pp("tr"))
                mk(a.copy(region((sil, 0), 6 * P)[SR], ps[SR, 6:8, :].rearrange("p a b -> p (a b)")[:, 0:6 * P]), "vbk")
                mk(a.copy(cbon[SR], ps[SR, 7, 256:260]), "bon")
                on(pp("D2"))
                mk(a.copy(smat[2][SR], ps[SR, 0, 0:P].rearrange("p (h t) -> p h t", h=RH)), "D2")
                on(pp("U"))
                mk(a.copy(us[SR], ps[SR, 6, 0:RW]), "U")
                on(dv("ag3"))
                mk(act(rstd[SR], mv[SR].rearrange("p (h s) -> p h s", s=2)[:, :, 1], ACT.Ln, bias=RWKV_EPS), "ln")
                on(ac("ln"))
                mk(act(rstd[SR], rstd[SR], ACT.Exp, scale=-0.5), "rstd")
                on(pp("ro"))
                mk(a.copy(mixB[:, 0:2, T:NT], ps[:, 6, 0:2 * NS].rearrange("p (m t) -> p m t", m=2)), "ro")
                on(pp("nat"))
                mk(a.copy(nat_out[0:HD].rearrange("v b (m k) -> v m b k", m=2), ps[0:HD, 0:4, :].rearrange("v (m c) (b k) -> v m (c b) k", m=2, k=P)), "nat")

                for j in (J_EQ + 1, J_EQ + 3):
                    on((gemm_done, l * PJOBS + j + 1))
                    a.copy(eqk[:, j - J_EQ, :].rearrange("p (a b) -> p a b", a=3), job_psum(j)).then_inc(evac[1], 1)
                evac_tm(l, J_EV + 1, evg, 1)
                evac_tm(l, J_EV + 2, evg, 2, ACT.Silu)
                evac_tm(l, J_EV + 3, evg, 3, ACT.Silu)
                with a.Fori(0, NTT) as c:
                    it = l * NTT + c
                    RT_ACT.start()
                    a.wait_ge(rt_dve, RT_DVE.at(it, "ag3"))
                    RT_ACT.mark(act(rstd, mv.rearrange("p (h s) -> p h s", s=2)[:, :, 1], ACT.Ln, bias=RET_EPS), rt_act, "ln")
                    a.wait_ge(rt_act, RT_ACT.at(it, "ln"))
                    RT_ACT.mark(act(rstd, rstd, ACT.Exp, scale=-0.5), rt_act, "rstd")
                    a.wait_ge(rt_pe, RT_PE.at(it, "ro"))
                    RT_ACT.mark(a.copy(mixB[:, 2:4, bass.ds(c * P, P)], ps[:, 6, 0:2 * P].rearrange("p (m t) -> p m t", m=2)), rt_act, "ro")
                RE_ACT.start()
                a.wait_ge(re_dve, RE_DVE.at(l, "ag3"))
                RE_ACT.mark(act(rstd[SR], mv[SR].rearrange("p (h s) -> p h s", s=2)[:, :, 1], ACT.Ln, bias=RET_EPS), re_act, "ln")
                a.wait_ge(re_act, RE_ACT.at(l, "ln"))
                RE_ACT.mark(act(rstd[SR], rstd[SR], ACT.Exp, scale=-0.5), re_act, "rstd")
                a.wait_ge(re_pe, RE_PE.at(l, "ro"))
                RE_ACT.mark(a.copy(mixB[:, 2:4, T:NT], ps[:, 6, 0:2 * NS].rearrange("p (m t) -> p m t", m=2)), re_act, "ro")
                for j in range(J_FQ + 1, J_FV, 2):
                    on((gemm_done, l * PJOBS + j + 1))
                    a.copy(fqk[:, j - J_FQ, :].rearrange("p (a b) -> p a b", a=3), job_psum(j)).then_inc(evac[1], 1)
                for j in range(J_FV + 1, J_OUT, 2):
                    evac_tm(l, j, fv, j - J_FV)
                with a.Fori(0, 4) as i:
                    it = l * 4 + i
                    FN_ACT.start()
                    for u in range(2):
                        r3 = frs[:, u, :].rearrange("p (a b) -> p a b", a=3)
                        a.wait_ge(fn_pe, FN_PE.at(it, f"ss{u}"))
                        FN_ACT.mark(act(r3, ps[:, 3 * u:3 * u + 3, 0:TB], ACT.Ln, scale=1.0 / HD, bias=EPS), fn_act, f"ln{u}")
                        a.wait_ge(fn_act, FN_ACT.at(it, f"ln{u}"))
                        FN_ACT.mark(act(frs[:, u, :], frs[:, u, :], ACT.Exp, scale=-0.5), fn_act, f"rs{u}")
                FG_ACT.start()
                fga = lambda ins, n: FG_ACT.mark(ins, fg_act, n)
                a.wait_ge(fg_dve, FG_DVE.at(l, "abs"))
                fga(act(fe, fz, ACT.Exp, scale=-1.0), "exp")
                a.wait_ge(fg_act, FG_ACT.at(l, "exp"))
                fga(act(fe, fe, ACT.Ln, bias=1.0), "ln")
                a.wait_ge(fg_pe, FG_PE.at(l, "lft"))
                fga(a.copy(lft, ps[:, 7, 0:(NTT + 1) * FH]), "lft")
                with a.Fori(0, 4) as p:
                    it = l * 4 + p
                    FP_ACT.start()
                    fm = lambda ins, n: FP_ACT.mark(ins, fp_act, n)
                    fd = lambda n: (fp_dve, FP_DVE.at(it, n))
                    fpp = lambda n: (fp_pe, FP_PE.at(it, n))
                    on(fpp("ko"))
                    fm(a.copy(ko.rearrange("p i t -> p (i t)"), ps[:, 4:6, :].rearrange("p a b -> p (a b)")), "ko")
                    fm(a.copy(kos[SR], ps[SR, 6, 0:P]), "kos")
                    for s in SC:
                        i, hh = s // 2, s % 2
                        on(fd(f"n{s}"))
                        w = P * (i + 1)
                        fm(act(sp_[:, hh, 0:w], sp_[:, hh, 0:w], ACT.Exp, bias=nmx[:, s:s + 1], accum_out=rsum[:, s:s + 1]), f"e{s}")
                        if s % 2 == 0:
                            on(fpp(f"T{s}"))
                            fm(a.copy(ptt[:, hh, 0:i + 1, :], ps[:, 4:6, :].rearrange("p a (b c) -> p (a b) c", c=P)[:, 0:i + 1, :]), f"pt{s}")
                    on(fpp("oT"))
                    fm(a.copy(hT[:, bass.ds(p, 1), 0:T].rearrange("p a t -> p (a t)"), ps[:, 4:6, :].rearrange("p a b -> p (a b)")), "oT")
                with a.Fori(0, 2) as g:
                    it = l * 2 + g
                    G_ACT.start()
                    gm = lambda ins, n: G_ACT.mark(ins, fgr_act, n)
                    gd = lambda n: (fgr_dve, G_DVE.at(it, n))
                    gp = lambda n: (fgr_pe, G_PE.at(it, n))
                    for b in range(4):
                        for p in (0, 2):
                            on(gp(f"T{b}{p}"))
                            if b or p == 2:
                                on(gp(f"S{b}0") if p == 2 else gp(f"S{b - 1}2"))
                            gm(a.copy(keyt[0], ps[:, 3:5, :].rearrange("p a b -> p (a b)")), f"kt{b}{p}")
                    on(gd("neg"))
                    gm(act(pss[:, 0:NP], ps[:, 0:2, :].rearrange("p a b -> p (a b)"), ACT.Exp, bias=fsm[:, 3:4], accum_out=fsm[:, 4:5]), "e")
                    gm(act(pss[:, NP:NP + TS], smn, ACT.Exp, bias=fsm[:, 3:4], accum_out=fsm[:, 5:6]), "en")
                    on(gp("P0"))
                    gm(a.copy(pts[:, 0:4, :], ps[:, 3, :].rearrange("p (j r) -> p j r", j=4)), "pt0")
                norm(l, 1)
                with a.Fori(0, FT // 2) as q:
                    for u in range(2):
                        a.wait_ge(evac[1], l * HALF + q * 2 + ((J_FF + 2 * u + 1 - RING) // 2 + 2))
                        a.wait_ge(gemm_done, l * PJOBS + q * RING + (J_FF + 2 * u + 1))
                        act(sil[:, u * NT:(u + 1) * NT].rearrange("p (a b) -> p a b", a=3), job_psum(0), ACT.Silu).then_inc(evac[0], 1)
            def y_rows(t, u):
                a.wait_ge(y_pe, t * 2 + (u + 1))
                a.copy(yrows[:, u, :].rearrange("p (a b) -> p a b", a=2), ps[:, 4 * u:4 * u + 2, :]).then_inc(y_ev, 1)

            for u in range(2):
                y_rows(0, u)
            with a.Fori(1, NTT // 2) as t:
                for u in range(2):
                    a.wait_ge(y_out[u], t * 16)
                    y_rows(t, u)
            a.wait_ge(y_pe, NTT + 1)
            a.wait_ge(y_out[0], 16 * (NTT // 2))
            a.copy(yrows[0:NS, 0, :].rearrange("p (a b) -> p a b", a=2), ps[0:NS, 0:2, :]).then_inc(y_ev, 1)


_INS = ['x_prompt', 'x_sample', 'cache_fox_k', 'cache_fox_v', 'cache_fox_logf', 'state_rwkv', 'state_rwkv_shift',
        'state_ret', 'page_table', 'ln_mix_g', 'w_in', 'fox_qn_g', 'fox_kn_g', 'fox_f_b', 'rwkv_mu', 'rwkv_w0', 'rwkv_w2',
        'rwkv_a0', 'rwkv_a2', 'rwkv_g2', 'rwkv_k_k', 'rwkv_k_a', 'rwkv_r_k', 'rwkv_lnx_w', 'rwkv_lnx_b', 'ret_gn_w',
        'w_out', 'ln_ffn_g', 'w_gate', 'w_up', 'w_down']
_NP = T // PG
_OUTS = [("y_prompt", (1, T, D)), ("y_sample", (DB, TS, D)),
         ("fox_k_prompt", (DEPTH, _NP, PG, FH, HD)), ("fox_v_prompt", (DEPTH, _NP, PG, FH, HD)),
         ("fox_logf_prompt", (DEPTH, _NP, PG, FH)),
         ("rwkv_state_prompt", (DEPTH, 1, RH, HD, HD)), ("rwkv_shift_prompt", (DEPTH, 1, RPROJ)),
         ("ret_state_prompt", (DEPTH, 1, EH, HD, HD)),
         ("fox_k_sample", (DEPTH, DB, TS, FH, HD)), ("fox_v_sample", (DEPTH, DB, TS, FH, HD)),
         ("fox_logf_sample", (DEPTH, DB, TS, FH)),
         ("rwkv_state_sample", (DEPTH, DB, RH, HD, HD)), ("rwkv_shift_sample", (DEPTH, DB, RPROJ)),
         ("ret_state_sample", (DEPTH, DB, EH, HD, HD))]


def shape_constants(np):
    c = np.zeros((P, NCONST), np.float32)

    def put(name, a):
        o, w = CONSTS[name]
        a = np.asarray(a, np.float32).reshape(a.shape[0], -1)
        assert a.shape[1] == w, (name, a.shape, w)
        c[:a.shape[0], o:o + w] = a

    i = np.arange(P)
    t, s = i[:, None], i[None, :]
    put("ident", (t == s))
    put("blk", (t // HD == s // HD))
    half = HD // 2
    put("rot", np.where(s % HD < half, -1.0 * (t == s + half), 1.0 * (t == s - half)))
    put("m_d", (s < t) & (s // 16 == t // 16))
    put("m_n", s // 16 < t // 16)
    put("m_dt", (t < s) & (s // 16 == t // 16))
    put("m_u", t < s)
    put("m_ui", t <= s)
    put("fmask", np.where(s <= t, 0.0, -1e30))
    j = np.arange(NS)
    t4, s4 = j[:, None], j[None, :]
    same = t4 // TS == s4 // TS
    put("s_l", same & (s4 < t4))
    put("s_lt", same & (t4 < s4))
    put("s_u", same & (t4 < s4))
    put("s_ui", same & (t4 <= s4))
    put("s_row", (j[:, None] // TS == np.arange(DB)[None, :]))
    put("s_col", np.broadcast_to((np.arange(DB)[:, None] == j[None, :] // TS)[None], (P, DB, NS)))
    lg = np.log1p(-np.exp2(-5.0 - np.arange(EH, dtype=np.float32))).astype(np.float32)
    head = 2 * np.arange(2)[None, :, None] + i[:, None, None] // HD
    put("cross", np.exp(lg[head] * (i[None, None, :] + 1.0)))
    put("inner", np.exp(lg[None, :] * (P - 1.0 - i[:, None])))
    put("gam", np.exp(lg[head[:, :, 0]] * P))
    put("dmask", np.where(t[:, None] <= i[None, None, :], np.exp(lg[None, :, None] * np.maximum(i[None, None, :] - t[:, None], 0.0)), 0.0))
    put("s_dmask", np.where(same[:, None] & (t4[:, None] <= j[None, None, :]), np.exp(lg[None, :, None] * np.maximum(j[None, None, :] - t4[:, None], 0.0)), 0.0))
    put("s_cross", np.exp(lg[head] * (j[None, None, :] % TS + 1.0)))
    put("s_inner", np.exp(lg[None, :] * (TS - 1.0 - j[:, None] % TS)))
    put("s_gam", np.exp(lg[head[:, :, 0]] * TS))
    inv = (np.float32(10000.0) ** (-np.arange(half, dtype=np.float32) / np.float32(half))).astype(np.float32)
    pos = np.concatenate([np.arange(T), NPG * PG + np.arange(NS) % TS]).astype(np.float32)
    ang = (pos[None, :] * inv[i % half][:, None]).astype(np.float32)
    put("cos", np.cos(ang))
    put("sin", np.sin(ang))
    r = np.arange(P)
    g = np.arange(2)
    put("s_sel", ((np.arange(64)[:, None, None] // FH == 4 * g[None, :, None] + r[None, None, :] // 32)
         & (np.arange(64)[:, None, None] % FH == r[None, None, :] % 32 // TS)))
    put("s_req", np.arange(DB)[None, None, :] == 4 * g[None, :, None] + r[:, None, None] // 32)
    put("s_fmask", np.where(np.arange(TS)[None, :] <= r[:, None] % TS, 0.0, -1e30))
    return c


def kernel(**inputs):
    import numpy as np
    import concourse.bacc as bacc
    from concourse.bass_utils import run_bass_kernel_spmd

    nc = bacc.Bacc("TRN2", target_bir_lowering=False, num_devices=1)
    arrays, ins, outs = {}, {}, {}
    given = {name: np.ascontiguousarray(inputs[name]) for name in _INS}
    given["consts"] = shape_constants(np)
    for name, a in given.items():
        arrays[f"in_{name}"] = a
        ins[name] = nc.dram_tensor(f"in_{name}", a.shape, mybir.dt.from_np(a.dtype), kind="ExternalInput").ap()
    for name, shape in _OUTS:
        outs[name] = nc.dram_tensor(f"out_{name}", shape, F32, kind="ExternalOutput").ap()
    build(nc, ins, outs, nc.dram_tensor("decay_rows", (FH, T), F32, kind="Internal").ap())
    r = run_bass_kernel_spmd(nc, [arrays], core_ids=[0])
    return tuple(r.results[0][f"out_{name}"] for name, _ in _OUTS)
```

```python
from contextlib import ExitStack

import concourse.bass as bass
from concourse import mybir

F32 = mybir.dt.float32
ALU = mybir.AluOpType
ACT = mybir.ActivationFunctionType
AX = mybir.AxisListType

D = 1024
T = 1024
DEPTH = 2
DB, TS = 8, 4
NPG, PG = 8, 128
HD = 64
FH, RH, EH = 8, 4, 4
FW, RW, EW = FH * HD, RH * HD, EH * HD
RPROJ = 3 * RW + 128
FF = 2816
N_POOL = DB * NPG * 5 // 4
V_SP = 5
EPS = 1e-6
RWKV_EPS = 64e-5
RET_EPS = 1e-5
KAPPA = 0.6065306597126334

P = 128
NS = DB * TS
NT = T + NS
KT = D // P
TB = NT // 3
NTT = T // P
FT = FF // P

C_FQ, C_FK, C_FV, C_FL = 0, FW, 2 * FW, 3 * FW
C_R = 3 * FW + FH
C_EQ = C_R + RPROJ
C_EV = C_EQ + 2 * EW

J_R, J_EQ, J_EV, J_FQ, J_FV, J_OUT, J_FF = 0, 8, 12, 16, 24, 28, 36
JOBS = J_FF + 2 * FT
J_DOWN = JOBS
PJOBS = JOBS + KT
RING = 4

CONSTS = {}
_n = 0
for _name, _w in (("ident", P), ("blk", P), ("rot", P),
                  ("m_d", P), ("m_n", P), ("m_dt", P), ("m_u", P), ("m_ui", P), ("fmask", P),
                  ("s_l", NS), ("s_lt", NS), ("s_u", NS), ("s_ui", NS), ("s_row", DB), ("s_col", DB * NS),
                  ("s_dmask", EH * NS), ("s_cross", 2 * NS), ("s_inner", EH), ("s_gam", 2),
                  ("s_sel", 2 * P), ("s_req", 2 * DB), ("s_fmask", TS), ("s_tok", 4 * TS), ("s_head", FH),
                  ("cross", 2 * P), ("inner", EH), ("gam", 2),
                  ("dmask", EH * P), ("cos", NT), ("sin", NT)):
    CONSTS[_name] = (_n, _w)
    _n += _w
NCONST = _n

COLS = {}
_n = 0
for _name, _w in (("ln_mix", 8), ("ln_ffn", 8), ("mu", 7), ("w0", 2), ("a0", 2), ("kk", 2), ("ka", 2),
                  ("rk", 4), ("qn", 1), ("kn", 1), ("fb", 1)):
    COLS[_name] = (_n, _w)
    _n += _w
NCOLS = _n


class Steps:

    def __init__(self, *names, first=0):
        self.names = names
        self.first = first
        self.n = len(names)
        self.seen = 0

    def at(self, it, name):
        return it * self.n + (self.first + self.names.index(name) + 1)

    def start(self):
        self.seen = 0

    def mark(self, ins, sem, name):
        assert self.names[self.seen] == name, (self.names[self.seen], name)
        self.seen += 1
        ins.then_inc(sem, 1)


def names(pattern, *counts):
    out = [pattern]
    for c in counts:
        out = [o + str(i) for o in out for i in range(c)]
    return out


def build(nc, I, O, decay_rows):
    ctx = ExitStack()
    with ctx:
        def sb(name, shape):
            return ctx.enter_context(nc.sbuf_tensor(name, shape, F32))

        def sem(name):
            return ctx.enter_context(nc.semaphore(name))

        xT = sb("xT", [P, KT, NT])
        hT = sb("hT", [P, KT, NT])
        big = sb("big", [P, FT * NT])
        ring = sb("ring", [P, RING, KT, P])
        wd = sb("wd", [P, 2, FT, P])
        sil = sb("sil", [P, 2 * NT])
        ident = sb("ident", [P, P])
        blk = sb("blk", [P, P])
        ones = sb("ones", [P, P])
        share = sb("share", [P, P])
        cols_all = sb("cols_all", [P, DEPTH, NCOLS])
        cols = sb("cols", [P, NCOLS])
        ptab = ctx.enter_context(nc.sbuf_tensor("ptab", [1, DB * NPG], mybir.dt.int32))
        ps = ctx.enter_context(nc.psum_tensor("ps", [P, 8, 512], F32))

        wdf = wd[:, :, :, :].rearrange("p a b c -> p (a b c)")

        def region(base, *dims):
            n = 1
            for d in dims:
                n *= d
            a, off = base
            ap = a[:, off:off + n]
            if len(dims) == 2:
                ap = ap.rearrange("p (a b) -> p a b", a=dims[0])
            if len(dims) == 3:
                ap = ap.rearrange("p (a b c) -> p a b c", a=dims[0], b=dims[1])
            return ap

        def col(name, i=0, rows=slice(0, P)):
            return cols[rows, COLS[name][0] + i:COLS[name][0] + i + 1]

        mixB0 = FT * NT - 4 * NT
        mixB = region((big, mixB0), 4, NT)
        fl = region((big, mixB0 - NT), NT)
        PW = 1 + T + DB * (TS + 1)
        XW = PW - 1
        rp = region((big, 0), 7, PW)
        xs = region((big, 7 * PW), 7, XW)
        kk_ = region((big, 0), 2, XW)
        bv = region((big, 2 * XW), 2, XW)
        sw = region((big, 4 * XW), 2, XW)
        prB = 7 * PW + 7 * XW
        WM = 0
        m_d, m_n, m_dt, m_u, m_ui = (region((wdf, WM + P * i), P) for i in range(5))
        rows = region((wdf, 640), 3, RW)
        lora = region((wdf, 1408), RW)
        SM_ = 1664
        A0 = 2096
        rn = [region((wdf, A0), XW), region((big, prB), XW)]
        sq1 = [region((wdf, A0 + XW), XW), region((big, prB + XW), XW)]
        sl = [region((wdf, A0 + 512 * i), 4, P) for i in range(6)] + [region((big, prB + 512 * i), 4, P) for i in range(5)]
        cum = region((wdf, A0 + 3072), 2, P + 1)
        f0 = prB + 2560
        st = region((big, f0), 2, HD)
        stm = region((big, f0 + 128), 2, HD)
        small = region((big, f0 + 256), 96)
        kpos, kneg, fmid, cbon, stats, mv, rstd = (small[:, a:b] for a, b in
            ((0, 2), (2, 4), (4, 6), (8, 12), (12, 36), (36, 44), (44, 48)))
        kac = small[:, 48:50]
        dend = small[:, 50:52]
        vbk = region((sil, 0), 6, P)
        ar = region((sil, 768), 2, 2, P)
        bt = region((sil, 1280), 2, P)
        kt_ = region((sil, 1536), 2, P)
        pe_ = region((sil, 1792), 2, P + 1)
        c0 = 6 * XW
        pinv = region((big, c0), 2, P)
        rk2 = region((big, c0 + 256), 2, P)
        vs = region((big, c0 + 512), 2, P)
        sg = region((big, c0 + 768), P)
        s_l, s_lt, s_u, s_ui = (region((wdf, SM_ + NS * i), NS) for i in range(4))
        s_row = region((wdf, SM_ + 4 * NS), DB)
        s_col = region((wdf, SM_ + 4 * NS + DB), DB, NS)
        nat = region((wdf, A0), DB, RH * HD)
        smat = [region((wdf, A0 + 2048 + P * i), RH, NS) for i in range(8)]
        sts = region((big, prB), 2, DB, HD)
        aex = region((big, prB + 1024), 2, DB, NS)
        rex = region((big, prB + 2048), 2, DB, NS)
        x0s = region((big, c0), RW)
        us = region((big, c0 + 256), RW)
        uex = region((big, 0), RH, DB, HD)
        vex = region((big, 2048), RH, DB, HD)
        yns = region((big, 4096), RW)
        nat_out = region((big, 8832), DB, RH * HD)
        vbks = region((sil, 0), 6, P)
        ars = region((sil, 768), 2, 2, NS)
        bts = region((sil, 896), 2, NS)
        kts = region((sil, 960), 2, NS)
        rk2s = region((sil, 1024), 2, NS)
        vss = region((sil, 1088), 2, NS)
        sgs = region((sil, 1152), NS)
        cum5 = region((sil, 1184), 2, DB, TS + 1)
        e5 = region((sil, 1264), 2, DB, TS + 1)
        pi5 = region((sil, 1344), 2, DB, TS + 1)
        eqk = region((big, 0), 4, NT)
        evg = region((big, 4 * NT), NTT + 1, 2 * EW)
        RC = 8832 + DB * RH * HD
        rconst = region((big, RC), 2 * P + EH + 2 + EH * P + 2 * NT)
        cross = rconst[:, 0:2 * P].rearrange("p (m t) -> p m t", m=2)
        inner = rconst[:, 2 * P:2 * P + EH]
        gam = rconst[:, 2 * P + EH:2 * P + EH + 2]
        dmask = rconst[:, 262:262 + EH * P].rearrange("p (a b t) -> p b a t", a=2, b=2)
        cos_t = rconst[:, 774:774 + NT]
        sin_t = rconst[:, 774 + NT:774 + 2 * NT]
        RS0 = RC + 2886
        s_dmask = region((big, RS0), EH * NS).rearrange("p (a b t) -> p b a t", a=2, b=2)
        s_cross = region((big, RS0 + P), 2, NS)
        s_inner = region((big, RS0 + 192), EH)
        s_gam = region((big, RS0 + 196), 2)
        rot = region((big, RS0 + 198), P)
        W0 = RS0 + 198 + P
        ropet = region((big, W0), NT)
        qs = region((big, W0 + NT), 2, P)
        ks = region((big, W0 + NT + 256), 2, P)
        qd = region((big, W0 + NT + 512), 2, P)
        ve = region((big, W0 + NT + 768), EW)
        rst = region((big, W0 + NT + 1024), 2, HD)
        assert W0 + NT + 1024 + 128 <= prB + 1536
        yce = region((big, prB + 2048), 2, P)
        kd = region((sil, 0), EH, HD)
        stt = region((sil, 256), EH, P)
        yne = region((sil, 768), EW)
        qex = region((sil, 1024), 2, DB, NS)
        qds = region((sil, 1536), 2, NS)
        stts = region((sil, 1600), EH, NS)
        kds = region((sil, 1728), EH, HD)
        rss = region((wdf, A0), 2, DB, HD)
        vexe = region((wdf, A0 + 1024), EH, DB, HD)
        fqk = region((big, 0), 8, NT)
        fv = region((big, 8 * NT), NTT + 1, FW)
        FB = 8 * NT + (NTT + 1) * FW
        fsq = region((big, FB), 2, NT)
        frs = region((big, FB + 2 * NT), 2, NT)
        fz = region((sil, 0), NT)[0:FH]
        fe = region((sil, NT), NT)[0:FH]
        ncr = region((sil, 0), T)[0:FH]
        lft = region((big, FB + T), (NTT + 1) * FH)
        ringf = ring[:, :, :, :].rearrange("p a b c -> p (a b c)")
        qtp = [hT[:, 4, :], region((ringf, 0), NT)]
        ktp = [hT[:, 5, :], region((ringf, NT), NT)]
        ncb = [region((hT[:, 6:8, :].rearrange("p a b -> p (a b)"), 0), 2, T), region((sil, 0), 2, T)]
        sp_ = region((wdf, 0), 2, T)
        ptt = region((wdf, 2 * T), 2, NTT, P)
        vp = [region((wdf, 4 * T), NTT, P), region((ringf, 2 * NT), NTT, P)]
        otok = region((big, FB + T + 72), NTT, P)
        ko = region((big, FB + 2 * T + 72), NTT, P)
        kos = region((big, FB + 3 * T + 72), P)
        fmask = region((big, FB + 3 * T + 72 + P), P)
        fcol = region((big, FB + 4 * NT), 72)
        mx, nmx, rsum, rrec = (fcol[:, 16 * i:16 * i + 16] for i in range(4))
        gq8 = fcol[:, 64:65]
        NP = NPG * PG
        slot = [region((big, 4 * T * i), NPG, FW) for i in range(4)]
        qb = region((wdf, 0), DB, 4, NS)
        qn = region((ringf, 3136), 4, NS)
        kn = region((ringf, 3264), 4, NS)
        vn = region((ringf, 3392), FW)
        ssel = region((wdf, 1664), 2, P)
        sreq = region((wdf, 1920), 2, DB)
        sfm = region((wdf, 1936), TS)
        stok = region((wdf, 1940), 4 * TS)
        shead = region((wdf, 1956), FH)
        cur_q = region((wdf, 1964), 4, 4, NS)
        cur_k = region((wdf, 2476), 4, 16)
        cur_sel = region((wdf, 2540), P)
        cur_req = region((wdf, 2668), DB)
        lfp = region((big, FB + 4 * NT + 72), NPG, DB * FH)
        ncs = region((wdf, 3164), NP + TS)
        lfnew = region((wdf, 5120), TS)
        pss = region((wdf, 4192), NP + TS)
        fsm = region((wdf, 5220), 24)
        pn = region((wdf, 5244), DB, TS)
        pnt = region((wdf, 5276), P)
        keyt = [region((sil, NP * i), NP) for i in range(2)]
        pts = hT[:, 4, 0:NPG * PG].rearrange("p (j r) -> p j r", j=NPG)
        smn = hT[:, 5, 0:TS]
        om = pss[:, 0:FW]
        lfs = hT[:, 6, 0:NP + TS]
        h2 = region((big, 0), FT, NT)
        nsq = region((sil, 0), 2, NT)
        nrs = hT[0:96, 7, 0:TB]
        xstage = region((big, 0), 2, D)
        ytile = region((big, 2 * D), KT, P)
        yrows = region((big, 3 * D), 2, D)

        consts_in = sem("consts_in")
        x_in = [sem("x_in0"), sem("x_in1")]
        params_in, cols_in, cols_ready = sem("params_in"), sem("vectors_in"), sem("vectors_ready")
        loaded = [sem(f"loaded{i}") for i in range(RING)]
        down_loaded = [sem(f"down_loaded{i}") for i in range(2)]
        gemm_done = sem("gemm_done")
        evac = [sem("evac0"), sem("evac1")]
        xt_pe, xt_ev = sem("xt_pe"), sem("xt_ev")
        n_pe, n_dve, n_act = sem("norm_pe"), sem("norm_dve"), sem("norm_act")
        out_done = sem("out_done")
        zero_done = sem("zero_done")
        shift_in, shift_out = sem("shift_in"), sem("shift_out")
        pr_dve, pr_act, pr_pe = sem("prep_dve"), sem("prep_act"), sem("prep_pe")
        rw_dve, rw_act, rw_pe, rw_pool = sem("rwkv_dve"), sem("rwkv_act"), sem("rwkv_pe"), sem("rwkv_pool")
        rp_dve, rp_act, rp_pe, rv_act = sem("operands_dve"), sem("operands_act"), sem("operands_pe"), sem("operands_tok")
        rs_dve, rs_act, rs_pe, rs_in, rs_out = (sem(f"rsample_{x}") for x in ("dve", "act", "pe", "in", "out"))
        re_in, re_out, re_dve, re_act, re_pe = (sem(f"ret_{x}") for x in ("in", "out", "dve", "act", "pe"))
        rt_dve, rt_act, rt_pe, rt_pool = (sem(f"retchunk_{x}") for x in ("dve", "act", "pe", "pool"))
        rq_dve, rq_pe, ret_rows, ret_rows_out = sem("retscores_dve"), sem("retscores_pe"), sem("ret_rows"), sem("ret_rows_out")
        fn_dve, fn_act, fn_pe = (sem(f"foxnorm_{x}") for x in ("dve", "act", "pe"))
        fg_dve, fg_act, fg_pe = (sem(f"gate_{x}") for x in ("dve", "act", "pe"))
        fp_dve, fp_act, fp_pe, fp_pool = (sem(f"foxprompt_{x}") for x in ("dve", "act", "pe", "pool"))
        fp_ncb = [sem("decay_rows_in0"), sem("decay_rows_in1")]
        ko_free = sem("fox_k_stored")
        fs_dve, fs_pe = sem("foxsample_dve"), sem("foxsample_pe")
        fgr_dve, fgr_act, fgr_pe = (sem(f"foxgroup_{x}") for x in ("dve", "act", "pe"))
        fox_const, fox_out, fox_out2, ko_out = sem("fox_const"), sem("fox_v_out"), sem("fox_v_sample_out"), sem("fox_k_out")
        decay_out, past_in = sem("decay_rows_out"), sem("past_gates_in")
        page_in = [sem(f"pages_in{i}") for i in range(4)]
        vpage_in = [sem(f"last_v_pages_in{i}") for i in range(4)]
        table_in, lft_out = sem("table_in"), sem("log_gates_out")
        ro_pe, ro_act, ro_out = sem("rstate_pe"), sem("rstate_act"), sem("rstate_out")
        one_done = sem("one_done")
        passed = sem("passed")
        y_st, y_pe, y_ev, y_out = sem("y_st"), sem("y_pe"), sem("y_ev"), [sem("y_out0"), sem("y_out1")]

        HALF = PJOBS // 2
        NPAST = (NPG + 1) * DB * 16
        NPARAM = 8
        NCOLS_IN = DEPTH * 16

        def evac_at(l, j):
            return evac[j % 2], l * HALF + j // 2 + 2

        def job_psum(j):
            s = 3 * (j % 2)
            return ps[:, s:s + 3, 0:TB]

        def job_psum_tm(j):
            s = 3 * (j % 2)
            return ps[:, s:s + 3, :].rearrange("p a (b c) -> p (a b) c", c=P)

        NRM_DVE = Steps(*names("sq", KT), *names("h", KT))
        NRM_PE = Steps(*names("sum", KT), "rows")
        NRM_ACT = Steps("ln", "rstd")
        PR_DVE = Steps("zero", "cum0", "st0", "kac", *names("diff", 7), *names("xs", 7),
                       *[f"{a}{m}" for step in (("kk", "ksq"), ("kmax", "kmul", "k2"), ("kkn", "bv")) for m in range(2) for a in step])
        PR_ACT = Steps("tanh", "sg", *[f"{a}{m}" for m in range(2) for a in ("sw", "a")],
                       "ln0", "rn0", "ln1", "rn1")
        PR_PE = Steps(*[f"{a}{m}" for m in range(2) for a in ("w", "a")], "ss0", "ss1")
        RW_POOL = Steps("vs", "sg")
        RP_DVE = Steps("cum0", "cum1", "kp", "kn", "B", "K", "rk2", "A", "R", "dend", "sm0", "sm1")
        RP_ACT = Steps("e0", "e1", "pi0", "pi1", "fm")
        RP_PE = Steps("Lab", "L", "Lk", "tr")
        chunk = lambda c: c % NTT
        RW_DVE = Steps("DT", "Lrb", "D", "Z1", "N", "Lak", "Lrk", "Z2", "D8", "Z3", "Z4", "QT", "Y0",
                       "Q2T", "Y1", "Y2", "X0a", "X0b", "s0", "sf0", "sf1",
                       *names("bn", 4), *names("ag", 4), *names("yn", 4), "yw", "yb", *names("bo", 4), "yg")
        RW_ACT = Steps("D2", "D2T", "D4", "D4T",
                       "Q", "M", "Q2", "Q4", "TT", "g", "U", "Y", "ln", "rstd", "ro", first=1)
        RV_ACT = Steps("vbk", "bon")
        RW_PE = Steps("D2", "D2T", "D4", "D4T", "Z2", "D8", "Z3", "g", "Z4", "Q", "QT", "M",
                      "Q2", "Q2T", "Q4", "Y1", "Y2", "X0", "TT", "U", "Y", "dS", "ro")

        RS_DVE = Steps("zero", "cum0", "cum1", "cum2", "cum3", "A0", "A1", "R", "B", "K", "rk2", "vs", "sg", "aex", "rex", "sts",
                       "D", "DT", "Z1", "Lrb", "Lak", "Lrk", "Z2", "X0", *names("uex", 4), *names("vex", 4), "s0", "sf",
                       *names("bn", 4), *names("ag", 4), *names("yn", 4), "yw", "yb", *names("bo", 4), "yg")
        RS_ACT = Steps("e5", "pi5", "vbk", "bon", "D2", "U", "ln", "rstd", "ro", "nat")
        RS_PE = Steps("st", "L", "tr", "D2", "Z2", "g", "X0", "U", "Y", "dS", "ro", "nat")

        NORM4 = (*names("bn", 4), *names("ag", 4), *names("yn", 4), "yw", "yg")
        RE_DVE = Steps("R", *[f"{a}{i}" for i in range(4) for a in ("xc", "ts", "add")],
                       "qd", "qex", "st", "kd", *names("vex", 4), "R0", "R1", *NORM4)
        RE_PE = Steps(*names("rot", 4), "S", "kt", "O", "dR", "ro")
        RE_ACT = Steps("ln", "rstd", "ro")
        RT_POOL = Steps("q", "k", "qd", "v")
        RQ_PE = Steps("S", "kt")
        RQ_DVE = Steps("st", "kd")
        RT_DVE = Steps("R0", "R1", *NORM4, first=3)
        RT_PE = Steps("O", "dR")
        RT_ACT = Steps("Y", "ln", "rstd")

        FN_DVE = Steps("sq0", "sq1", "n0", "n1")
        FN_ACT = Steps("ln0", "rs0", "ln1", "rs1")
        FN_PE = Steps("ss0", "ss1")
        FG_DVE = Steps("z", "abs", "logf", "nc", "gq", "q0", "k0", "q", "kn", "vn")
        FG_ACT = Steps("exp", "ln", "lft")
        FG_PE = Steps("lft")
        SC = range(2 * NTT)
        FP_POOL = Steps("v", "q", "k")
        ahead = lambda s: s + 1 < 2 * NTT
        soft_ = lambda u, s: [f"{u}d{s}", f"{u}n{s}"]
        FP_DVE = Steps(*[x for u in range(2) for x in soft_(u, 0) + [y for s in SC for y in (soft_(u, s + 1) if ahead(s) else [])
                       + ([f"{u}pt{s}"] if s % 2 else []) + [f"{u}r{s}", f"{u}o{s}"]]])
        FP_ACT = Steps(*[x for u in range(2) for x in [f"{u}ko", f"{u}kos", f"{u}e0"] + [y for s in SC for y in ([f"{u}e{s + 1}"] if ahead(s) else [])
                       + ([f"{u}pt{s}"] if s % 2 == 0 else [])] + [f"{u}oT"]], first=1)
        FP_PE = Steps(*[x for u in range(2) for x in [f"{u}ko", f"{u}S0", f"{u}S1"] + [y for s in SC for y in [f"{u}T{s}"]
                      + ([f"{u}S{s + 2}"] if s + 2 < 2 * NTT else []) + [f"{u}V{s}"]] + [f"{u}oT"]])
        FS_DVE = Steps("qz", *[f"q{p}{k}" for p in range(4) for k in range(2)], "lfs", "lfn", "ncs")
        G_DVE = Steps("cq", "ck", "csel", "creq", *[f"kt{b}{p}" for b in range(4) for p in (1, 3)],
                      "sn", "mx", "mn", "max", "neg", "sum", "rec", "pn", "pne", "pt1", "pnt", "om", "o")
        G_ACT = Steps(*[f"kt{b}{p}" for b in range(4) for p in (0, 2)], "e", "en", "pt0")
        G_PE = Steps("bias", *[x for b in range(4) for x in [f"T{b}0"] + [y for p in range(4) for y in ([f"T{b}{p + 1}"] if p < 3 else []) + [f"S{b}{p}"]]],
                     "P0", "P1", "Pn", "V0", "V1", "V2", "V3", "F", first=5)

        block = ctx.enter_context(nc.Block())
        w_in = I["w_in"]

        @block.sync
        def _(sp):
            def w_block(l, w, c, kt=KT):
                return w[bass.ds(l, 1), :, bass.ds(c, P)].rearrange("a (k p) c -> p (a k) c", p=P)

            def load(l, j, src):
                sp.dma_start(ring[:, j % RING, :, :], src).then_inc(loaded[j % RING], 16)

            def free(l, j):
                sp.wait_ge(gemm_done, l * PJOBS + j - RING + 1)
                sp.sem_inc(passed, 1)

            RFC = [C_R + P * m for m in range(7)] + [C_FL]
            for j in range(RING):
                load(0, j, w_block(0, w_in, RFC[j]))
            vecs = (("ln_mix", "ln_mix_g", 8), ("ln_ffn", "ln_ffn_g", 8), ("mu", "rwkv_mu", 7), ("w0", "rwkv_w0", 2),
                    ("a0", "rwkv_a0", 2), ("kk", "rwkv_k_k", 2), ("ka", "rwkv_k_a", 2))
            sp.wait_ge(one_done, 3)
            with nc.allow_non_contiguous_dma("short parameter vectors"):
                for i in range(DEPTH):
                    for name, src, n in vecs:
                        c = COLS[name][0]
                        sp.dma_start(cols_all[:, i, c:c + n], I[src][i, :].rearrange("(m p) -> p m", p=P)).then_inc(cols_in, 16)
                    for h in range(RH):
                        r = slice(HD * (h % 2), HD * (h % 2) + HD)
                        sp.dma_start(cols_all[r, i, COLS["rk"][0] + h:COLS["rk"][0] + h + 1], I["rwkv_r_k"][i, h, :].unsqueeze(1)).then_inc(cols_in, 16)
                    for name, src in (("qn", "fox_qn_g"), ("kn", "fox_kn_g")):
                        for k in range(2):
                            sp.dma_start(cols_all[HD * k:HD * k + HD, i, COLS[name][0]:COLS[name][0] + 1], I[src][i, :].unsqueeze(1)).then_inc(cols_in, 16)
                    sp.dma_start(cols_all[0:FH, i, COLS["fb"][0]:COLS["fb"][0] + 1], I["fox_f_b"][i, :].unsqueeze(1)).then_inc(cols_in, 16)
            with sp.Fori(0, DEPTH) as l:
                for j in range(RING, 8):
                    free(l, j)
                    load(l, j, w_block(l, w_in, RFC[j]))
                for j0, c0_, n in ((J_EQ, C_EQ, 4), (J_EV, C_EV, 4), (J_FQ, C_FQ, 8), (J_FV, C_FV, 4)):
                    for j in range(j0, j0 + n):
                        free(l, j)
                        load(l, j, w_block(l, w_in, c0_ + P * (j - j0)))
                sp.wait_ge(table_in, 16)
                sp.wait_ge(fg_dve, FG_DVE.at(l, "vn"))
                sp.wait_ge(fp_pool, FP_POOL.at(l * 4 + 3, "k"))
                sp.wait_ge(fox_out, l * 16 + 16)
                sp.wait_ge(fox_out2, l * 16 + 16)
                sp.sem_inc(passed, 1)
                with sp.Fori(0, 2) as g:
                    it = l * 2 + g
                    for b in range(4):
                        if b == 3:
                            sp.wait_ge(fp_act, FP_ACT.at(l * 2 + 1, "1oT"))
                            sp.wait_ge(lft_out, l * 32 + 32)
                            sp.wait_ge(ko_out, l * 128 + 128)
                            sp.sem_inc(passed, 1)
                        sp.wait_ge(fgr_pe, G_PE.at(it - 1, f"V{b}"))
                        sp.sem_inc(passed, 1)
                        for j in range(NPG):
                            page = sp.value_load(ptab[0:1, bass.ds(g * (4 * NPG) + (b * NPG + j), 1)], min_val=0, max_val=N_POOL - 1)
                            sp.dma_start(slot[b][:, j, :], I["cache_fox_k"][bass.ds(l, 1), bass.ds(page, 1)].rearrange("a n p h d -> p (a n h d)")).then_inc(page_in[b], 16)
                    for b in range(4):
                        sp.wait_ge(fgr_pe, G_PE.at(it, f"T{b}3"))
                        sp.sem_inc(passed, 1)
                        for j in range(V_SP):
                            page = sp.value_load(ptab[0:1, bass.ds(g * (4 * NPG) + (b * NPG + j), 1)], min_val=0, max_val=N_POOL - 1)
                            sp.dma_start(slot[b][:, j, :], I["cache_fox_v"][bass.ds(l, 1), bass.ds(page, 1)].rearrange("a n p h d -> p (a n h d)")).then_inc(page_in[b], 16)
                    sp.sem_inc(passed, 1)
                sp.wait_ge(fgr_pe, G_PE.at(l * 2 + 1, "F"))
                for j in range(J_OUT, J_OUT + RING):
                    sp.sem_inc(passed, 1)
                    free(l, j)
                    load(l, j, w_block(l, I["w_out"], P * (j - J_OUT)))
                for j in range(J_OUT + RING, J_FF):
                    free(l, j)
                    load(l, j, w_block(l, I["w_out"], P * (j - J_OUT)))
                with sp.Fori(0, FT // 2) as q:
                    for u in range(RING):
                        sp.wait_ge(gemm_done, l * PJOBS + q * RING + (J_FF + u - RING + 1))
                        load(l, u, w_block(l, I["w_gate" if u % 2 == 0 else "w_up"], q * (2 * P) + P * (u // 2)))
                for j in range(2):
                    if j == 0:
                        sp.wait_ge(gemm_done, l * PJOBS + J_OUT + 1)
                    sp.dma_start(wd[:, j, :, :], w_block(l, I["w_down"], P * j)).then_inc(down_loaded[j], 16)
                for j in range(2, KT):
                    sp.wait_ge(gemm_done, l * PJOBS + J_DOWN + j - 2 + 1)
                    sp.dma_start(wd[:, j % 2, :, :], w_block(l, I["w_down"], P * j)).then_inc(down_loaded[j % 2], 16)
                for j in range(RING):
                    sp.wait_ge(gemm_done, l * PJOBS + JOBS - RING + j + 1)
                    sp.sem_inc(passed, 1)
                    load(0, j, w_block(DEPTH - 1 - l, w_in, RFC[j]))
            for s in range(RING):
                sp.wait_ge(loaded[s], 16 * (DEPTH * JOBS // RING + 1))

        @block.gpsimd
        def _(pool):
            cst = I["consts"]

            def const(dst, name, width=None):
                c, w = CONSTS[name]
                pool.dma_start(dst, cst[:, c:c + (width or w)]).then_inc(consts_in, 16)

            const(ident[:, :], "ident")
            const(blk[:, :], "blk")
            pool.dma_start(ptab[:, :], I["page_table"].rearrange("b j -> (b j)").unsqueeze(0)).then_inc(table_in, 16)
            for u in range(2):
                pool.dma_start(xstage[:, u, :], I["x_prompt"][0, P * u:P * u + P, :]).then_inc(x_in[u], 16)
            with pool.Fori(1, NTT // 2) as t:
                for u in range(2):
                    pool.wait_ge(xt_pe, t * 2 + u - 1)
                    pool.dma_start(xstage[:, u, :], I["x_prompt"][0, bass.ds((t * 2 + u) * P, P), :]).then_inc(x_in[u], 16)
            pool.wait_ge(xt_pe, NTT - 1)
            pool.dma_start(xstage[0:NS, 0, :], I["x_sample"].rearrange("b t d -> (b t) d")).then_inc(x_in[0], 16)
            with pool.Fori(0, DEPTH) as l:
                pool.wait_ge(evac[0], l * HALF + 1)
                pool.wait_ge(evac[1], l * HALF + 1)
                for r0, src, n in ((0, "rwkv_w2", 32), (32, "rwkv_a2", 32), (64, "rwkv_g2", 64)):
                    pool.dma_start(lora[r0:r0 + n, :], I[src][bass.ds(l, 1), :, :].rearrange("a k c -> k (a c)")).then_inc(params_in, 16)
                for k, src in enumerate(("rwkv_lnx_w", "rwkv_lnx_b", "ret_gn_w")):
                    pool.dma_start(rows[:, k, :], I[src][bass.ds(l, 1), :].to_broadcast((P, RW))).then_inc(params_in, 16)
                pool.dma_start(region((wdf, WM), 5 * P), cst[:, CONSTS["m_d"][0]:CONSTS["m_d"][0] + 5 * P]).then_inc(params_in, 16)
                pool.dma_start(region((wdf, SM_), 392), cst[:, CONSTS["s_l"][0]:CONSTS["s_l"][0] + 392]).then_inc(params_in, 16)
                pool.wait_ge(pr_dve, PR_DVE.at(l, "zero"))
                with nc.allow_non_contiguous_dma("feature-major rows"):
                    for m in range(7):
                        pool.dma_start(rp[:, m, 1 + T:PW].rearrange("p (b t) -> p b t", t=TS + 1)[:, :, 0],
                                       I["state_rwkv_shift"][bass.ds(l, 1), :, P * m:P * m + P].rearrange("a b p -> p (a b)")).then_inc(shift_in, 16)
                    pool.wait_ge(*evac_at(l, 6))
                    pool.wait_ge(*evac_at(l, 5))
                    pool.sem_inc(passed, 1)
                    pool.dma_start(O["rwkv_shift_prompt"][bass.ds(l, 1), 0, :].rearrange("a (m p) -> p (a m)", p=P), rp[:, :, T]).then_inc(shift_out, 16)
                    for m in range(7):
                        pool.dma_start(O["rwkv_shift_sample"][bass.ds(l, 1), :, P * m:P * m + P].rearrange("a b p -> p (a b)"),
                                       rp[:, m, 1 + T:PW].rearrange("p (b t) -> p b t", t=TS + 1)[:, :, TS]).then_inc(shift_out, 16)
                pool.wait_ge(pr_dve, PR_DVE.at(l, "xs6"))
                pool.wait_ge(pr_act, PR_ACT.at(l, "sg"))
                pool.sem_inc(passed, 1)
                with pool.Fori(0, NTT + 1) as c:
                    it = l * (NTT + 1) + c
                    RW_POOL.start()
                    pool.wait_ge(rp_dve, RP_DVE.at(it, "rk2"))
                    RW_POOL.mark(pool.tensor_copy(vs, xs[:, 4:6, bass.ds(chunk(c) * P, P)]), rw_pool, "vs")
                    pool.wait_ge(rw_pool, RW_POOL.at(it, "vs"))
                    RW_POOL.mark(pool.tensor_copy(sg[64:P], xs[64:P, 6, bass.ds(chunk(c) * P, P)]), rw_pool, "sg")
                pool.wait_ge(rw_pool, RW_POOL.at(l * (NTT + 1) + NTT, "sg"))
                pool.wait_ge(rw_act, RW_ACT.at(l * NTT + NTT - 1, "ro"))
                pool.dma_start(nat[0:HD].rearrange("v b (h k) -> v (b h) k", h=RH),
                               I["state_rwkv"][bass.ds(l, 1)].rearrange("a b h v k -> v (a b h) k")).then_inc(rs_in, 16)
                pool.wait_ge(ro_act, l + 1)
                pool.sem_inc(passed, 1)
                pool.dma_start(O["rwkv_state_prompt"][bass.ds(l, 1), 0].rearrange("a h v k -> v (a h) k"),
                               sl[9][0:HD, 0:2, :].rearrange("v m (h k) -> v (m h) k", h=2)).then_inc(ro_out, 16)
                pool.wait_ge(rs_act, RS_ACT.at(l, "nat"))
                pool.sem_inc(passed, 1)
                pool.dma_start(O["rwkv_state_sample"][bass.ds(l, 1)].rearrange("a b h v k -> v (a b h) k"),
                               nat_out[0:HD].rearrange("v b (h k) -> v (b h) k", h=RH)).then_inc(rs_out, 16)
                pool.wait_ge(rs_dve, RS_DVE.at(l, "vex3"))
                pool.sem_inc(passed, 1)
                for dst, name, w in ((rconst, "cross", 2886), (region((big, RS0), 198), "s_dmask", 198), (rot, "rot", P)):
                    pool.dma_start(dst, cst[:, CONSTS[name][0]:CONSTS[name][0] + w]).then_inc(re_in, 16)
                for m in range(2):
                    pool.dma_start(rss[:, m, :, :], I["state_ret"][bass.ds(l, 1), :, 2 * m:2 * m + 2].rearrange("a b h d e -> (h d) (a b) e")).then_inc(re_in, 16)
                pool.wait_ge(re_dve, RE_DVE.at(l, "add3"))
                pool.sem_inc(passed, 1)

                def queries_keys(c):
                    RT_POOL.start()
                    tk = bass.ds(c * P, P)
                    RT_POOL.mark(pool.tensor_copy(qs, eqk[:, 0:2, tk]), rt_pool, "q")
                    RT_POOL.mark(pool.tensor_copy(ks, eqk[:, 2:4, tk]), rt_pool, "k")

                def decayed_values(c):
                    RT_POOL.mark(pool.tensor_tensor(qd, eqk[:, 0:2, bass.ds(c * P, P)], cross, ALU.mult), rt_pool, "qd")
                    RT_POOL.mark(pool.tensor_copy(ve, evg[:, bass.ds(c, 1), 0:EW].rearrange("p a e -> p (a e)")), rt_pool, "v")

                queries_keys(0)
                decayed_values(0)
                with pool.Fori(0, NTT) as c:
                    pool.wait_ge(rq_pe, RQ_PE.at(l * (NTT + 1) + c, "kt"))
                    queries_keys(chunk(c + 1))
                    pool.wait_ge(rt_pe, RT_PE.at(l * NTT + c, "dR"))
                    pool.sem_inc(passed, 1)
                    decayed_values(chunk(c + 1))
                pool.wait_ge(rt_dve, RT_DVE.at(l * NTT + NTT - 1, "R1"))
                pool.sem_inc(passed, 1)
                pool.dma_start(O["ret_state_prompt"][bass.ds(l, 1), 0].rearrange("a (m h) d e -> (h d) (a m) e", m=2), rst).then_inc(re_out, 16)
                pool.wait_ge(re_dve, RE_DVE.at(l, "R1"))
                pool.sem_inc(passed, 1)
                for m in range(2):
                    pool.dma_start(O["ret_state_sample"][bass.ds(l, 1), :, 2 * m:2 * m + 2].rearrange("a b h d e -> (h d) (a b) e"), rss[:, m, :, :]).then_inc(re_out, 16)
                pool.wait_ge(re_dve, RE_DVE.at(l, "yg"))
                pool.wait_ge(re_act, RE_ACT.at(l, "ro"))
                pool.sem_inc(passed, 1)
                pool.wait_ge(table_in, 16)
                with pool.Fori(0, DB) as b:
                    for j in range(NPG):
                        page = pool.value_load(ptab[0:1, bass.ds(b * NPG + j, 1)], min_val=0, max_val=N_POOL - 1)
                        pool.dma_start(lfp[:, j, bass.ds(b * FH, FH)], I["cache_fox_logf"][bass.ds(l, 1), bass.ds(page, 1)].rearrange("a n p h -> p (a n h)")).then_inc(past_in, 16)
                pool.wait_ge(fg_dve, FG_DVE.at(l, "nc"))
                pool.sem_inc(passed, 1)
                pool.dma_start(decay_rows, ncr).then_inc(decay_out, 16)
                for b in range(DB):
                    pool.dma_start(lfnew[FH * b:FH * b + FH, :], fl[0:FH, T + TS * b:T + TS * b + TS]).then_inc(past_in, 16)
                pool.wait_ge(*evac_at(l, J_OUT - 2))
                pool.wait_ge(*evac_at(l, J_OUT - 1))
                pool.dma_start(O["fox_v_prompt"][bass.ds(l, 1)].rearrange("a n p h d -> p (a n) (h d)"), fv[:, 0:NTT, :]).then_inc(fox_out, 16)
                pool.dma_start(O["fox_v_sample"][bass.ds(l, 1)].rearrange("a b t h d -> (a b t) (h d)"), fv[0:NS, NTT, :]).then_inc(fox_out2, 16)
                def stage(p, copy=True):
                    if copy:
                        FP_POOL.mark(pool.tensor_copy(qtp[p % 2], fqk[:, p, :]), fp_pool, "q")
                        FP_POOL.mark(pool.tensor_copy(ktp[p % 2], fqk[:, 4 + p, :]), fp_pool, "k")
                    else:
                        pool.wait_ge(fg_dve, FG_DVE.at(l, "k0"))
                        pool.sem_inc(fp_pool, 2)

                def stage_values(p):
                    FP_POOL.start()
                    pool.dma_start(ncb[p % 2], decay_rows[2 * p:2 * p + 2, :].unsqueeze(0).to_broadcast((P, 2, T))).then_inc(fp_ncb[p % 2], 16)
                    FP_POOL.mark(pool.tensor_copy(vp[p % 2], fv[:, 0:NTT, P * p:P * p + P]), fp_pool, "v")

                pool.wait_ge(decay_out, l * 16 + 16)
                pool.sem_inc(passed, 1)
                stage_values(0)
                pool.wait_ge(fn_dve, FN_DVE.at(l * 4 + 3, "n1"))
                pool.sem_inc(passed, 1)
                pool.dma_start(fmask, cst[:, CONSTS["fmask"][0]:CONSTS["fmask"][0] + P]).then_inc(fox_const, 16)
                stage(0, copy=False)
                pool.wait_ge(fg_act, FG_ACT.at(l, "lft"))
                pool.sem_inc(passed, 1)
                lf3 = lft.rearrange("p (n h) -> p n h", h=FH)
                pool.dma_start(O["fox_logf_prompt"][bass.ds(l, 1)].rearrange("a n p h -> p (a n) h"), lf3[:, 0:NTT, :]).then_inc(lft_out, 16)
                pool.dma_start(O["fox_logf_sample"][bass.ds(l, 1)].rearrange("a b t h -> (a b t) h"), lf3[0:NS, NTT, :]).then_inc(lft_out, 16)
                stage_values(1)
                stage(1)
                for p in range(4):
                    it = l * 2 + p // 2
                    pool.wait_ge(fp_act, FP_ACT.at(it, f"{p % 2}kos"))
                    pool.sem_inc(passed, 1)
                    pool.dma_start(O["fox_k_prompt"][bass.ds(l, 1), :, :, 2 * p:2 * p + 2, :].rearrange("a n p h d -> p (a n) (h d)"), ko).then_inc(ko_out, 16)
                    pool.dma_start(O["fox_k_sample"][bass.ds(l, 1), :, :, 2 * p:2 * p + 2, :].rearrange("a b t h d -> (a b t) (h d)"), kos[0:NS]).then_inc(ko_out, 16)
                    pool.wait_ge(ko_out, l * 128 + (p * 32 + 32))
                    pool.sem_inc(ko_free, 1)
                    if p < 2:
                        pool.wait_ge(fp_act, FP_ACT.at(it, f"{p % 2}oT"))
                        pool.sem_inc(passed, 1)
                        stage_values(p + 2)
                        stage(p + 2)
                pool.wait_ge(fp_act, FP_ACT.at(l * 2 + 1, "1oT"))
                pool.sem_inc(passed, 1)
                for dst, name, w in ((ssel, "s_sel", 2 * P), (sreq, "s_req", 2 * DB), (region((wdf, 1936), 28), "s_fmask", 28)):
                    pool.dma_start(dst, cst[:, CONSTS[name][0]:CONSTS[name][0] + w]).then_inc(fox_const, 16)
                with pool.Fori(0, 2) as g:
                    it = l * 2 + g
                    for b in range(4):
                        pool.wait_ge(fgr_pe, G_PE.at(it, f"T{b}3"))
                        pool.sem_inc(passed, 1)
                        for j in range(V_SP, NPG):
                            page = pool.value_load(ptab[0:1, bass.ds(g * (4 * NPG) + (b * NPG + j), 1)], min_val=0, max_val=N_POOL - 1)
                            pool.dma_start(slot[b][:, j, :], I["cache_fox_v"][bass.ds(l, 1), bass.ds(page, 1)].rearrange("a n p h d -> p (a n h d)")).then_inc(vpage_in[b], 16)
            pool.wait_ge(fox_out, DEPTH * 16)
            pool.wait_ge(fox_out2, DEPTH * 16)
            pool.wait_ge(lft_out, DEPTH * 32)
            pool.wait_ge(ko_out, DEPTH * 128)
            pool.wait_ge(re_out, DEPTH * 48)
            pool.wait_ge(shift_out, DEPTH * 8 * 16)
            pool.wait_ge(rs_out, DEPTH * 16)
            pool.wait_ge(ro_out, DEPTH * 16)
            with pool.Fori(0, NTT // 2) as t:
                for u in range(2):
                    pool.wait_ge(y_ev, t * 2 + u + 1)
                    pool.dma_start(O["y_prompt"][0, bass.ds((t * 2 + u) * P, P), :], yrows[:, u, :]).then_inc(y_out[u], 16)
            pool.wait_ge(y_ev, NTT + 1)
            pool.dma_start(O["y_sample"].rearrange("b t d -> (b t) d"), yrows[0:NS, 0, :]).then_inc(y_out[0], 16)
            pool.wait_ge(y_out[0], 16 * (NTT // 2 + 1))
            pool.wait_ge(y_out[1], 16 * (NTT // 2))

        @block.tensor
        def _(pe):
            def mm(out, lhsT, rhs, start=True, stop=True):
                return pe.matmul(out, lhsT, rhs, start=start, stop=stop, skip_group_check=True)

            def tr(out, in_):
                n = in_.shape[0]
                return pe.transpose(out, in_, ident[0:n, 0:n])

            def norm_sum(it, k):
                if k == 0:
                    NRM_PE.start()
                pe.wait_ge(n_dve, NRM_DVE.at(it, f"sq{k}"))
                for b in range(3):
                    last = mm(ps[32 * b:32 * b + 32, 6, 0:TB], ones[:, 0:32], nsq[:, k % 2, TB * b:TB * b + TB], k == 0, k == KT - 1)
                NRM_PE.mark(last, n_pe, f"sum{k}")

            def norm_rows(it):
                pe.wait_ge(n_act, NRM_ACT.at(it, "rstd"))
                for b in range(3):
                    last = mm(ps[:, 3 + b, 0:TB], share[32 * b:32 * b + 32, :], nrs[32 * b:32 * b + 32, :])
                NRM_PE.mark(last, n_pe, "rows")

            def job_fm(l, j, rhs, q=0, norm=None):
                pe.wait_ge(loaded[j % RING], l * (16 * JOBS // RING) + q * 16 + 16 * (j // RING + 1))
                pe.wait_ge(evac[j % 2], l * HALF + q * 2 + (j // 2 + 1))
                for b in range(3):
                    for k in range(KT):
                        if norm is not None and b == 0:
                            pe.wait_ge(n_dve, NRM_DVE.at(norm, f"h{k}"))
                        last = mm(ps[:, 3 * (j % 2) + b, 0:TB], ring[:, j % RING, k, :], rhs(k)[:, TB * b:TB * b + TB], k == 0, k == KT - 1)
                last.then_inc(gemm_done, 1)

            def job_tm(l, j):
                pe.wait_ge(loaded[j % RING], l * (16 * JOBS // RING) + 16 * (j // RING + 1))
                pe.wait_ge(evac[j % 2], l * HALF + (j // 2 + 1))
                for i in range(NTT + 1):
                    n = P if i < NTT else NS
                    for k in range(KT):
                        last = mm(ps[0:n, 3 * (j % 2) + i // 4, P * (i % 4):P * (i % 4) + P], hT[:, k, P * i:P * i + n], ring[:, j % RING, k, :], k == 0, k == KT - 1)
                last.then_inc(gemm_done, 1)

            def h_tile(k):
                return hT[:, k, :]

            def col2(name, i):
                return cols[:, COLS[name][0] + i:COLS[name][0] + i + 2]

            pe.wait_ge(consts_in, 2 * 16)
            with pe.Fori(0, NTT // 2) as t:
                for u in range(2):
                    pe.wait_ge(x_in[u], t * 16 + 16)
                    pe.wait_ge(xt_ev, t * 2 + u + 1)
                    for k in range(KT):
                        last = tr(ps[:, 4 * u + k // 4, P * (k % 4):P * (k % 4) + P], xstage[:, u, P * k:P * k + P])
                    last.then_inc(xt_pe, 1)
            pe.wait_ge(x_in[0], 16 * (NTT // 2 + 1))
            pe.wait_ge(xt_ev, NTT + 1)
            for k in range(KT):
                last = tr(ps[:, 0, NS * k:NS * k + NS], xstage[0:NS, 0, P * k:P * k + P])
            last.then_inc(xt_pe, 1)

            for k in range(KT):
                norm_sum(0, k)
            with pe.Fori(0, DEPTH) as l:
                norm_rows(2 * l)
                job_fm(l, J_R, h_tile, norm=2 * l)
                for j in range(J_R + 1, J_EQ):
                    job_fm(l, j, h_tile)

                PR_PE.start()
                for m in range(2):
                    for s, (name, r0) in enumerate((("w", 0), ("a", 32))):
                        if m == 0:
                            pe.wait_ge(*((pr_act, PR_ACT.at(l, "tanh")) if s == 0 else (pr_dve, PR_DVE.at(l, "xs6"))))
                            if s == 0:
                                pe.wait_ge(*evac_at(l, 6))
                                pe.wait_ge(*evac_at(l, 7))
                                pe.wait_ge(params_in, l * (16 * NPARAM) + 16 * NPARAM)
                                pe.wait_ge(cols_ready, l + 1)
                        else:
                            pe.wait_ge(pr_act, PR_ACT.at(l, f"{'sw' if s == 0 else 'a'}0"))
                        for b, (a, e) in enumerate(((0, 512), (512, 1024), (1024, XW))):
                            last = mm(ps[:, 4 * s + b, 0:e - a], lora[r0:r0 + 32, P * m:P * m + P], xs[r0:r0 + 32, 6, a:e])
                        PR_PE.mark(last, pr_pe, f"{name}{m}")
                for m in range(2):
                    pe.wait_ge(pr_dve, PR_DVE.at(l, f"ksq{m}"))
                    pe.wait_ge(pr_act, PR_ACT.at(l, "a1"))
                    for b, (a, e) in enumerate(((0, 512), (512, 1024), (1024, XW))):
                        last = mm(ps[:, 4 * m + b, 0:e - a], blk[:, :], sq1[m][:, a:e])
                    PR_PE.mark(last, pr_pe, f"ss{m}")

                pos = lambda h: 2 * (h % 2) + h // 2
                half = lambda h: slice(HD * (h % 2), HD * (h % 2) + HD)

                def operands(it):
                    RP_PE.start()
                    pe.wait_ge(rp_dve, RP_DVE.at(it, "R"))
                    arh = lambda h: ar[half(h), h // 2, :, :].rearrange("p a t -> p (a t)")
                    for h in range(RH):
                        last = mm(ps[:, h % 2, 256 * (h // 2):256 * (h // 2) + 256], bt[half(h), h // 2, :], arh(h))
                    RP_PE.mark(last, rp_pe, "Lab")
                    pe.wait_ge(rp_dve, RP_DVE.at(it, "sm1"))
                    for h in range(RH):
                        last = mm(ps[:, 4 + h % 2, P * (h // 2):P * (h // 2) + P], ar[half(h), h // 2, 0, :], bt[half(h), h // 2, :])
                    RP_PE.mark(last, rp_pe, "L")
                    for h in range(RH):
                        last = mm(ps[:, 2 + h % 2, 256 * (h // 2):256 * (h // 2) + 256], kt_[half(h), h // 2, :], arh(h))
                    RP_PE.mark(last, rp_pe, "Lk")
                    pe.wait_ge(rw_pool, RW_POOL.at(it, "sg"))
                    for m in range(2):
                        tr(ps[:, 6, P * m:P * m + P], vs[:, m, :])
                        tr(ps[:, 6, 256 + P * m:256 + P * m + P], bt[:, m, :])
                        tr(ps[:, 7, P * m:P * m + P], kt_[:, m, :])
                        last = mm(ps[:, 7, 256 + 2 * m:258 + 2 * m], rk2[:, m, :], col2("rk", 2 * m))
                    RP_PE.mark(last, rp_pe, "tr")

                pe.wait_ge(pr_dve, PR_DVE.at(l, "bv1"))
                operands(l * (NTT + 1))
                with pe.Fori(0, NTT) as c:
                    it = l * NTT + c
                    RW_PE.start()

                    def heads(name, bank, lhsT, rhs, waits, width=P):
                        for s, v in waits:
                            pe.wait_ge(s, v)
                        for h in range(RH):
                            o = ps[:, bank, width * h:width * h + width]
                            last = mm(o, lhsT(h), rhs(h))
                        RW_PE.mark(last, rw_pe, name)

                    def dv(n):
                        return (rw_dve, RW_DVE.at(it, n))

                    def ac(n):
                        return (rw_act, RW_ACT.at(it, n))

                    S = lambda i: (lambda h: sl[i][:, h, :])
                    vtok = lambda h: vbk[:, h // 2, half(h)]
                    btok = lambda h: vbk[:, 2 + h // 2, half(h)]
                    ktok = lambda h: vbk[:, 4 + h // 2, half(h)]
                    x0 = lambda h: sl[4][:, 0:2, :].rearrange("p a b -> p (a b)")[:, HD * h:HD * h + HD]
                    uu = lambda h: sl[5][:, 0:2, :].rearrange("p a b -> p (a b)")[:, HD * h:HD * h + HD]
                    x_out = lambda h: ps[:, 5, P + HD * (h // 2):P + HD * (h // 2) + HD] if h % 2 else ps[:, 6, HD * (h // 2):HD * (h // 2) + HD]
                    y_out_ = lambda h: ps[:, 4 - h % 2, HD * (h // 2):HD * (h // 2) + HD]
                    s_out = lambda h: ps[half(h), 5, HD * (h // 2):HD * (h // 2) + HD]

                    def x_state(h):
                        return mm(x_out(h), ar[half(h), h // 2, 0, :], stm[half(h), h // 2, :], h < 2, False)

                    def x_values(h):
                        return mm(x_out(h), sl[1][:, pos(h), :], vtok(h), False, True)

                    def y_state(h):
                        return mm(y_out_(h), ar[half(h), h // 2, 1, :], stm[half(h), h // 2, :], h < 2, False)

                    def y_values(h):
                        return mm(y_out_(h), sl[3][:, pos(h), :], vtok(h), False, False)

                    def new_keys(h):
                        return mm(s_out(h), ktok(h), vtok(h), False, False)

                    heads("D2", 0, S(5), S(4), [dv("D")])
                    heads("D2T", 1, S(4), S(5), [])
                    pe.wait_ge(*dv("N"))
                    pe.wait_ge(rw_act, RW_ACT.at(it - 1, "ro"))
                    pe.wait_ge(rv_act, RV_ACT.at(l * (NTT + 1) + c, "vbk"))
                    x_state(0)
                    x_state(1)
                    heads("D4", 2, S(7), S(6), [ac("D2T"), dv("Lrk")])
                    heads("D4T", 3, S(6), S(7), [])
                    heads("Z2", 4, S(6), S(8), [])
                    heads("D8", 0, S(5), S(4), [ac("D4T")])
                    heads("Z3", 1, S(4), S(8), [dv("Z2")])
                    pe.wait_ge(rv_act, RV_ACT.at(l * (NTT + 1) + c, "bon"))
                    last = mm(ps[:, 7, 0:RW], sg[64:P, :], lora[64:P, :])
                    RW_PE.mark(last, rw_pe, "g")
                    heads("Z4", 2, S(6), S(8), [dv("Z3")])
                    new_keys(0)
                    new_keys(1)
                    heads("Q", 3, S(8), S(0), [dv("Z4")])
                    heads("QT", 4, S(0), S(8), [])
                    for h in range(RH):
                        last = tr(ps[:, 0, P * h:P * h + P], sl[8][:, h, :])
                    RW_PE.mark(last, rw_pe, "M")
                    new_keys(2)
                    new_keys(3)
                    heads("Q2", 1, S(5), S(4), [ac("Q"), dv("Y0")])
                    heads("Q2T", 2, S(4), S(5), [])
                    x_state(2)
                    x_state(3)
                    heads("Q4", 3, S(7), S(6), [ac("Q2"), dv("Q2T")])
                    heads("Y1", 4, S(6), S(10), [])
                    x_values(0)
                    x_values(1)
                    heads("Y2", 0, S(4), S(10), [ac("Q4"), dv("Y1")])
                    x_values(2)
                    last = x_values(3)
                    RW_PE.mark(last, rw_pe, "X0")
                    heads("TT", 1, S(9), S(10), [dv("Y2")])
                    for h in range(2):
                        y_state(h)
                        y_values(h)
                    pe.wait_ge(*ac("TT"))
                    pe.wait_ge(*dv("X0b"))
                    for h in range(RH):
                        last = mm(ps[:, 2, HD * h:HD * h + HD], sl[8][:, pos(h), :], x0(h))
                    RW_PE.mark(last, rw_pe, "U")
                    for h in range(2, RH):
                        y_state(h)
                        y_values(h)
                    pe.wait_ge(*ac("U"))
                    for h in range(RH):
                        last = mm(y_out_(h), sl[2][:, pos(h), :], uu(h), False, True)
                    RW_PE.mark(last, rw_pe, "Y")
                    for h in range(RH):
                        last = mm(s_out(h), btok(h), uu(h), False, True)
                    RW_PE.mark(last, rw_pe, "dS")
                    pe.wait_ge(*ac("Y"))
                    operands(l * (NTT + 1) + c + 1)
                    pe.wait_ge(rv_act, RV_ACT.at(l * (NTT + 1) + c + 1, "vbk"))
                    pe.wait_ge(*dv("yg"))
                    for m in range(2):
                        last = tr(ps[:, 6, P * m:P * m + P], sl[6][:, m, :])
                    RW_PE.mark(last, rw_pe, "ro")
                pe.wait_ge(rw_act, RW_ACT.at(l * NTT + NTT - 1, "ro"))
                pe.sem_inc(passed, 1)
                for m in range(2):
                    last = tr(ps[0:HD, 0, P * m:P * m + P], st[:, m, :])
                last.then_inc(ro_pe, 1)

                RS_PE.start()
                ac = lambda n: (rs_act, RS_ACT.at(l, n))
                dv = lambda n: (rs_dve, RS_DVE.at(l, n))
                SR = slice(0, NS)
                pe.wait_ge(rs_in, l * 16 + 16)
                pe.wait_ge(ro_act, l + 1)
                pe.sem_inc(passed, 1)
                for m in range(2):
                    for b in range(DB):
                        last = tr(ps[:, m, HD * b:HD * b + HD], nat[0:HD, b, P * m:P * m + P])
                RS_PE.mark(last, rs_pe, "st")
                pe.wait_ge(*dv("sts"))
                pe.sem_inc(passed, 1)
                for h in range(RH):
                    m, r = h // 2, half(h)
                    arh = ars[r, m, :, :].rearrange("p a t -> p (a t)")
                    mm(ps[SR, h % 2, 64 * m:64 * m + 64], bts[r, m, :], arh)
                    mm(ps[SR, 2 + h % 2, 64 * m:64 * m + 64], kts[r, m, :], arh)
                    last = mm(ps[SR, 4 + h % 2, NS * m:NS * m + NS], ars[r, m, 0, :], bts[r, m, :])
                RS_PE.mark(last, rs_pe, "L")
                for m in range(2):
                    tr(ps[SR, 6, P * m:P * m + P], vss[:, m, :])
                    tr(ps[SR, 6, 256 + P * m:256 + P * m + P], bts[:, m, :])
                    tr(ps[SR, 7, P * m:P * m + P], kts[:, m, :])
                    last = mm(ps[SR, 7, 256 + 2 * m:258 + 2 * m], rk2s[:, m, :], col2("rk", 2 * m))
                RS_PE.mark(last, rs_pe, "tr")
                pe.wait_ge(*dv("Lrk"))
                pe.sem_inc(passed, 1)
                for h in range(RH):
                    last = mm(ps[SR, 0, NS * h:NS * h + NS], smat[1][SR, h, :], smat[0][SR, h, :])
                RS_PE.mark(last, rs_pe, "D2")
                pe.wait_ge(*ac("D2"))
                pe.sem_inc(passed, 1)
                for h in range(RH):
                    last = mm(ps[SR, 1, NS * h:NS * h + NS], smat[2][SR, h, :], smat[3][SR, h, :])
                RS_PE.mark(last, rs_pe, "Z2")
                last = mm(ps[SR, 7, 0:RW], sgs[64:P, :], lora[64:P, :])
                RS_PE.mark(last, rs_pe, "g")
                vts = lambda h: vbks[SR, h // 2, half(h)]
                hd = lambda t, h: t[SR, HD * h:HD * h + HD]
                for h in range(RH):
                    m, r = h // 2, half(h)
                    o = ps[SR, 2 + h % 2, HD * m:HD * m + HD]
                    for b in range(DB):
                        mm(o, aex[r, m, b, :], sts[r, m, b, :], b == 0, False)
                    last = mm(o, smat[5][SR, pos(h), :], vts(h), False, True)
                RS_PE.mark(last, rs_pe, "X0")
                pe.wait_ge(*dv("X0"))
                pe.sem_inc(passed, 1)
                for h in range(RH):
                    last = mm(ps[SR, 6, HD * h:HD * h + HD], smat[3][SR, pos(h), :], hd(x0s, h))
                RS_PE.mark(last, rs_pe, "U")
                pe.wait_ge(*ac("U"))
                pe.sem_inc(passed, 1)
                for h in range(RH):
                    m, r = h // 2, half(h)
                    o = ps[SR, 4 - h % 2, HD * m:HD * m + HD]
                    for b in range(DB):
                        mm(o, rex[r, m, b, :], sts[r, m, b, :], b == 0, False)
                    mm(o, smat[6][SR, pos(h), :], vts(h), False, False)
                    last = mm(o, smat[4][SR, pos(h), :], hd(us, h), False, True)
                RS_PE.mark(last, rs_pe, "Y")
                pe.wait_ge(*dv("vex3"))
                for h in range(RH):
                    m, r = h // 2, half(h)
                    o = ps[r, m, :]
                    mm(o, vbks[SR, 2 + m, half(h)], uex[SR, h].rearrange("p b d -> p (b d)"), True, False)
                    last = mm(o, vbks[SR, 4 + m, half(h)], vex[SR, h].rearrange("p b d -> p (b d)"), False, True)
                RS_PE.mark(last, rs_pe, "dS")
                pe.wait_ge(*dv("yg"))
                pe.sem_inc(passed, 1)
                for m in range(2):
                    last = tr(ps[:, 6, NS * m:NS * m + NS], yns[SR, P * m:P * m + P])
                RS_PE.mark(last, rs_pe, "ro")
                for m in range(2):
                    for b in range(DB):
                        last = tr(ps[0:HD, 2 * m + b // 4, P * (b % 4):P * (b % 4) + P], sts[:, m, b, :])
                RS_PE.mark(last, rs_pe, "nat")

                pe.wait_ge(*ac("nat"))
                pe.wait_ge(ro_act, l + 1)
                for j in range(J_EQ, J_EV):
                    job_fm(l, j, h_tile)
                for j in range(J_EV, J_FQ):
                    job_tm(l, j)
                pe.wait_ge(*evac_at(l, J_EV + 2))
                pe.wait_ge(*evac_at(l, J_EV + 3))
                pe.wait_ge(re_in, l * 80 + 80)
                RE_PE.start()
                for i in range(4):
                    if i >= 2:
                        pe.wait_ge(re_dve, RE_DVE.at(l, f"ts{i - 2}"))
                    for b in range(3):
                        last = mm(ps[:, 3 * (i % 2) + b, 0:TB], rot, eqk[:, i, TB * b:TB * b + TB])
                    RE_PE.mark(last, re_pe, f"rot{i}")
                pe.wait_ge(re_dve, RE_DVE.at(l, "add3"))
                pe.sem_inc(passed, 1)

                def ret_scores(it):
                    RQ_PE.start()
                    pe.wait_ge(rt_pool, RT_POOL.at(it, "k"))
                    for h in range(EH):
                        m, r = h // 2, half(h)
                        last = mm(ps[:, h % 2, P * m:P * m + P], ks[r, m, :], qs[r, m, :])
                    RQ_PE.mark(last, rq_pe, "S")
                    for m in range(2):
                        last = tr(ps[:, 2, P * m:P * m + P], ks[:, m, :])
                    RQ_PE.mark(last, rq_pe, "kt")

                ret_scores(l * (NTT + 1))
                with pe.Fori(0, NTT) as c:
                    it = l * NTT + c
                    now = l * (NTT + 1) + c
                    RT_PE.start()
                    pe.wait_ge(rt_pool, RT_POOL.at(now, "v"))
                    pe.wait_ge(rq_dve, RQ_DVE.at(now, "kd"))
                    for h in range(EH):
                        m, r = h // 2, half(h)
                        o = ps[:, 4 - h % 2, HD * m:HD * m + HD]
                        mm(o, stt[:, pos(h), :], ve[:, HD * h:HD * h + HD], True, False)
                        last = mm(o, qd[r, m, :], rst[r, m, :], False, True)
                    RT_PE.mark(last, rt_pe, "O")
                    for h in range(EH):
                        last = mm(ps[half(h), 5, HD * (h // 2):HD * (h // 2) + HD], kd[:, h, :], ve[:, HD * h:HD * h + HD])
                    RT_PE.mark(last, rt_pe, "dR")
                    ret_scores(now + 1)
                pe.wait_ge(rt_dve, RT_DVE.at(l * NTT + NTT - 1, "yg"))
                for m in range(2):
                    for i in range(NTT):
                        last = tr(ps[:, 4 + 2 * m + i // 4, P * (i % 4):P * (i % 4) + P], evg[:, i, EW + P * m:EW + P * m + P])
                last.then_inc(ret_rows, 1)
                pe.wait_ge(ret_rows_out, l + 1)
                pe.wait_ge(rt_pool, RT_POOL.at(l * (NTT + 1) + NTT, "v"))
                pe.wait_ge(rq_dve, RQ_DVE.at(l * (NTT + 1) + NTT, "kd"))
                pe.sem_inc(passed, 1)
                for h in range(EH):
                    m, r = h // 2, half(h)
                    last = mm(ps[SR, h % 2, NS * m:NS * m + NS], eqk[r, 2 + m, T:NT], eqk[r, m, T:NT])
                RE_PE.mark(last, re_pe, "S")
                for m in range(2):
                    last = tr(ps[SR, 2, P * m:P * m + P], eqk[:, 2 + m, T:NT])
                RE_PE.mark(last, re_pe, "kt")
                pe.wait_ge(re_dve, RE_DVE.at(l, "st"))
                pe.sem_inc(passed, 1)
                for h in range(EH):
                    m, r = h // 2, half(h)
                    o = ps[SR, 4 - h % 2, HD * m:HD * m + HD]
                    mm(o, stts[SR, pos(h), :], evg[SR, NTT, HD * h:HD * h + HD], True, False)
                    for b in range(DB):
                        last = mm(o, qex[r, m, b, :], rss[r, m, b, :], False, b == DB - 1)
                RE_PE.mark(last, re_pe, "O")
                pe.wait_ge(re_dve, RE_DVE.at(l, "vex3"))
                for h in range(EH):
                    last = mm(ps[half(h), h // 2, :], kds[SR, h, :], vexe[SR, h].rearrange("p b e -> p (b e)"))
                RE_PE.mark(last, re_pe, "dR")
                pe.wait_ge(re_dve, RE_DVE.at(l, "yg"))
                pe.sem_inc(passed, 1)
                for m in range(2):
                    last = tr(ps[:, 6, NS * m:NS * m + NS], yne[SR, P * m:P * m + P])
                RE_PE.mark(last, re_pe, "ro")
                pe.wait_ge(re_act, RE_ACT.at(l, "ro"))
                for j in range(J_FQ, J_FV):
                    job_fm(l, j, h_tile)
                for j in range(J_FV, J_OUT):
                    job_tm(l, j)
                pe.wait_ge(*evac_at(l, J_OUT - 1))
                pe.wait_ge(*evac_at(l, J_OUT - 2))
                pe.sem_inc(passed, 1)
                with pe.Fori(0, 4) as i:
                    it = l * 4 + i
                    FN_PE.start()
                    for u in range(2):
                        pe.wait_ge(fn_dve, FN_DVE.at(it, f"sq{u}"))
                        for b in range(3):
                            last = mm(ps[:, 3 * u + b, 0:TB], blk[:, :], fsq[:, u, TB * b:TB * b + TB])
                        FN_PE.mark(last, fn_pe, f"ss{u}")
                FG_PE.start()
                pe.wait_ge(fg_dve, FG_DVE.at(l, "logf"))
                pe.sem_inc(passed, 1)
                for i in range(NTT + 1):
                    n = P if i < NTT else NS
                    last = tr(ps[0:n, 7, FH * i:FH * i + FH], fl[0:FH, P * i:P * i + n])
                FG_PE.mark(last, fg_pe, "lft")
                pe.wait_ge(fg_act, FG_ACT.at(l, "lft"))
                pe.sem_inc(passed, 1)
                pe.wait_ge(fox_const, l * 64 + 16)
                pe.sem_inc(passed, 1)
                with pe.Fori(0, 2) as pp:
                    it = l * 2 + pp
                    FP_PE.start()
                    fd = lambda n: (fp_dve, FP_DVE.at(it, n))
                    fa = lambda n: (fp_act, FP_ACT.at(it, n))

                    def scores(u, s):
                        i, hh = s // 2, s % 2
                        if s >= 2:
                            pe.wait_ge(*fd(f"{u}d{s - 2}"))
                        r = slice(HD * hh, HD * hh + HD)
                        for a in range(0, P * (i + 1), 512):
                            e = min(a + 512, P * (i + 1))
                            mm(ps[:, 2 * hh + a // 512, 0:e - a], qtp[u][r, P * i:P * i + P], ktp[u][r, a:e], True, e < P * (i + 1))
                        last = mm(ps[:, 2 * hh + i // 4, P * (i % 4):P * (i % 4) + P], ident[:, :], fmask, False, True)
                        FP_PE.mark(last, fp_pe, f"{u}S{s}")

                    for u in range(2):
                        pe.wait_ge(fp_pool, FP_POOL.at(l * 4 + pp * 2 + u, "k"))
                        pe.wait_ge(fp_act, FP_ACT.at(it, "0oT") if u else FP_ACT.at(it - 1, "1oT"))
                        for i in range(NTT):
                            tr(ps[:, 4 + i // 4, P * (i % 4):P * (i % 4) + P], ktp[u][:, P * i:P * i + P])
                        last = tr(ps[0:NS, 6, 0:P], ktp[u][:, T:NT])
                        FP_PE.mark(last, fp_pe, f"{u}ko")
                        scores(u, 0)
                        scores(u, 1)
                        for s in SC:
                            i, hh = s // 2, s % 2
                            pe.wait_ge(*fa(f"{u}e{s}"))
                            pe.wait_ge(*(fa(f"{u}kos") if s == 0 else fd(f"{u}pt{s - 1}") if (s - 1) % 2 else fa(f"{u}pt{s - 1}")))
                            for k in range(i + 1):
                                last = tr(ps[:, 4 + k // 4, P * (k % 4):P * (k % 4) + P], sp_[:, hh, P * k:P * k + P])
                            FP_PE.mark(last, fp_pe, f"{u}T{s}")
                            if s + 2 < 2 * NTT:
                                scores(u, s + 2)
                            pe.wait_ge(*(fd(f"{u}pt{s}") if s % 2 else fa(f"{u}pt{s}")))
                            if s >= 2:
                                pe.wait_ge(*fd(f"{u}o{s - 2}"))
                            for k in range(i + 1):
                                last = mm(ps[:, 6 + hh, 0:P], ptt[:, hh, k, :], vp[u][:, k, :], k == 0, k == i)
                            FP_PE.mark(last, fp_pe, f"{u}V{s}")
                        pe.wait_ge(*fd(f"{u}o{2 * NTT - 1}"))
                        for i in range(NTT):
                            last = tr(ps[:, 4 + i // 4, P * (i % 4):P * (i % 4) + P], otok[:, i, :])
                        FP_PE.mark(last, fp_pe, f"{u}oT")
                pe.wait_ge(fp_act, FP_ACT.at(l * 2 + 1, "1oT"))
                pe.wait_ge(past_in, l * NPAST + NPAST)
                pe.wait_ge(fox_const, l * 64 + 64)
                pe.sem_inc(passed, 1)
                for j in range(NPG):
                    last = tr(ps[0:DB * FH, j // 4, P * (j % 4):P * (j % 4) + P], lfp[:, j, :])
                last.then_inc(fs_pe, 1)
                with pe.Fori(0, 2) as g:
                    it = l * 2 + g
                    G_PE.start()
                    gd = lambda n: (fgr_dve, G_DVE.at(it, n))
                    ga = lambda n: (fgr_act, G_ACT.at(it, n))
                    ev = lambda b, p: (gd if p % 2 else ga)(f"kt{b}{p}")
                    pe.wait_ge(*gd("creq"))
                    R64 = slice(0, DB * FH)
                    for a in range(2):
                        mm(ps[:, a, :], cur_sel[R64, :], ncs[R64, 512 * a:512 * a + 512], True, False)
                    last = mm(ps[:, 2, 0:TS], cur_sel[R64, :], ncs[R64, NP:NP + TS], True, False)
                    G_PE.mark(last, fgr_pe, "bias")

                    def key_tr(b, p):
                        if b or p >= 2:
                            pe.wait_ge(*(ev(b, p - 2) if p >= 2 else ev(b - 1, p + 2)))
                        for j in range(NPG):
                            last = tr(ps[:, 3 + 2 * (p % 2) + j // 4, P * (j % 4):P * (j % 4) + P], slot[b][:, j, P * p:P * p + P])
                        G_PE.mark(last, fgr_pe, f"T{b}{p}")

                    for b in range(4):
                        pe.wait_ge(page_in[b], it * ((NPG + V_SP) * 16) + NPG * 16)
                        key_tr(b, 0)
                        for p in range(4):
                            if p < 3:
                                key_tr(b, p + 1)
                            pe.wait_ge(*ev(b, p))
                            o = slice(NS * b, NS * b + NS)
                            last_one = p == 3
                            for a in range(2):
                                mm(ps[o, a, :], cur_q[:, b, p, :], keyt[p % 2][:, 512 * a:512 * a + 512], False, last_one)
                            last = mm(ps[o, 2, 0:TS], cur_q[:, b, p, :], cur_k[:, p, TS * b:TS * b + TS], False, last_one)
                            G_PE.mark(last, fgr_pe, f"S{b}{p}")
                    pe.wait_ge(*gd("pn"))
                    for c in range(2):
                        for j in range(4 * c, 4 * c + 4):
                            last = tr(ps[:, 3 + c, P * (j % 4):P * (j % 4) + P], pss[:, P * j:P * j + P])
                        G_PE.mark(last, fgr_pe, f"P{c}")
                    pe.wait_ge(*gd("pne"))
                    last = tr(ps[0:NS, 5, 0:P], pn.rearrange("p b s -> p (b s)"))
                    G_PE.mark(last, fgr_pe, "Pn")
                    pe.wait_ge(*gd("pnt"))
                    pe.wait_ge(*ga("pt0"))
                    mm(ps[:, 7, :], pnt[0:NS, :], vn[0:NS, :], True, False)
                    for b in range(4):
                        pe.wait_ge(page_in[b], it * ((NPG + V_SP) * 16) + (NPG + V_SP) * 16)
                        pe.wait_ge(vpage_in[b], it * ((NPG - V_SP) * 16) + (NPG - V_SP) * 16)
                        o = slice(NS * b, NS * b + NS)
                        for j in range(NPG):
                            last = mm(ps[o, 7, :], pts[:, j, o], slot[b][:, j, :], False, j == NPG - 1)
                        G_PE.mark(last, fgr_pe, f"V{b}")
                    pe.wait_ge(*gd("om"))
                    for p in range(4):
                        last = mm(ps[:, 5, 16 * p:16 * p + 16], om[:, P * p:P * p + P], stok)
                    G_PE.mark(last, fgr_pe, "F")
                pe.wait_ge(fgr_dve, G_DVE.at(l * 2 + 1, "o"))
                for j in range(J_OUT, J_FF):
                    job_fm(l, j, lambda k: hT[:, k, :] if k < 4 else mixB[:, k - 4, :])
                    if j > J_OUT:
                        norm_sum(2 * l + 1, j - J_OUT - 1)
                norm_sum(2 * l + 1, KT - 1)
                norm_rows(2 * l + 1)
                pe.wait_ge(n_dve, NRM_DVE.at(2 * l + 1, "h0"))
                pe.sem_inc(passed, 1)
                with pe.Fori(0, FT // 2) as q:
                    job_fm(l, J_FF, h_tile, q=q, norm=2 * l + 1)
                    for u in range(1, RING):
                        job_fm(l, J_FF + u, h_tile, q=q)
                pe.wait_ge(*evac_at(l, JOBS - 1))
                for j in range(KT):
                    pe.wait_ge(down_loaded[j % 2], l * (16 * KT // 2) + 16 * (j // 2 + 1))
                    pe.wait_ge(evac[j % 2], l * HALF + ((J_DOWN + j) // 2 + 1))
                    for b in range(3):
                        for k in range(FT):
                            last = mm(ps[:, 3 * (j % 2) + b, 0:TB], wd[:, j % 2, k, :], h2[:, k, TB * b:TB * b + TB], k == 0, k == FT - 1)
                    last.then_inc(gemm_done, 1)
                    if j:
                        norm_sum(2 * l + 2, j - 1)
                norm_sum(2 * l + 2, KT - 1)
            def y_tile(t, u):
                pe.wait_ge(y_st, t * 2 + (u + 1))
                for k in range(KT):
                    last = tr(ps[:, 4 * u + k // 4, P * (k % 4):P * (k % 4) + P], ytile[:, k, :])
                last.then_inc(y_pe, 1)

            for u in range(2):
                y_tile(0, u)
            with pe.Fori(1, NTT // 2) as t:
                for u in range(2):
                    pe.wait_ge(y_ev, t * 2 + (u - 1))
                    y_tile(t, u)
            pe.wait_ge(y_ev, NTT - 1)
            pe.wait_ge(y_st, NTT + 1)
            for k in range(KT):
                last = tr(ps[0:NS, k // 4, P * (k % 4):P * (k % 4) + P], ytile[:, k, 0:NS])
            last.then_inc(y_pe, 1)

        @block.vector
        def _(v):
            def on(*waits):
                for s, val in waits:
                    v.wait_ge(s, val)

            def norm_sq(it, k):
                if k == 0:
                    NRM_DVE.start()
                if k >= 2:
                    on((n_pe, NRM_PE.at(it, f"sum{k - 2}")))
                NRM_DVE.mark(v.tensor_tensor(nsq[:, k % 2, :], xT[:, k, :], xT[:, k, :], ALU.mult), n_dve, f"sq{k}")

            def norm(l, which, gain):
                it = 2 * l + which
                on((n_pe, NRM_PE.at(it, "rows")))
                for k in range(KT):
                    NRM_DVE.mark(v.scalar_tensor_tensor(hT[:, k, :].rearrange("p (a b) -> p a b", a=3), xT[:, k, :].rearrange("p (a b) -> p a b", a=3),
                                                        col(gain, k), ps[:, 3:6, 0:TB], ALU.mult, ALU.mult), n_dve, f"h{k}")

            v.memset(ones[:, :], 1.0).then_inc(one_done, 1)
            v.memset(share[:, :], 1.0 / 32).then_inc(one_done, 1)
            v.memset(cols_all[:, :, :], 0.0).then_inc(one_done, 1)
            v.sem_inc(evac[0], 1)
            v.sem_inc(evac[1], 1)
            v.sem_inc(xt_ev, 2)
            v.sem_inc(ko_free, 1)
            v.sem_inc(fp_act, 1)
            v.sem_inc(rw_act, 1)
            v.sem_inc(rt_dve, RT_DVE.first)
            v.sem_inc(fgr_pe, 5)
            v.wait_ge(one_done, 3)
            with v.Fori(0, NTT // 2) as t:
                for u in range(2):
                    v.wait_ge(xt_pe, t * 2 + u + 1)
                    v.tensor_copy(xT[:, :, bass.ds((t * 2 + u) * P, P)],
                                  ps[:, 4 * u:4 * u + 2, :].rearrange("p a (b c) -> p (a b) c", c=P)).then_inc(xt_ev, 1)
            v.wait_ge(xt_pe, NTT + 1)
            v.tensor_copy(xT[:, :, T:NT], ps[:, 0, 0:KT * NS].rearrange("p (a b) -> p a b", a=KT)).then_inc(xt_ev, 1)
            v.wait_ge(xt_ev, NTT + 3)

            def evac_tm(l, j, dst, n):
                v.wait_ge(gemm_done, l * PJOBS + j + 1)
                v.tensor_copy(dst[:, 0:NTT, P * n:P * n + P], job_psum_tm(j)[:, 0:NTT, :])
                v.tensor_copy(dst[0:NS, NTT, P * n:P * n + P], job_psum_tm(j)[0:NS, NTT, :]).then_inc(evac[j % 2], 1)

            def evac_rows(l, j):
                v.wait_ge(gemm_done, l * PJOBS + j + 1)
                s = 3 * (j % 2)
                v.tensor_copy(rp[:, j, 1:1 + 2 * TB].rearrange("p (a b) -> p a b", a=2), ps[:, s:s + 2, 0:TB])
                v.tensor_copy(rp[:, j, 1 + 2 * TB:1 + T], ps[:, s + 2, 0:T - 2 * TB])
                v.tensor_copy(rp[:, j, 1 + T:PW].rearrange("p (b t) -> p b t", t=TS + 1)[:, :, 1:],
                              ps[:, s + 2, T - 2 * TB:TB].rearrange("p (b t) -> p b t", t=TS)).then_inc(evac[j % 2], 1)

            for k in range(KT):
                norm_sq(0, k)
            with v.Fori(0, DEPTH) as l:
                v.wait_ge(cols_in, 16 * NCOLS_IN)
                v.tensor_copy(cols[:, :].unsqueeze(1), cols_all[:, bass.ds(l, 1), :]).then_inc(cols_ready, 1)
                v.wait_ge(cols_ready, l + 1)
                norm(l, 0, "ln_mix")
                pd = lambda n: (pr_dve, PR_DVE.at(l, n))
                pa = lambda n: (pr_act, PR_ACT.at(l, n))
                mark = PR_DVE.mark
                PR_DVE.start()
                on((n_dve, NRM_DVE.at(2 * l, "h7")))
                mark(v.memset(rp[:, :, 0], 0.0), pr_dve, "zero")
                mark(v.memset(cum[:, :, 0], 0.0), pr_dve, "cum0")
                mark(v.memset(st, 0.0), pr_dve, "st0")
                mark(v.tensor_scalar(kac, cols[:, COLS["ka"][0]:COLS["ka"][0] + 2], -1.0, 1.0, ALU.mult, ALU.add), pr_dve, "kac")
                for j in (0, 2, 4, 6):
                    evac_rows(l, j)
                on((shift_in, l * (7 * 16) + 7 * 16))
                for m in range(7):
                    on(evac_at(l, m))
                    mark(v.tensor_tensor(xs[:, m, :], rp[:, m, 0:XW], rp[:, m, 1:PW], ALU.subtract), pr_dve, f"diff{m}")
                for m in range(7):
                    on(pd(f"diff{m}"))
                    mark(v.scalar_tensor_tensor(xs[:, m, :], xs[:, m, :], col("mu", m), rp[:, m, 1:PW], ALU.mult, ALU.add), pr_dve, f"xs{m}")
                on((shift_out, l * (8 * 16) + 8 * 16), pd("xs6"))
                for m in range(2):
                    mark(v.tensor_scalar(kk_[:, m, :], xs[:, 2 + m, :], col("kk", m), None, ALU.mult), pr_dve, f"kk{m}")
                    on(pd(f"kk{m}"))
                    mark(v.tensor_tensor(sq1[m], kk_[:, m, :], kk_[:, m, :], ALU.mult), pr_dve, f"ksq{m}")
                for m in range(2):
                    on((pr_pe, PR_PE.at(l, f"ss{m}")))
                    mark(v.tensor_scalar(rn[m], ps[:, 4 * m:4 * m + 3, :].rearrange("p a b -> p (a b)")[:, 0:XW], 1e-24, None, ALU.max), pr_dve, f"kmax{m}")
                    mark(v.tensor_scalar(sq1[m], bv[:, m, :], col("ka", m), kac[:, m:m + 1], ALU.mult, ALU.add), pr_dve, f"kmul{m}")
                    on(pd(f"kmul{m}"))
                    mark(v.tensor_tensor(xs[:, 2 + m, :], xs[:, 2 + m, :], sq1[m], ALU.mult), pr_dve, f"k2{m}")
                for m in range(2):
                    on(pa(f"rn{m}"))
                    mark(v.tensor_tensor(kk_[:, m, :], kk_[:, m, :], rn[m], ALU.mult), pr_dve, f"kkn{m}")
                    on(pd(f"kkn{m}"))
                    mark(v.tensor_tensor(bv[:, m, :], bv[:, m, :], kk_[:, m, :], ALU.mult), pr_dve, f"bv{m}")
                on(pd("bv1"))
                v.sem_inc(passed, 1)

                rd = lambda it, n: (rp_dve, RP_DVE.at(it, n))

                def decays(it, c):
                    RP_DVE.start()
                    tk = bass.ds(c * P, P)
                    for m in range(2):
                        RP_DVE.mark(v.tensor_tensor_scan(cum[:, m, 1:P + 1], ones[:, :], sw[:, m, tk], 0.0, ALU.mult, ALU.add), rp_dve, f"cum{m}")
                    on(rd(it, "cum1"))
                    RP_DVE.mark(v.tensor_scalar(kpos, cum[:, :, 64], KAPPA, None, ALU.mult), rp_dve, "kp")
                    RP_DVE.mark(v.tensor_scalar(kneg, cum[:, :, 64], -KAPPA, None, ALU.mult), rp_dve, "kn")

                def keys(it, c):
                    tk = bass.ds(c * P, P)
                    on((rp_act, RP_ACT.at(it, "fm")))
                    RP_DVE.mark(v.tensor_tensor(bt, bv[:, :, tk], pinv, ALU.mult), rp_dve, "B")
                    RP_DVE.mark(v.tensor_tensor(kt_, xs[:, 2:4, tk], pinv, ALU.mult), rp_dve, "K")
                    RP_DVE.mark(v.tensor_tensor(rk2, xs[:, 0:2, tk], xs[:, 2:4, tk], ALU.mult), rp_dve, "rk2")

                def queries(it, c):
                    tk = bass.ds(c * P, P)
                    RP_DVE.mark(v.scalar_tensor_tensor(ar[:, :, 0, :], kk_[:, :, tk], -1.0, pe_[:, :, 0:P], ALU.mult, ALU.mult), rp_dve, "A")
                    RP_DVE.mark(v.tensor_tensor(ar[:, :, 1, :], xs[:, 0:2, tk], pe_[:, :, 1:P + 1], ALU.mult), rp_dve, "R")

                def middle(it):
                    RP_DVE.mark(v.tensor_copy(dend, pe_[:, :, P]), rp_dve, "dend")
                    for m in range(2):
                        RP_DVE.mark(v.tensor_scalar(stm[:, m, :], st[:, m, :], fmid[:, m:m + 1], None, ALU.mult), rp_dve, f"sm{m}")

                decays(l * (NTT + 1), 0)
                keys(l * (NTT + 1), 0)
                queries(l * (NTT + 1), 0)
                middle(l * (NTT + 1))
                with v.Fori(0, NTT) as c:
                    it = l * NTT + c
                    now = l * (NTT + 1) + c
                    RW_DVE.start()
                    dv = lambda n: (rw_dve, RW_DVE.at(it, n))
                    ac = lambda n: (rw_act, RW_ACT.at(it, n))
                    pp = lambda n: (rw_pe, RW_PE.at(it, n))
                    mk = lambda ins, n: RW_DVE.mark(ins, rw_dve, n)
                    four = lambda b: ps[:, b, :].rearrange("p (h t) -> p h t", h=4)
                    pair = lambda b, a: ps[:, b:b + 2, :].rearrange("p b (h a t) -> p (b h) a t", h=2, a=2)[:, :, a, :]
                    bc = lambda mask: mask.unsqueeze(1).to_broadcast((P, 4, P))
                    lab = ps[:, 4:6, 0:256].rearrange("p b (h t) -> p b h t", h=2)
                    bc2 = lambda mask: mask.unsqueeze(1).unsqueeze(1).to_broadcast((P, 2, 2, P))
                    sl2 = lambda i: sl[i].rearrange("p (b h) t -> p b h t", b=2)
                    on((rp_pe, RP_PE.at(now, "Lab")))
                    mk(v.tensor_tensor(sl[5], pair(0, 0), bc(m_dt), ALU.mult), "DT")
                    mk(v.tensor_tensor(sl[2], pair(0, 1), bc(m_ui), ALU.mult), "Lrb")
                    on((rp_pe, RP_PE.at(now, "L")))
                    mk(v.tensor_tensor(sl2(4), lab, bc2(m_d), ALU.mult), "D")
                    on(dv("DT"))
                    mk(v.tensor_tensor(sl[8], sl[5], bc(ident[:, :]), ALU.add), "Z1")
                    mk(v.tensor_tensor(sl2(0), lab, bc2(m_n), ALU.mult), "N")
                    on((rp_pe, RP_PE.at(now, "Lk")))
                    mk(v.tensor_tensor(sl[1], pair(2, 0), bc(m_u), ALU.mult), "Lak")
                    mk(v.tensor_tensor(sl[3], pair(2, 1), bc(m_ui), ALU.mult), "Lrk")
                    decays(now + 1, chunk(c + 1))
                    on(pp("Z2"), dv("Z1"))
                    mk(v.tensor_tensor(sl[8], four(4), sl[8], ALU.add), "Z2")
                    on(pp("D8"))
                    mk(v.tensor_copy(sl[6], four(0)), "D8")
                    on(pp("Z3"), dv("Z2"))
                    mk(v.tensor_tensor(sl[8], four(1), sl[8], ALU.add), "Z3")
                    on(pp("Z4"), dv("Z3"))
                    mk(v.tensor_tensor(sl[8], four(2), sl[8], ALU.add), "Z4")
                    on(pp("QT"))
                    mk(v.tensor_copy(sl[5], four(4)), "QT")
                    mk(v.tensor_tensor(sl[10], four(4), bc(ident[:, :]), ALU.add), "Y0")
                    on(pp("Q2T"))
                    mk(v.tensor_copy(sl[7], four(2)), "Q2T")
                    on(pp("Y1"), dv("Y0"))
                    mk(v.tensor_tensor(sl[10], four(4), sl[10], ALU.add), "Y1")
                    on(pp("Y2"), dv("Y1"))
                    mk(v.tensor_tensor(sl[10], four(0), sl[10], ALU.add), "Y2")
                    on(pp("X0"))
                    mk(v.tensor_copy(sl[4][:, 0:2, 0:HD], ps[:, 6, 0:P].rearrange("p (a d) -> p a d", a=2)), "X0a")
                    mk(v.tensor_copy(sl[4][:, 0:2, HD:P], ps[:, 5, P:2 * P].rearrange("p (a d) -> p a d", a=2)), "X0b")
                    keys(now + 1, chunk(c + 1))
                    on(pp("Y"))
                    queries(now + 1, chunk(c + 1))
                    on(pp("dS"))
                    mk(v.tensor_tensor(st, ps[:, 5, 0:P].rearrange("p (m k) -> p m k", m=2), stm, ALU.add), "s0")
                    on(dv("s0"))
                    for m in range(2):
                        mk(v.tensor_scalar(st[:, m, :], st[:, m, :], dend[:, m:m + 1], None, ALU.mult), f"sf{m}")
                    on(dv("sf1"))
                    middle(now + 1)
                    on(ac("Y"))
                    y4 = lambda h: sl[7][:, 1 - h % 2, HD * (h // 2):HD * (h // 2) + HD]
                    yn = sl[6][:, 0:2, :].rearrange("p a b -> p (a b)")
                    st4 = stats.rearrange("p (h s) -> p h s", h=RH)
                    for h in range(RH):
                        mk(v.bn_stats(st4[:, h, :], y4(h)), f"bn{h}")
                    on(dv("bn3"))
                    v.sem_inc(passed, 1)
                    for h in range(RH):
                        mk(v.bn_aggr(mv[:, 2 * h:2 * h + 2], st4[:, h, :]), f"ag{h}")
                    on(ac("rstd"), dv("ag3"))
                    for h in range(RH):
                        mk(v.tensor_scalar(yn[:, HD * h:HD * h + HD], y4(h), mv[:, 2 * h:2 * h + 1], rstd[:, h:h + 1], ALU.subtract, ALU.mult), f"yn{h}")
                    on(dv("yn3"))
                    mk(v.tensor_tensor(yn, yn, rows[:, 0, :], ALU.mult), "yw")
                    on(dv("yw"))
                    mk(v.tensor_tensor(yn, yn, rows[:, 1, :], ALU.add), "yb")
                    on(dv("yb"))
                    for h in range(RH):
                        y = yn[:, HD * h:HD * h + HD]
                        mk(v.scalar_tensor_tensor(y, vbk[:, h // 2, HD * (h % 2):HD * (h % 2) + HD], cbon[:, h:h + 1], y, ALU.mult, ALU.add), f"bo{h}")
                    on(dv("bo3"))
                    mk(v.tensor_tensor(yn, sl[7][:, 2:4, :].rearrange("p a b -> p (a b)"), yn, ALU.mult), "yg")
                on((rw_dve, RW_DVE.at(l * NTT + NTT - 1, "yg")), (rw_act, RW_ACT.at(l * NTT + NTT - 1, "ro")))

                RS_DVE.start()
                dv = lambda n: (rs_dve, RS_DVE.at(l, n))
                ac = lambda n: (rs_act, RS_ACT.at(l, n))
                pp = lambda n: (rs_pe, RS_PE.at(l, n))
                mk = lambda ins, n: RS_DVE.mark(ins, rs_dve, n)
                SR = slice(0, NS)
                tok = lambda t, m: t[:, m, T:XW].rearrange("p (b t) -> p b t", t=TS + 1)[:, :, 1:]
                tok2 = lambda t, m0: t[:, m0:m0 + 2, T:XW].rearrange("p m (b t) -> p m b t", t=TS + 1)[:, :, :, 1:]
                bt4 = lambda t: t.rearrange("p m (b t) -> p m b t", t=TS)
                mk(v.memset(cum5[:, :, :, 0], 0.0), "zero")
                mk(v.tensor_copy(cum5[:, :, :, 1:], tok2(sw, 0)), "cum0")
                for i in range(2, TS + 1):
                    on(dv(f"cum{i - 2}"))
                    mk(v.tensor_tensor(cum5[:, :, :, i], cum5[:, :, :, i], cum5[:, :, :, i - 1], ALU.add), f"cum{i - 1}")
                on(ac("pi5"))
                for m in range(2):
                    mk(v.scalar_tensor_tensor(ars[:, m, 0, :].rearrange("p (b t) -> p b t", t=TS), tok(kk_, m), -1.0, e5[:, m, :, 0:TS], ALU.mult, ALU.mult), f"A{m}")
                mk(v.tensor_tensor(bt4(ars[:, :, 1, :]), tok2(xs, 0), e5[:, :, :, 1:], ALU.mult), "R")
                mk(v.tensor_tensor(bt4(bts), tok2(bv, 0), pi5[:, :, :, 1:], ALU.mult), "B")
                mk(v.tensor_tensor(bt4(kts), tok2(xs, 2), pi5[:, :, :, 1:], ALU.mult), "K")
                mk(v.tensor_tensor(bt4(rk2s), tok2(xs, 0), tok2(xs, 2), ALU.mult), "rk2")
                mk(v.tensor_copy(bt4(vss), tok2(xs, 4)), "vs")
                mk(v.tensor_copy(sgs[64:P].rearrange("p (b t) -> p b t", t=TS), tok(xs, 6)[64:P]), "sg")
                on(dv("R"))
                for n, dst, i in (("aex", aex, 0), ("rex", rex, 1)):
                    mk(v.tensor_tensor(dst, ars[:, :, i, :].unsqueeze(2).to_broadcast((P, 2, DB, NS)), s_col.unsqueeze(1).to_broadcast((P, 2, DB, NS)), ALU.mult), n)
                on(pp("st"))
                mk(v.tensor_copy(sts.rearrange("p m b d -> p m (b d)"), ps[:, 0:2, :]), "sts")
                on(pp("L"))
                lab = ps[SR, 4:6, 0:2 * NS].rearrange("p b (h t) -> p b h t", h=2)
                spair = lambda b, i: ps[SR, b:b + 2, 0:4 * NS].rearrange("p b (h a t) -> p b h a t", h=2, a=2)[:, :, :, i, :]
                sm2 = lambda i: smat[i][SR].rearrange("p (b h) t -> p b h t", b=2)
                sbc = lambda t: t[SR].unsqueeze(1).unsqueeze(1).to_broadcast((NS, 2, 2, NS))
                mk(v.tensor_tensor(sm2(0), lab, sbc(s_l), ALU.mult), "D")
                mk(v.tensor_tensor(sm2(1), spair(0, 0), sbc(s_lt), ALU.mult), "DT")
                on(dv("DT"))
                mk(v.tensor_tensor(smat[3][SR], smat[1][SR], ident[SR, SR].unsqueeze(1).to_broadcast((NS, RH, NS)), ALU.add), "Z1")
                mk(v.tensor_tensor(sm2(4), spair(0, 1), sbc(s_ui), ALU.mult), "Lrb")
                mk(v.tensor_tensor(sm2(5), spair(2, 0), sbc(s_u), ALU.mult), "Lak")
                mk(v.tensor_tensor(sm2(6), spair(2, 1), sbc(s_ui), ALU.mult), "Lrk")
                on(pp("Z2"), dv("Z1"))
                mk(v.tensor_tensor(smat[3][SR], ps[SR, 1, 0:P].rearrange("p (h t) -> p h t", h=RH), smat[3][SR], ALU.add), "Z2")
                on(pp("X0"))
                mk(v.tensor_copy(x0s[SR].rearrange("p (a b d) -> p b a d", a=2, b=2), ps[SR, 2:4, 0:P].rearrange("p b (a d) -> p b a d", a=2)), "X0")
                on(ac("U"))
                rowm = s_row[SR].unsqueeze(2).to_broadcast((NS, DB, HD))
                for h in range(RH):
                    mk(v.tensor_tensor(uex[SR, h], us[SR, HD * h:HD * h + HD].unsqueeze(1).to_broadcast((NS, DB, HD)), rowm, ALU.mult), f"uex{h}")
                for h in range(RH):
                    mk(v.tensor_tensor(vex[SR, h], vbks[SR, h // 2, HD * (h % 2):HD * (h % 2) + HD].unsqueeze(1).to_broadcast((NS, DB, HD)), rowm, ALU.mult), f"vex{h}")
                on(pp("dS"))
                mk(v.tensor_tensor(sts.rearrange("p m b d -> p m (b d)"), ps[:, 0:2, :], sts.rearrange("p m b d -> p m (b d)"), ALU.add), "s0")
                on(dv("s0"))
                mk(v.tensor_tensor(sts, sts, e5[:, :, :, TS].unsqueeze(3).to_broadcast((P, 2, DB, HD)), ALU.mult), "sf")
                y4 = lambda h: ps[SR, 4 - h % 2, HD * (h // 2):HD * (h // 2) + HD]
                for h in range(RH):
                    mk(v.bn_stats(stats[SR, 6 * h:6 * h + 6], y4(h)), f"bn{h}")
                on(dv("bn3"))
                v.sem_inc(passed, 1)
                for h in range(RH):
                    mk(v.bn_aggr(mv[SR, 2 * h:2 * h + 2], stats[SR, 6 * h:6 * h + 6]), f"ag{h}")
                on(ac("rstd"), dv("ag3"))
                for h in range(RH):
                    mk(v.tensor_scalar(yns[SR, HD * h:HD * h + HD], y4(h), mv[SR, 2 * h:2 * h + 1], rstd[SR, h:h + 1], ALU.subtract, ALU.mult), f"yn{h}")
                on(dv("yn3"))
                mk(v.tensor_tensor(yns[SR], yns[SR], rows[SR, 0, :], ALU.mult), "yw")
                on(dv("yw"))
                mk(v.tensor_tensor(yns[SR], yns[SR], rows[SR, 1, :], ALU.add), "yb")
                on(dv("yb"))
                for h in range(RH):
                    y = yns[SR, HD * h:HD * h + HD]
                    mk(v.scalar_tensor_tensor(y, vbks[SR, h // 2, HD * (h % 2):HD * (h % 2) + HD], cbon[SR, h:h + 1], y, ALU.mult, ALU.add), f"bo{h}")
                on(dv("bo3"))
                mk(v.tensor_tensor(yns[SR], ps[SR, 7, 0:RW], yns[SR], ALU.mult), "yg")

                for j in (J_EQ, J_EQ + 2):
                    on((gemm_done, l * PJOBS + j + 1))
                    v.tensor_copy(eqk[:, j - J_EQ, :].rearrange("p (a b) -> p a b", a=3), job_psum(j)).then_inc(evac[0], 1)
                evac_tm(l, J_EV, evg, 0)
                RE_DVE.start()
                on((re_in, l * 80 + 80))
                mk = lambda ins, n: RE_DVE.mark(ins, re_dve, n)
                dv = lambda n: (re_dve, RE_DVE.at(l, n))
                pp = lambda n: (re_pe, RE_PE.at(l, n))
                mk(v.memset(rst, 0.0), "R")
                for i in range(4):
                    scale = 1.0 if i < 2 else HD ** -0.5
                    x = eqk[:, i, :]
                    on(pp(f"rot{i}"), evac_at(l, J_EQ + i))
                    mk(v.scalar_tensor_tensor(x, x, scale, cos_t, ALU.mult, ALU.mult), f"xc{i}")
                    if i:
                        on(dv(f"add{i - 1}"))
                    mk(v.scalar_tensor_tensor(ropet.rearrange("p (a b) -> p a b", a=3), ps[:, 3 * (i % 2):3 * (i % 2) + 3, 0:TB], scale,
                                              sin_t.rearrange("p (a b) -> p a b", a=3), ALU.mult, ALU.mult), f"ts{i}")
                    on(dv(f"ts{i}"))
                    mk(v.tensor_tensor(x, x, ropet, ALU.add), f"add{i}")

                def ret_norm(mk, dv, ac, R, y4, gate, out):
                    for h in range(EH):
                        mk(v.bn_stats(stats[R, 6 * h:6 * h + 6], y4(h)), f"bn{h}")
                    on(dv("bn3"))
                    v.sem_inc(passed, 1)
                    for h in range(EH):
                        mk(v.bn_aggr(mv[R, 2 * h:2 * h + 2], stats[R, 6 * h:6 * h + 6]), f"ag{h}")
                    on(ac("rstd"), dv("ag3"))
                    for h in range(EH):
                        mk(v.tensor_scalar(yne[R, HD * h:HD * h + HD], y4(h), mv[R, 2 * h:2 * h + 1], rstd[R, h:h + 1], ALU.subtract, ALU.mult), f"yn{h}")
                    on(dv("yn3"))
                    mk(v.tensor_tensor(yne[R], yne[R], rows[R, 2, :], ALU.mult), "yw")
                    on(dv("yw"))
                    mk(v.tensor_tensor(out, yne[R], gate, ALU.mult), "yg")

                on(evac_at(l, J_EV + 1), evac_at(l, J_EV + 3))
                v.sem_inc(passed, 1)

                def ret_scores(it):
                    RQ_DVE.start()
                    on((rq_pe, RQ_PE.at(it, "S")))
                    RQ_DVE.mark(v.tensor_tensor(stt.rearrange("p (b a) t -> p b a t", b=2), ps[:, 0:2, 0:2 * P].rearrange("p b (a t) -> p b a t", a=2), dmask, ALU.mult), rq_dve, "st")
                    on((rq_pe, RQ_PE.at(it, "kt")))
                    RQ_DVE.mark(v.tensor_tensor(kd, ps[:, 2, 0:EW].rearrange("p (h d) -> p h d", h=EH), inner.unsqueeze(2).to_broadcast((P, EH, HD)), ALU.mult), rq_dve, "kd")

                ret_scores(l * (NTT + 1))
                with v.Fori(0, NTT) as c:
                    it = l * NTT + c
                    RT_DVE.start()
                    mkt = lambda ins, n: RT_DVE.mark(ins, rt_dve, n)
                    dvt = lambda n: (rt_dve, RT_DVE.at(it, n))
                    act_ = lambda n: (rt_act, RT_ACT.at(it, n))
                    on((rt_pe, RT_PE.at(it, "dR")))
                    v.sem_inc(passed, 1)
                    for m in range(2):
                        mkt(v.scalar_tensor_tensor(rst[:, m, :], rst[:, m, :], gam[:, m:m + 1], ps[:, 5, HD * m:HD * m + HD], ALU.mult, ALU.add), f"R{m}")
                    on(act_("Y"))
                    ret_scores(l * (NTT + 1) + c + 1)
                    gate = evg[:, bass.ds(c, 1), EW:2 * EW].rearrange("p a e -> p (a e)")
                    ret_norm(mkt, dvt, act_, slice(0, P), lambda h: yce[:, 1 - h % 2, HD * (h // 2):HD * (h // 2) + HD], gate, gate)
                ac = lambda n: (re_act, RE_ACT.at(l, n))
                mk(v.tensor_tensor(qds, eqk[:, 0:2, T:NT], s_cross, ALU.mult), "qd")
                on(dv("qd"))
                mk(v.tensor_tensor(qex, qds.unsqueeze(2).to_broadcast((P, 2, DB, NS)), s_col.unsqueeze(1).to_broadcast((P, 2, DB, NS)), ALU.mult), "qex")
                on(pp("S"))
                mk(v.tensor_tensor(stts[SR].rearrange("p (b a) t -> p b a t", b=2), ps[SR, 0:2, 0:2 * NS].rearrange("p b (a t) -> p b a t", a=2), s_dmask[SR], ALU.mult), "st")
                on(pp("kt"))
                mk(v.tensor_tensor(kds[SR], ps[SR, 2, 0:EW].rearrange("p (h d) -> p h d", h=EH), s_inner[SR].unsqueeze(2).to_broadcast((NS, EH, HD)), ALU.mult), "kd")
                for h in range(EH):
                    mk(v.tensor_tensor(vexe[SR, h], evg[SR, NTT, HD * h:HD * h + HD].unsqueeze(1).to_broadcast((NS, DB, HD)),
                                       s_row[SR].unsqueeze(2).to_broadcast((NS, DB, HD)), ALU.mult), f"vex{h}")
                on(pp("dR"))
                for m in range(2):
                    rm = rss[:, m].rearrange("p b e -> p (b e)")
                    mk(v.scalar_tensor_tensor(rm, rm, s_gam[:, m:m + 1], ps[:, m, :], ALU.mult, ALU.add), f"R{m}")
                ret_norm(mk, dv, ac, SR, lambda h: ps[SR, 4 - h % 2, HD * (h // 2):HD * (h // 2) + HD], evg[SR, NTT, EW:2 * EW], yne[SR])
                on(dv("yg"), (re_out, l * 48 + 48), (re_act, RE_ACT.at(l, "ro")), (rs_out, l * 16 + 16), (ro_out, l * 16 + 16))
                fr = slice(0, FH)
                FG_DVE.start()
                on(evac_at(l, J_EQ - 1))
                fgm = lambda ins, n: FG_DVE.mark(ins, fg_dve, n)
                fgd = lambda n: (fg_dve, FG_DVE.at(l, n))
                fgm(v.tensor_scalar(fl[fr], fl[fr], col("fb", 0, fr), None, ALU.add), "z")
                on(fgd("z"))
                fgm(v.scalar_tensor_tensor(fz, fl[fr], -1.0, fl[fr], ALU.mult, ALU.max), "abs")
                on((fg_act, FG_ACT.at(l, "ln")))
                fgm(v.scalar_tensor_tensor(fl[fr], fl[fr], 0.0, fe, ALU.min, ALU.subtract), "logf")
                on(fgd("logf"))
                fgm(v.tensor_tensor_scan(ncr, ones[fr, 0:1].to_broadcast((FH, T)), fl[fr, 0:T], 0.0, ALU.mult, ALU.subtract), "nc")
                for j in range(J_FQ, J_FV, 2):
                    on((gemm_done, l * PJOBS + j + 1))
                    v.tensor_copy(fqk[:, j - J_FQ, :].rearrange("p (a b) -> p a b", a=3), job_psum(j)).then_inc(evac[0], 1)
                for j in range(J_FV, J_OUT, 2):
                    evac_tm(l, j, fv, j - J_FV)
                FG_DVE.mark(v.tensor_scalar(gq8, col("qn"), HD ** -0.5, None, ALU.mult), fg_dve, "gq")
                on(evac_at(l, J_OUT - 1), evac_at(l, J_FV - 1), (fg_dve, FG_DVE.at(l, "gq")))
                v.sem_inc(passed, 1)
                with v.Fori(0, 4) as i:
                    it = l * 4 + i
                    FN_DVE.start()
                    for u in range(2):
                        x = fqk[:, bass.ds(i + 4 * u, 1), :].rearrange("p a t -> p (a t)")
                        FN_DVE.mark(v.tensor_tensor(fsq[:, u, :], x, x, ALU.mult), fn_dve, f"sq{u}")
                    for u in range(2):
                        x = fqk[:, bass.ds(i + 4 * u, 1), :].rearrange("p a t -> p (a t)")
                        v.wait_ge(fn_act, FN_ACT.at(it, f"rs{u}"))
                        FN_DVE.mark(v.scalar_tensor_tensor(x, x, gq8 if u == 0 else col("kn"), frs[:, u, :], ALU.mult, ALU.mult), fn_dve, f"n{u}")
                fgm = lambda ins, n: FG_DVE.mark(ins, fg_dve, n)
                on((fn_dve, FN_DVE.at(l * 4 + 3, "n1")))
                fgm(v.tensor_copy(qtp[0], fqk[:, 0, :]), "q0")
                fgm(v.tensor_copy(ktp[0], fqk[:, 4, :]), "k0")
                fgm(v.tensor_copy(qn, fqk[:, 0:4, T:NT]), "q")
                fgm(v.tensor_copy(kn, fqk[:, 4:8, T:NT]), "kn")
                fgm(v.tensor_copy(vn[SR], fv[SR, NTT, :]), "vn")
                with v.Fori(0, 2) as pp:
                    it = l * 2 + pp
                    FP_DVE.start()
                    fm = lambda ins, n: FP_DVE.mark(ins, fp_dve, n)
                    fd = lambda n: (fp_dve, FP_DVE.at(it, n))
                    fa = lambda n: (fp_act, FP_ACT.at(it, n))
                    fpp = lambda n: (fp_pe, FP_PE.at(it, n))

                    def soft(u, s):
                        i, hh = s // 2, s % 2
                        w = P * (i + 1)
                        on(fpp(f"{u}S{s}"))
                        v.sem_inc(passed, 1)
                        fm(v.tensor_tensor_reduce(sp_[:, hh, 0:w], ps[:, 2 * hh:2 * hh + 2, :].rearrange("p a b -> p (a b)")[:, 0:w],
                                                  ncb[u][:, hh, 0:w], 1.0, -3.0e38, ALU.add, ALU.max, mx[:, s:s + 1]), f"{u}d{s}")
                        on(fd(f"{u}d{s}"))
                        fm(v.tensor_scalar(nmx[:, s:s + 1], mx[:, s:s + 1], -1.0, None, ALU.mult), f"{u}n{s}")

                    def out_(u, s):
                        i, hh = s // 2, s % 2
                        if s % 2:
                            on(fpp(f"{u}T{s}"))
                            fm(v.tensor_copy(ptt[:, hh, 0:i + 1, :], ps[:, 4:6, :].rearrange("p a (b c) -> p (a b) c", c=P)[:, 0:i + 1, :]), f"{u}pt{s}")
                        on(fa(f"{u}e{s}"))
                        fm(v.reciprocal(rrec[:, s:s + 1], rsum[:, s:s + 1]), f"{u}r{s}")
                        on(fd(f"{u}r{s}"), fpp(f"{u}V{s}"))
                        fm(v.tensor_scalar(otok[:, i, HD * hh:HD * hh + HD], ps[:, 6 + hh, HD * hh:HD * hh + HD], rrec[:, s:s + 1], None, ALU.mult), f"{u}o{s}")

                    for u in range(2):
                        on((fp_ncb[u], it * 16 + 16))
                        soft(u, 0)
                        for s in SC:
                            if ahead(s):
                                soft(u, s + 1)
                            out_(u, s)
                fsm_ = lambda ins, n: FS_DVE.mark(ins, fs_dve, n)
                fsd = lambda n: (fs_dve, FS_DVE.at(l, n))
                FS_DVE.start()
                on((fp_act, FP_ACT.at(l * 2 + 1, "1oT")))
                fsm_(v.memset(qb, 0.0), "qz")
                on(fsd("qz"))
                for p in range(4):
                    for k in range(2):
                        r = slice(HD * k, HD * k + HD)
                        c = 8 * p + 4 * k
                        fsm_(v.tensor_copy(qb[r, :, p, c:c + TS], qn[r, p, :].rearrange("p (b t) -> p b t", t=TS)), f"q{p}{k}")
                R64 = slice(0, DB * FH)
                on((fs_pe, l + 1), (past_in, l * NPAST + NPAST))
                fsm_(v.tensor_copy(lfs[R64, 0:NP], ps[R64, 0:2, :].rearrange("p a b -> p (a b)")), "lfs")
                fsm_(v.tensor_copy(lfs[R64, NP:NP + TS], lfnew[R64, :]), "lfn")
                on(fsd("lfn"))
                fsm_(v.tensor_tensor_scan(ncs[R64], ones[R64, 0:1].to_broadcast((DB * FH, NP + TS)), lfs[R64], 0.0, ALU.mult, ALU.subtract), "ncs")
                on(fsd("ncs"), (fox_const, l * 64 + 64))
                v.sem_inc(passed, 1)
                with v.Fori(0, 2) as g:
                    it = l * 2 + g
                    G_DVE.start()
                    gm = lambda ins, n: G_DVE.mark(ins, fgr_dve, n)
                    gd = lambda n: (fgr_dve, G_DVE.at(it, n))
                    ga = lambda n: (fgr_act, G_ACT.at(it, n))
                    gp = lambda n: (fgr_pe, G_PE.at(it, n))
                    gm(v.tensor_copy(cur_q, qb[:, bass.ds(g * 4, 4), :, :]), "cq")
                    gm(v.tensor_copy(cur_k, kn[:, :, bass.ds(g * 16, 16)]), "ck")
                    gm(v.tensor_copy(cur_sel[R64], ssel[R64, bass.ds(g, 1), :].rearrange("p a b -> p (a b)")), "csel")
                    gm(v.tensor_copy(cur_req, sreq[:, bass.ds(g, 1), :].rearrange("p a b -> p (a b)")), "creq")
                    for b in range(4):
                        for p in (1, 3):
                            on(gp(f"T{b}{p}"))
                            if b or p == 3:
                                on(gp(f"S{b}1") if p == 3 else gp(f"S{b - 1}3"))
                            gm(v.tensor_copy(keyt[1], ps[:, 5:7, :].rearrange("p a b -> p (a b)")), f"kt{b}{p}")
                    on(gp("S33"))
                    past = ps[:, 0:2, :].rearrange("p a b -> p (a b)")
                    gm(v.tensor_tensor(smn, ps[:, 2, 0:TS], sfm, ALU.add), "sn")
                    gm(v.tensor_reduce(fsm[:, 0:1], past, AX.X, ALU.max), "mx")
                    on(gd("sn"))
                    gm(v.tensor_reduce(fsm[:, 1:2], smn, AX.X, ALU.max), "mn")
                    on(gd("mn"))
                    gm(v.tensor_tensor(fsm[:, 2:3], fsm[:, 0:1], fsm[:, 1:2], ALU.max), "max")
                    on(gd("max"))
                    gm(v.tensor_scalar(fsm[:, 3:4], fsm[:, 2:3], -1.0, None, ALU.mult), "neg")
                    on(ga("en"))
                    gm(v.tensor_tensor(fsm[:, 6:7], fsm[:, 4:5], fsm[:, 5:6], ALU.add), "sum")
                    on(gd("sum"))
                    gm(v.reciprocal(fsm[:, 7:8], fsm[:, 6:7]), "rec")
                    on(gd("rec"))
                    gm(v.tensor_scalar(pss, pss, fsm[:, 7:8], None, ALU.mult), "pn")
                    on(gd("pn"))
                    gm(v.tensor_tensor(pn, pss[:, NP:NP + TS].unsqueeze(1).to_broadcast((P, DB, TS)), cur_req.unsqueeze(2).to_broadcast((P, DB, TS)), ALU.mult), "pne")
                    on(gp("P1"))
                    gm(v.tensor_copy(pts[:, 4:8, :], ps[:, 4, :].rearrange("p (j r) -> p j r", j=4)), "pt1")
                    on(gp("Pn"))
                    gm(v.tensor_copy(pnt[SR], ps[SR, 5, 0:P]), "pnt")
                    on(gp("V3"))
                    gm(v.tensor_tensor(om.rearrange("p (h d) -> p h d", h=FH), ps[:, 7, :].rearrange("p (h d) -> p h d", h=FH),
                                       shead.unsqueeze(2).to_broadcast((P, FH, HD)), ALU.mult), "om")
                    on(gp("F"))
                    gm(v.tensor_copy(hT[:, 0:4, bass.ds(g * 16 + T, 16)], ps[:, 5, 0:64].rearrange("p (m c) -> p m c", m=4)), "o")
                on((fgr_dve, G_DVE.at(l * 2 + 1, "o")), (fox_out2, l * 16 + 16), (lft_out, l * 32 + 32))
                for j in range(J_OUT, J_FF):
                    on((gemm_done, l * PJOBS + j + 1))
                    xk = xT[:, j - J_OUT, :].rearrange("p (a b) -> p a b", a=3)
                    v.tensor_tensor(xk, job_psum(j), xk, ALU.add).then_inc(evac[j % 2], 1)
                    on(evac_at(l, j))
                    norm_sq(2 * l + 1, j - J_OUT)
                norm(l, 1, "ln_ffn")
                with v.Fori(0, FT // 2) as q:
                    for u in range(2):
                        v.wait_ge(evac[0], l * HALF + q * 2 + ((J_FF + 2 * u) // 2 + 2))
                        v.wait_ge(gemm_done, l * PJOBS + q * RING + (J_FF + 2 * u + 2))
                        v.tensor_tensor(big[:, bass.ds((q * 2 + u) * NT, NT)].rearrange("p (a b) -> p a b", a=3), job_psum(1),
                                        sil[:, u * NT:(u + 1) * NT].rearrange("p (a b) -> p a b", a=3), ALU.mult).then_inc(evac[1], 1)
                for j in range(KT):
                    on((gemm_done, l * PJOBS + J_DOWN + j + 1))
                    xk = xT[:, j, :].rearrange("p (a b) -> p a b", a=3)
                    v.tensor_tensor(xk, job_psum(j), xk, ALU.add).then_inc(evac[j % 2], 1)
                    on((evac[j % 2], l * HALF + ((J_DOWN + j) // 2 + 2)))
                    norm_sq(2 * l + 2, j)
                v.wait_ge(evac[0], l * HALF + HALF + 1)
                v.wait_ge(evac[1], l * HALF + HALF + 1)
            v.tensor_copy(ytile, xT[:, :, 0:P]).then_inc(y_st, 1)
            with v.Fori(1, NTT) as t:
                v.wait_ge(y_pe, t)
                v.tensor_copy(ytile, xT[:, :, bass.ds(t * P, P)]).then_inc(y_st, 1)
            v.wait_ge(y_pe, NTT)
            v.tensor_copy(ytile[:, :, 0:NS], xT[:, :, T:NT]).then_inc(y_st, 1)

        @block.scalar
        def _(a):
            def on(*waits):
                for s, val in waits:
                    a.wait_ge(s, val)

            act = a.activation

            def log_exp():
                a.preload_act_table_set("natural_log_exp_and_others")

            def evac_tm(l, j, dst, n, func=ACT.Copy):
                a.wait_ge(gemm_done, l * PJOBS + j + 1)
                act(dst[:, 0:NTT, P * n:P * n + P], job_psum_tm(j)[:, 0:NTT, :], func)
                act(dst[0:NS, NTT, P * n:P * n + P], job_psum_tm(j)[0:NS, NTT, :], func).then_inc(evac[j % 2], 1)

            def norm(l, which):
                it = 2 * l + which
                NRM_ACT.start()
                on((n_pe, NRM_PE.at(it, "sum7")))
                NRM_ACT.mark(act(nrs, ps[0:96, 6, 0:TB], ACT.Ln, scale=1.0 / D, bias=EPS), n_act, "ln")
                on((n_act, NRM_ACT.at(it, "ln")))
                NRM_ACT.mark(act(nrs, nrs, ACT.Exp, scale=-0.5), n_act, "rstd")

            with a.Fori(0, DEPTH) as l:
                norm(l, 0)
                for j in (1, 3, 5):
                    on((gemm_done, l * PJOBS + j + 1))
                    s = 3 * (j % 2)
                    a.copy(rp[:, j, 1:1 + 2 * TB].rearrange("p (a b) -> p a b", a=2), ps[:, s:s + 2, 0:TB])
                    a.copy(rp[:, j, 1 + 2 * TB:1 + T], ps[:, s + 2, 0:T - 2 * TB])
                    a.copy(rp[:, j, 1 + T:PW].rearrange("p (b t) -> p b t", t=TS + 1)[:, :, 1:],
                           ps[:, s + 2, T - 2 * TB:TB].rearrange("p (b t) -> p b t", t=TS)).then_inc(evac[j % 2], 1)
                on((gemm_done, l * PJOBS + 7 + 1))
                a.copy(fl.rearrange("p (a b) -> p a b", a=3), job_psum(7)).then_inc(evac[1], 1)
                pd = lambda n: (pr_dve, PR_DVE.at(l, n))
                pa = lambda n: (pr_act, PR_ACT.at(l, n))
                mark = PR_ACT.mark
                PR_ACT.start()
                on(pd("xs6"))
                mark(act(xs[0:32, 6, :], xs[0:32, 6, :], ACT.Tanh), pr_act, "tanh")
                mark(act(xs[64:P, 6, :], xs[64:P, 6, :], ACT.Sigmoid), pr_act, "sg")
                on((shift_out, l * (8 * 16) + 8 * 16))
                for m in range(2):
                    for s, (n, dst, b0) in enumerate((("w", sw, "w0"), ("a", bv, "a0"))):
                        on((pr_pe, PR_PE.at(l, f"{n}{m}")))
                        mark(act(dst[:, m, :], ps[:, 4 * s:4 * s + 3, :].rearrange("p a b -> p (a b)")[:, 0:XW], ACT.Sigmoid, bias=col(b0, m)),
                             pr_act, f"{'sw' if s == 0 else 'a'}{m}")
                for m in range(2):
                    on(pd(f"kmax{m}"))
                    mark(act(rn[m], rn[m], ACT.Ln, scale=2.0 ** 30), pr_act, f"ln{m}")
                    on(pa(f"ln{m}"))
                    mark(act(rn[m], rn[m], ACT.Exp, scale=-0.5, bias=15 * 0.6931471805599453), pr_act, f"rn{m}")

                def decays(it):
                    RP_ACT.start()
                    on((rp_dve, RP_DVE.at(it, "kn")))
                    for m in range(2):
                        RP_ACT.mark(act(pe_[:, m, :], cum[:, m, :], ACT.Exp, scale=-KAPPA, bias=kpos[:, m:m + 1]), rp_act, f"e{m}")
                    for m in range(2):
                        RP_ACT.mark(act(pinv[:, m, :], cum[:, m, 1:], ACT.Exp, scale=KAPPA, bias=kneg[:, m:m + 1]), rp_act, f"pi{m}")
                    RP_ACT.mark(act(fmid, kneg, ACT.Exp), rp_act, "fm")

                def tokens(it):
                    RV_ACT.start()
                    on((rp_pe, RP_PE.at(it, "tr")))
                    RV_ACT.mark(a.copy(region((sil, 0), 6 * P), ps[:, 6:8, :].rearrange("p a b -> p (a b)")[:, 0:6 * P]), rv_act, "vbk")
                    RV_ACT.mark(a.copy(cbon, ps[:, 7, 256:260]), rv_act, "bon")

                log_exp()
                decays(l * (NTT + 1))
                tokens(l * (NTT + 1))
                with a.Fori(0, NTT) as c:
                    it = l * NTT + c
                    now = l * (NTT + 1) + c
                    RW_ACT.start()
                    log_exp()
                    dv = lambda n: (rw_dve, RW_DVE.at(it, n))
                    ac = lambda n: (rw_act, RW_ACT.at(it, n))
                    pp = lambda n: (rw_pe, RW_PE.at(it, n))
                    mk = lambda ins, n: RW_ACT.mark(ins, rw_act, n)
                    four = lambda b: ps[:, b, :].rearrange("p (h t) -> p h t", h=4)
                    for n, b, s in (("D2", 0, 6), ("D2T", 1, 7), ("D4", 2, 4), ("D4T", 3, 5), ("Q", 3, 4), ("M", 0, 9), ("Q2", 1, 6), ("Q4", 3, 4), ("TT", 1, 8)):
                        on(pp(n))
                        mk(a.copy(sl[s], four(b)), n)
                        if n == "D4T":
                            decays(now + 1)
                    on(pp("g"))
                    mk(a.copy(sl[7][:, 2:4, :].rearrange("p a b -> p (a b)"), ps[:, 7, 0:RW]), "g")
                    on(pp("U"))
                    mk(a.copy(sl[5][:, 0:2, :].rearrange("p a b -> p (a b)"), ps[:, 2, 0:RW]), "U")
                    on(pp("Y"))
                    mk(a.copy(sl[7][:, 0:2, :], ps[:, 3:5, 0:P]), "Y")
                    on(dv("ag3"))
                    mk(act(rstd, mv.rearrange("p (h s) -> p h s", s=2)[:, :, 1], ACT.Ln, bias=RWKV_EPS), "ln")
                    on(ac("ln"))
                    mk(act(rstd, rstd, ACT.Exp, scale=-0.5), "rstd")
                    on(dv("bo3"))
                    tokens(now + 1)
                    on(pp("ro"))
                    mk(a.copy(mixB[:, 0:2, bass.ds(c * P, P)], ps[:, 6, 0:2 * P].rearrange("p (m t) -> p m t", m=2)), "ro")
                on((ro_pe, l + 1))
                a.copy(sl[9][0:HD, 0:2, :], ps[0:HD, 0, 0:2 * P].rearrange("p (m t) -> p m t", m=2)).then_inc(ro_act, 1)
                RS_ACT.start()
                log_exp()
                dv = lambda n: (rs_dve, RS_DVE.at(l, n))
                ac = lambda n: (rs_act, RS_ACT.at(l, n))
                pp = lambda n: (rs_pe, RS_PE.at(l, n))
                mk = lambda ins, n: RS_ACT.mark(ins, rs_act, n)
                SR = slice(0, NS)
                on(dv("cum3"))
                mk(act(e5, cum5, ACT.Exp, scale=-KAPPA), "e5")
                mk(act(pi5, cum5, ACT.Exp, scale=KAPPA), "pi5")
                on(pp("tr"))
                mk(a.copy(region((sil, 0), 6 * P)[SR], ps[SR, 6:8, :].rearrange("p a b -> p (a b)")[:, 0:6 * P]), "vbk")
                mk(a.copy(cbon[SR], ps[SR, 7, 256:260]), "bon")
                on(pp("D2"))
                mk(a.copy(smat[2][SR], ps[SR, 0, 0:P].rearrange("p (h t) -> p h t", h=RH)), "D2")
                on(pp("U"))
                mk(a.copy(us[SR], ps[SR, 6, 0:RW]), "U")
                on(dv("ag3"))
                mk(act(rstd[SR], mv[SR].rearrange("p (h s) -> p h s", s=2)[:, :, 1], ACT.Ln, bias=RWKV_EPS), "ln")
                on(ac("ln"))
                mk(act(rstd[SR], rstd[SR], ACT.Exp, scale=-0.5), "rstd")
                on(pp("ro"))
                mk(a.copy(mixB[:, 0:2, T:NT], ps[:, 6, 0:2 * NS].rearrange("p (m t) -> p m t", m=2)), "ro")
                on(pp("nat"))
                mk(a.copy(nat_out[0:HD].rearrange("v b (m k) -> v m b k", m=2), ps[0:HD, 0:4, :].rearrange("v (m c) (b k) -> v m (c b) k", m=2, k=P)), "nat")

                for j in (J_EQ + 1, J_EQ + 3):
                    on((gemm_done, l * PJOBS + j + 1))
                    a.copy(eqk[:, j - J_EQ, :].rearrange("p (a b) -> p a b", a=3), job_psum(j)).then_inc(evac[1], 1)
                evac_tm(l, J_EV + 1, evg, 1)
                evac_tm(l, J_EV + 2, evg, 2, ACT.Silu)
                evac_tm(l, J_EV + 3, evg, 3, ACT.Silu)
                with a.Fori(0, NTT) as c:
                    it = l * NTT + c
                    RT_ACT.start()
                    log_exp()
                    a.wait_ge(rt_pe, RT_PE.at(it, "O"))
                    a.wait_ge(rt_dve, RT_DVE.at(it - 1, "yn3"))
                    RT_ACT.mark(a.copy(yce, ps[:, 3:5, 0:P]), rt_act, "Y")
                    a.wait_ge(rt_dve, RT_DVE.at(it, "ag3"))
                    RT_ACT.mark(act(rstd, mv.rearrange("p (h s) -> p h s", s=2)[:, :, 1], ACT.Ln, bias=RET_EPS), rt_act, "ln")
                    a.wait_ge(rt_act, RT_ACT.at(it, "ln"))
                    RT_ACT.mark(act(rstd, rstd, ACT.Exp, scale=-0.5), rt_act, "rstd")
                a.wait_ge(ret_rows, l + 1)
                a.copy(mixB[:, 2:4, 0:T].rearrange("p m (a c) -> p m a c", a=2), ps[:, 4:8, :].rearrange("p (m a) c -> p m a c", m=2)).then_inc(ret_rows_out, 1)
                RE_ACT.start()
                log_exp()
                a.wait_ge(re_dve, RE_DVE.at(l, "ag3"))
                RE_ACT.mark(act(rstd[SR], mv[SR].rearrange("p (h s) -> p h s", s=2)[:, :, 1], ACT.Ln, bias=RET_EPS), re_act, "ln")
                a.wait_ge(re_act, RE_ACT.at(l, "ln"))
                RE_ACT.mark(act(rstd[SR], rstd[SR], ACT.Exp, scale=-0.5), re_act, "rstd")
                a.wait_ge(re_pe, RE_PE.at(l, "ro"))
                RE_ACT.mark(a.copy(mixB[:, 2:4, T:NT], ps[:, 6, 0:2 * NS].rearrange("p (m t) -> p m t", m=2)), re_act, "ro")
                FG_ACT.start()
                log_exp()
                fga = lambda ins, n: FG_ACT.mark(ins, fg_act, n)
                a.wait_ge(fg_dve, FG_DVE.at(l, "abs"))
                fga(act(fe, fz, ACT.Exp, scale=-1.0), "exp")
                a.wait_ge(fg_act, FG_ACT.at(l, "exp"))
                fga(act(fe, fe, ACT.Ln, bias=1.0), "ln")
                for j in range(J_FQ + 1, J_FV, 2):
                    on((gemm_done, l * PJOBS + j + 1))
                    a.copy(fqk[:, j - J_FQ, :].rearrange("p (a b) -> p a b", a=3), job_psum(j)).then_inc(evac[1], 1)
                for j in range(J_FV + 1, J_OUT, 2):
                    evac_tm(l, j, fv, j - J_FV)
                with a.Fori(0, 4) as i:
                    it = l * 4 + i
                    FN_ACT.start()
                    log_exp()
                    for u in range(2):
                        r3 = frs[:, u, :].rearrange("p (a b) -> p a b", a=3)
                        a.wait_ge(fn_pe, FN_PE.at(it, f"ss{u}"))
                        FN_ACT.mark(act(r3, ps[:, 3 * u:3 * u + 3, 0:TB], ACT.Ln, scale=1.0 / HD, bias=EPS), fn_act, f"ln{u}")
                        a.wait_ge(fn_act, FN_ACT.at(it, f"ln{u}"))
                        FN_ACT.mark(act(frs[:, u, :], frs[:, u, :], ACT.Exp, scale=-0.5), fn_act, f"rs{u}")
                a.wait_ge(fg_pe, FG_PE.at(l, "lft"))
                fga(a.copy(lft, ps[:, 7, 0:(NTT + 1) * FH]), "lft")
                with a.Fori(0, 2) as pp:
                    it = l * 2 + pp
                    FP_ACT.start()
                    log_exp()
                    fm = lambda ins, n: FP_ACT.mark(ins, fp_act, n)
                    fd = lambda n: (fp_dve, FP_DVE.at(it, n))
                    fpp = lambda n: (fp_pe, FP_PE.at(it, n))

                    def prob(u, s):
                        w = P * (s // 2 + 1)
                        on(fd(f"{u}n{s}"))
                        fm(act(sp_[:, s % 2, 0:w], sp_[:, s % 2, 0:w], ACT.Exp, bias=nmx[:, s:s + 1], accum_out=rsum[:, s:s + 1]), f"{u}e{s}")

                    for u in range(2):
                        on((ko_free, l * 4 + pp * 2 + (u + 1)))
                        on(fpp(f"{u}ko"))
                        fm(a.copy(ko.rearrange("p i t -> p (i t)"), ps[:, 4:6, :].rearrange("p a b -> p (a b)")), f"{u}ko")
                        fm(a.copy(kos[SR], ps[SR, 6, 0:P]), f"{u}kos")
                        prob(u, 0)
                        for s in SC:
                            if ahead(s):
                                prob(u, s + 1)
                            if s % 2 == 0:
                                on(fpp(f"{u}T{s}"))
                                fm(a.copy(ptt[:, 0, 0:s // 2 + 1, :], ps[:, 4:6, :].rearrange("p a (b c) -> p (a b) c", c=P)[:, 0:s // 2 + 1, :]), f"{u}pt{s}")
                        on(fpp(f"{u}oT"))
                        fm(a.copy(hT[:, bass.ds(pp * 2 + u, 1), 0:T].rearrange("p a t -> p (a t)"), ps[:, 4:6, :].rearrange("p a b -> p (a b)")), f"{u}oT")
                with a.Fori(0, 2) as g:
                    it = l * 2 + g
                    G_ACT.start()
                    log_exp()
                    gm = lambda ins, n: G_ACT.mark(ins, fgr_act, n)
                    gd = lambda n: (fgr_dve, G_DVE.at(it, n))
                    gp = lambda n: (fgr_pe, G_PE.at(it, n))
                    for b in range(4):
                        for p in (0, 2):
                            on(gp(f"T{b}{p}"))
                            if b or p == 2:
                                on(gp(f"S{b}0") if p == 2 else gp(f"S{b - 1}2"))
                            gm(a.copy(keyt[0], ps[:, 3:5, :].rearrange("p a b -> p (a b)")), f"kt{b}{p}")
                    on(gd("neg"))
                    gm(act(pss[:, 0:NP], ps[:, 0:2, :].rearrange("p a b -> p (a b)"), ACT.Exp, bias=fsm[:, 3:4], accum_out=fsm[:, 4:5]), "e")
                    gm(act(pss[:, NP:NP + TS], smn, ACT.Exp, bias=fsm[:, 3:4], accum_out=fsm[:, 5:6]), "en")
                    on(gp("P0"))
                    gm(a.copy(pts[:, 0:4, :], ps[:, 3, :].rearrange("p (j r) -> p j r", j=4)), "pt0")
                norm(l, 1)
                with a.Fori(0, FT // 2) as q:
                    for u in range(2):
                        a.wait_ge(evac[1], l * HALF + q * 2 + ((J_FF + 2 * u + 1 - RING) // 2 + 2))
                        a.wait_ge(gemm_done, l * PJOBS + q * RING + (J_FF + 2 * u + 1))
                        act(sil[:, u * NT:(u + 1) * NT].rearrange("p (a b) -> p a b", a=3), job_psum(0), ACT.Silu).then_inc(evac[0], 1)
            def y_rows(t, u):
                a.wait_ge(y_pe, t * 2 + (u + 1))
                a.copy(yrows[:, u, :].rearrange("p (a b) -> p a b", a=2), ps[:, 4 * u:4 * u + 2, :]).then_inc(y_ev, 1)

            for u in range(2):
                y_rows(0, u)
            with a.Fori(1, NTT // 2) as t:
                for u in range(2):
                    a.wait_ge(y_out[u], t * 16)
                    y_rows(t, u)
            a.wait_ge(y_pe, NTT + 1)
            a.wait_ge(y_out[0], 16 * (NTT // 2))
            a.copy(yrows[0:NS, 0, :].rearrange("p (a b) -> p a b", a=2), ps[0:NS, 0:2, :]).then_inc(y_ev, 1)


_INS = ['x_prompt', 'x_sample', 'cache_fox_k', 'cache_fox_v', 'cache_fox_logf', 'state_rwkv', 'state_rwkv_shift',
        'state_ret', 'page_table', 'ln_mix_g', 'w_in', 'fox_qn_g', 'fox_kn_g', 'fox_f_b', 'rwkv_mu', 'rwkv_w0', 'rwkv_w2',
        'rwkv_a0', 'rwkv_a2', 'rwkv_g2', 'rwkv_k_k', 'rwkv_k_a', 'rwkv_r_k', 'rwkv_lnx_w', 'rwkv_lnx_b', 'ret_gn_w',
        'w_out', 'ln_ffn_g', 'w_gate', 'w_up', 'w_down']
_NP = T // PG
_OUTS = [("y_prompt", (1, T, D)), ("y_sample", (DB, TS, D)),
         ("fox_k_prompt", (DEPTH, _NP, PG, FH, HD)), ("fox_v_prompt", (DEPTH, _NP, PG, FH, HD)),
         ("fox_logf_prompt", (DEPTH, _NP, PG, FH)),
         ("rwkv_state_prompt", (DEPTH, 1, RH, HD, HD)), ("rwkv_shift_prompt", (DEPTH, 1, RPROJ)),
         ("ret_state_prompt", (DEPTH, 1, EH, HD, HD)),
         ("fox_k_sample", (DEPTH, DB, TS, FH, HD)), ("fox_v_sample", (DEPTH, DB, TS, FH, HD)),
         ("fox_logf_sample", (DEPTH, DB, TS, FH)),
         ("rwkv_state_sample", (DEPTH, DB, RH, HD, HD)), ("rwkv_shift_sample", (DEPTH, DB, RPROJ)),
         ("ret_state_sample", (DEPTH, DB, EH, HD, HD))]


def shape_constants(np):
    c = np.zeros((P, NCONST), np.float32)

    def put(name, a):
        o, w = CONSTS[name]
        a = np.asarray(a, np.float32).reshape(a.shape[0], -1)
        assert a.shape[1] == w, (name, a.shape, w)
        c[:a.shape[0], o:o + w] = a

    i = np.arange(P)
    t, s = i[:, None], i[None, :]
    put("ident", (t == s))
    put("blk", (t // HD == s // HD))
    half = HD // 2
    put("rot", np.where(s % HD < half, -1.0 * (t == s + half), 1.0 * (t == s - half)))
    put("m_d", (s < t) & (s // 16 == t // 16))
    put("m_n", s // 16 < t // 16)
    put("m_dt", (t < s) & (s // 16 == t // 16))
    put("m_u", t < s)
    put("m_ui", t <= s)
    put("fmask", np.where(s <= t, 0.0, -1e30))
    j = np.arange(NS)
    t4, s4 = j[:, None], j[None, :]
    same = t4 // TS == s4 // TS
    put("s_l", same & (s4 < t4))
    put("s_lt", same & (t4 < s4))
    put("s_u", same & (t4 < s4))
    put("s_ui", same & (t4 <= s4))
    put("s_row", (j[:, None] // TS == np.arange(DB)[None, :]))
    put("s_col", np.broadcast_to((np.arange(DB)[:, None] == j[None, :] // TS)[None], (P, DB, NS)))
    lg = np.log1p(-np.exp2(-5.0 - np.arange(EH, dtype=np.float32))).astype(np.float32)
    head = 2 * np.arange(2)[None, :, None] + i[:, None, None] // HD
    put("cross", np.exp(lg[head] * (i[None, None, :] + 1.0)))
    put("inner", np.exp(lg[None, :] * (P - 1.0 - i[:, None])))
    put("gam", np.exp(lg[head[:, :, 0]] * P))
    put("dmask", np.where(t[:, None] <= i[None, None, :], np.exp(lg[None, :, None] * np.maximum(i[None, None, :] - t[:, None], 0.0)), 0.0))
    put("s_dmask", np.where(same[:, None] & (t4[:, None] <= j[None, None, :]), np.exp(lg[None, :, None] * np.maximum(j[None, None, :] - t4[:, None], 0.0)), 0.0))
    put("s_cross", np.exp(lg[head] * (j[None, None, :] % TS + 1.0)))
    put("s_inner", np.exp(lg[None, :] * (TS - 1.0 - j[:, None] % TS)))
    put("s_gam", np.exp(lg[head[:, :, 0]] * TS))
    inv = (np.float32(10000.0) ** (-np.arange(half, dtype=np.float32) / np.float32(half))).astype(np.float32)
    pos = np.concatenate([np.arange(T), NPG * PG + np.arange(NS) % TS]).astype(np.float32)
    ang = (pos[None, :] * inv[i % half][:, None]).astype(np.float32)
    put("cos", np.cos(ang))
    put("sin", np.sin(ang))
    r = np.arange(P)
    g = np.arange(2)
    put("s_sel", ((np.arange(64)[:, None, None] // FH == 4 * g[None, :, None] + r[None, None, :] // 32)
         & (np.arange(64)[:, None, None] % FH == r[None, None, :] % 32 // TS)))
    put("s_req", np.arange(DB)[None, None, :] == 4 * g[None, :, None] + r[:, None, None] // 32)
    put("s_fmask", np.where(np.arange(TS)[None, :] <= r[:, None] % TS, 0.0, -1e30))
    put("s_tok", np.arange(16)[None, :] == r[:, None] // 32 * TS + r[:, None] % TS)
    put("s_head", np.arange(FH)[None, :] == r[:, None] % 32 // TS)
    return c


def kernel(**inputs):
    import numpy as np
    import concourse.bacc as bacc
    from concourse.bass_utils import run_bass_kernel_spmd

    nc = bacc.Bacc("TRN2", target_bir_lowering=False, num_devices=1)
    arrays, ins, outs = {}, {}, {}
    given = {name: np.ascontiguousarray(inputs[name]) for name in _INS}
    given["consts"] = shape_constants(np)
    for name, a in given.items():
        arrays[f"in_{name}"] = a
        ins[name] = nc.dram_tensor(f"in_{name}", a.shape, mybir.dt.from_np(a.dtype), kind="ExternalInput").ap()
    for name, shape in _OUTS:
        outs[name] = nc.dram_tensor(f"out_{name}", shape, F32, kind="ExternalOutput").ap()
    build(nc, ins, outs, nc.dram_tensor("decay_rows", (FH, T), F32, kind="Internal").ap())
    r = run_bass_kernel_spmd(nc, [arrays], core_ids=[0])
    return tuple(r.results[0][f"out_{name}"] for name, _ in _OUTS)
```
